# Optimizing a Trainium2 kernel written in Bass

```python
import math
import jax
import jax.numpy as jnp
from jax import lax
import numpy as np

D_MODEL = 1024
BATCH = 1
SEQ = 256
DEPTH = 2
DEC_BATCH = 8
DEC_SEQ = 8
PAST_LEN = 1024
PAGE_SIZE = 128

N_A = DEPTH // 2
N_B = DEPTH - N_A
HEAD_DIM = 64
H_A = D_MODEL // HEAD_DIM
H_B = D_MODEL // HEAD_DIM
D_FF = ((8 * D_MODEL // 3 + 255) // 256) * 256
LORA_W = 64
LORA_A = 64
LORA_V = 32
LORA_G = 128
ATTN_BLOCK = 128
RMS_EPS = 1e-6
LNX_EPS = 64e-5

kernel_name = 'rwkv7_fox_yoco_macaron_step'

def rms_norm(x, g):
    xf = x.astype(jnp.float32)
    y = xf * lax.rsqrt(jnp.mean(xf * xf, axis=-1, keepdims=True) + RMS_EPS)
    return y.astype(x.dtype) * g

def swiglu(x, w_in, w_out):
    gate, up = jnp.split(x @ w_in, 2, axis=-1)
    return (jax.nn.silu(gate) * up) @ w_out

def wkv7_scan(S0, r, w, k, v, kk, a):
    xs = tuple(jnp.moveaxis(t, 1, 0) for t in (r, w, k, v, kk, a))

    def step(S, inp):
        r_t, w_t, k_t, v_t, kk_t, a_t = inp
        sa = jnp.einsum('bhij,bhj->bhi', S, kk_t)
        S = (S * w_t[:, :, None, :]
             - sa[..., None] * (kk_t * a_t)[:, :, None, :]
             + v_t[..., None] * k_t[:, :, None, :])
        y = jnp.einsum('bhij,bhj->bhi', S, r_t)
        return S, y

    S, ys = lax.scan(step, S0, xs)
    return jnp.moveaxis(ys, 0, 1), S

def rwkv7_time_mix(x, shift_prev, S0, v_first, vres, mu, w_rkv, w0, w1, w2, a0, a1, a2,
                   g1, g2, k_k, k_a, r_k, lnx_w, lnx_b, w_o):
    B, T, D = x.shape
    x_prev = jnp.concatenate([shift_prev[:, None, :].astype(x.dtype), x[:, :-1]], axis=1)
    xs = x[None] + (x_prev - x)[None] * mu[:, None, None, :]
    r, k, v = jnp.einsum('nbtd,nde->nbte', xs[:3], w_rkv)
    xv, xw, xa, xg = xs[2], xs[3], xs[4], xs[5]
    w = -jax.nn.softplus(-(w0 + jnp.tanh(xw @ w1) @ w2).astype(jnp.float32)) - 0.5
    decay = jnp.exp(-jnp.exp(w))
    a = jax.nn.sigmoid(a0 + (xa @ a1) @ a2)
    g = jax.nn.sigmoid(xg @ g1) @ g2
    if vres is not None:
        v0, v1, v2 = vres
        v = v + (v_first - v) * jax.nn.sigmoid(v0 + (xv @ v1) @ v2)
    heads = lambda t: t.reshape(B, T, H_A, HEAD_DIM)
    kk = heads((k * k_k).astype(jnp.float32))
    kk = kk / jnp.maximum(jnp.linalg.norm(kk, axis=-1, keepdims=True), 1e-12)
    k = k * (1 + (a - 1) * k_a)
    rh, kh, vh, ah = [heads(t).astype(jnp.float32) for t in (r, k, v, a)]
    y, S = wkv7_scan(S0.astype(jnp.float32), rh, heads(decay), kh, vh, kk, ah)
    mean = jnp.mean(y, axis=-1, keepdims=True)
    var = jnp.mean(jnp.square(y - mean), axis=-1, keepdims=True)
    yn = ((y - mean) * lax.rsqrt(var + LNX_EPS)).reshape(B, T, D) * lnx_w + lnx_b
    bonus = (jnp.sum(rh * kh * r_k, axis=-1, keepdims=True) * vh).reshape(B, T, D)
    out = ((yn + bonus).astype(x.dtype) * g) @ w_o
    return out, S, x[:, -1], v

def shared_kv(h, kv_norm, w_kv, k_norm, w_f, b_f):
    B, T, _ = h.shape
    hn = rms_norm(h, kv_norm)
    k, v = jnp.split(hn @ w_kv, 2, axis=-1)
    k = rms_norm(k.reshape(B, T, H_B, HEAD_DIM), k_norm)
    v = v.reshape(B, T, H_B, HEAD_DIM)
    logf = jax.nn.log_sigmoid((hn @ w_f + b_f).astype(jnp.float32))
    return k, v, logf

def fox_attention(q, k, v, f_q, f_k, q_pos, k_pos):
    B, Tq, H, Dh = q.shape
    qb = ATTN_BLOCK if Tq % ATTN_BLOCK == 0 else Tq
    nb = Tq // qb
    scale = 1.0 / math.sqrt(Dh)
    q_blk = jnp.moveaxis(q.reshape(B, nb, qb, H, Dh), 1, 0)
    f_blk = jnp.moveaxis(f_q.reshape(B, nb, qb, H), 1, 0)
    p_blk = q_pos.reshape(nb, qb)
    f_key = jnp.transpose(f_k, (0, 2, 1))[:, :, None, :]

    def one_block(blk):
        q_i, f_i, pos_i = blk
        s = jnp.einsum('bqhd,bkhd->bhqk', q_i, k, preferred_element_type=jnp.float32) * scale
        s = s + jnp.transpose(f_i, (0, 2, 1))[..., None] - f_key
        s = jnp.where(k_pos[None, :] <= pos_i[:, None], s, -jnp.inf)
        p = jax.nn.softmax(s, axis=-1).astype(v.dtype)
        return jnp.einsum('bhqk,bkhd->bqhd', p, v)

    o = lax.map(one_block, (q_blk, f_blk, p_blk))
    return jnp.moveaxis(o, 0, 1).reshape(B, Tq, H, Dh)

def trunk(x, shift0, wkv0, past, prm):
    B, T, _ = x.shape
    h = x
    v_first = None
    new_wkv, new_shift = [], []
    k_new = v_new = logf_new = None
    k_all = v_all = f_q = f_k = q_pos = k_pos = None
    for i in range(DEPTH):
        if i == N_A:
            k_new, v_new, logf_new = shared_kv(h, prm['kv_norm'], prm['w_kv'], prm['k_norm'],
                                               prm['w_f'], prm['b_f'])
            f_q = lax.cumsum(logf_new, axis=1)
            if past is None:
                k_all, v_all, f_k = k_new, v_new, f_q
                q_pos = jnp.arange(T)
                k_pos = jnp.arange(T)
            else:
                k_p, v_p, lf_p = past
                P = k_p.shape[1]
                lf_p = lf_p.astype(jnp.float32)
                f_past = lf_p - lax.cumsum(lf_p, axis=1, reverse=True)
                f_k = jnp.concatenate([f_past, f_q], axis=1)
                k_all = jnp.concatenate([k_p.astype(k_new.dtype), k_new], axis=1)
                v_all = jnp.concatenate([v_p.astype(v_new.dtype), v_new], axis=1)
                q_pos = P + jnp.arange(T)
                k_pos = jnp.arange(P + T)
        h = h + 0.5 * swiglu(rms_norm(h, prm['ffn_norm'][i, 0]), prm['ffn_w_in'][i, 0], prm['ffn_w_out'][i, 0])
        xn = rms_norm(h, prm['mix_norm'][i])
        if i < N_A:
            vres = None if i == 0 else (prm['rw_v0'][i - 1], prm['rw_v1'][i - 1], prm['rw_v2'][i - 1])
            out, S, sh, v = rwkv7_time_mix(
                xn, shift0[i], wkv0[i], v_first, vres, prm['rw_mu'][i], prm['rw_w_rkv'][i],
                prm['rw_w0'][i], prm['rw_w1'][i], prm['rw_w2'][i], prm['rw_a0'][i], prm['rw_a1'][i],
                prm['rw_a2'][i], prm['rw_g1'][i], prm['rw_g2'][i], prm['rw_k_k'][i], prm['rw_k_a'][i],
                prm['rw_r_k'][i], prm['rw_lnx_w'][i], prm['rw_lnx_b'][i], prm['rw_w_o'][i])
            if i == 0:
                v_first = v
            new_wkv.append(S)
            new_shift.append(sh)
        else:
            j = i - N_A
            q = rms_norm((xn @ prm['fox_w_q'][j]).reshape(B, T, H_B, HEAD_DIM), prm['fox_q_norm'][j])
            o = fox_attention(q, k_all, v_all, f_q, f_k, q_pos, k_pos)
            out = o.reshape(B, T, D_MODEL) @ prm['fox_w_o'][j]
        h = h + out
        h = h + 0.5 * swiglu(rms_norm(h, prm['ffn_norm'][i, 1]), prm['ffn_w_in'][i, 1], prm['ffn_w_out'][i, 1])
    return h, k_new, v_new, logf_new, jnp.stack(new_wkv), jnp.stack(new_shift)

def setup_inputs(seed: int = 0) -> dict:
    key = jax.random.key(seed)
    ks = iter(jax.random.split(key, 48))
    f32 = jnp.float32
    nrm = lambda shape, scale: jax.random.normal(next(ks), shape, f32) * scale
    D = D_MODEL
    n_pages = PAST_LEN // PAGE_SIZE
    n_used = DEC_BATCH * n_pages
    n_pool = (n_used * 5 + 3) // 4
    inp = {}
    inp['x_prompt'] = nrm((BATCH, SEQ, D), 1.0)
    inp['x_sample'] = nrm((DEC_BATCH, DEC_SEQ, D), 1.0)
    inp['cache_k'] = nrm((n_pool, PAGE_SIZE, H_B, HEAD_DIM), 1.0)
    inp['cache_v'] = nrm((n_pool, PAGE_SIZE, H_B, HEAD_DIM), 1.0)
    inp['cache_logf'] = jax.nn.log_sigmoid(8.0 + nrm((n_pool, PAGE_SIZE, H_B), 0.5))
    inp['state_wkv'] = nrm((N_A, DEC_BATCH, H_A, HEAD_DIM, HEAD_DIM), 0.5)
    inp['state_shift'] = nrm((N_A, DEC_BATCH, D), 1.0)
    perm = jax.random.permutation(next(ks), n_pool)[:n_used]
    inp['page_table'] = perm.reshape(DEC_BATCH, n_pages).astype(jnp.int32)
    inp['ffn_norm'] = 1.0 + nrm((DEPTH, 2, D), 0.02)
    inp['ffn_w_in'] = nrm((DEPTH, 2, D, 2 * D_FF), D ** -0.5)
    inp['ffn_w_out'] = nrm((DEPTH, 2, D_FF, D), D_FF ** -0.5)
    inp['mix_norm'] = 1.0 + nrm((DEPTH, D), 0.02)
    inp['rw_mu'] = jax.random.uniform(next(ks), (N_A, 6, D), f32)
    inp['rw_w_rkv'] = nrm((N_A, 3, D, D), D ** -0.5)
    base = -6.5 + 5.0 * (jnp.arange(D, dtype=f32) / (D - 1)) ** 0.85
    inp['rw_w0'] = base[None, :] + nrm((N_A, D), 0.1)
    inp['rw_w1'] = nrm((N_A, D, LORA_W), D ** -0.5)
    inp['rw_w2'] = nrm((N_A, LORA_W, D), 0.1 * LORA_W ** -0.5)
    inp['rw_a0'] = nrm((N_A, D), 0.1)
    inp['rw_a1'] = nrm((N_A, D, LORA_A), D ** -0.5)
    inp['rw_a2'] = nrm((N_A, LORA_A, D), 0.1 * LORA_A ** -0.5)
    inp['rw_v0'] = 1.0 + nrm((N_A - 1, D), 0.1)
    inp['rw_v1'] = nrm((N_A - 1, D, LORA_V), D ** -0.5)
    inp['rw_v2'] = nrm((N_A - 1, LORA_V, D), 0.1 * LORA_V ** -0.5)
    inp['rw_g1'] = nrm((N_A, D, LORA_G), D ** -0.5)
    inp['rw_g2'] = nrm((N_A, LORA_G, D), LORA_G ** -0.5)
    inp['rw_k_k'] = 0.85 + nrm((N_A, D), 0.02)
    inp['rw_k_a'] = 1.0 + nrm((N_A, D), 0.02)
    inp['rw_r_k'] = nrm((N_A, H_A, HEAD_DIM), 0.1)
    inp['rw_lnx_w'] = 1.0 + nrm((N_A, D), 0.02)
    inp['rw_lnx_b'] = nrm((N_A, D), 0.02)
    inp['rw_w_o'] = nrm((N_A, D, D), D ** -0.5)
    inp['kv_norm'] = 1.0 + nrm((D,), 0.02)
    inp['w_kv'] = nrm((D, 2 * D), D ** -0.5)
    inp['k_norm'] = 1.0 + nrm((HEAD_DIM,), 0.02)
    inp['w_f'] = nrm((D, H_B), 0.5 * D ** -0.5)
    inp['b_f'] = jnp.linspace(2.0, 8.0, H_B, dtype=f32) + nrm((H_B,), 0.1)
    inp['fox_w_q'] = nrm((N_B, D, D), D ** -0.5)
    inp['fox_q_norm'] = 1.0 + nrm((N_B, HEAD_DIM), 0.02)
    inp['fox_w_o'] = nrm((N_B, D, D), D ** -0.5)
    return inp

def reference(x_prompt, x_sample, cache_k, cache_v, cache_logf, state_wkv, state_shift, page_table,
              ffn_norm, ffn_w_in, ffn_w_out, mix_norm,
              rw_mu, rw_w_rkv, rw_w0, rw_w1, rw_w2, rw_a0, rw_a1, rw_a2, rw_v0, rw_v1, rw_v2,
              rw_g1, rw_g2, rw_k_k, rw_k_a, rw_r_k, rw_lnx_w, rw_lnx_b, rw_w_o,
              kv_norm, w_kv, k_norm, w_f, b_f, fox_w_q, fox_q_norm, fox_w_o):
    prm = {
        'ffn_norm': ffn_norm, 'ffn_w_in': ffn_w_in, 'ffn_w_out': ffn_w_out, 'mix_norm': mix_norm,
        'rw_mu': rw_mu, 'rw_w_rkv': rw_w_rkv, 'rw_w0': rw_w0, 'rw_w1': rw_w1, 'rw_w2': rw_w2,
        'rw_a0': rw_a0, 'rw_a1': rw_a1, 'rw_a2': rw_a2, 'rw_v0': rw_v0, 'rw_v1': rw_v1, 'rw_v2': rw_v2,
        'rw_g1': rw_g1, 'rw_g2': rw_g2, 'rw_k_k': rw_k_k, 'rw_k_a': rw_k_a, 'rw_r_k': rw_r_k,
        'rw_lnx_w': rw_lnx_w, 'rw_lnx_b': rw_lnx_b, 'rw_w_o': rw_w_o,
        'kv_norm': kv_norm, 'w_kv': w_kv, 'k_norm': k_norm, 'w_f': w_f, 'b_f': b_f,
        'fox_w_q': fox_w_q, 'fox_q_norm': fox_q_norm, 'fox_w_o': fox_w_o,
    }
    Bp = x_prompt.shape[0]
    shift0_p = jnp.zeros((N_A, Bp, D_MODEL), x_prompt.dtype)
    wkv0_p = jnp.zeros((N_A, Bp, H_A, HEAD_DIM, HEAD_DIM), jnp.float32)
    y_prompt, k_prompt, v_prompt, logf_prompt, wkv_prompt, shift_prompt = trunk(
        x_prompt, shift0_p, wkv0_p, None, prm)
    Bd, n_pages = page_table.shape
    ps = cache_k.shape[1]
    k_past = cache_k[page_table].reshape(Bd, n_pages * ps, H_B, HEAD_DIM)
    v_past = cache_v[page_table].reshape(Bd, n_pages * ps, H_B, HEAD_DIM)
    lf_past = cache_logf[page_table].reshape(Bd, n_pages * ps, H_B)
    y_sample, k_sample, v_sample, logf_sample, wkv_sample, shift_sample = trunk(
        x_sample, state_shift, state_wkv, (k_past, v_past, lf_past), prm)
    return (y_prompt, y_sample, k_prompt, v_prompt, logf_prompt, wkv_prompt, shift_prompt,
            k_sample, v_sample, logf_sample, wkv_sample, shift_sample)


_drawn_inputs = setup_inputs


def setup_inputs(seed=0):
    import zlib

    import numpy as np

    out = dict(_drawn_inputs(seed))
    spreads = {}
    factors = {'cache_logf': 8.0,
     'ffn_norm': 3.369,
     'rw_w1': 8.0,
     'rw_w2': 8.0,
     'rw_lnx_w': 5.578,
     'rw_lnx_b': 5.06,
     'kv_norm': 2.876,
     'k_norm': 2.701,
     'fox_q_norm': 8.0}
    for name, (base, spread) in spreads.items():
        noise = np.random.default_rng([zlib.crc32(name.encode()), seed]).standard_normal(out[name].shape)
        drawn = base * np.exp(spread * noise) if base else spread * noise
        out[name] = jnp.asarray(drawn.astype(out[name].dtype))
    for name, factor in factors.items():
        out[name] = (out[name] * factor).astype(out[name].dtype)
    return out
```

```python
from contextlib import ExitStack

import numpy as np

import concourse.bass as bass
from concourse import mybir

P = 128
D = 1024
DT = D // P
TP, BS, TS = 256, 8, 64
T = TP + TS
QS = TS // BS
H, HD = 16, 64
HP = H // 2
FF = 2816
FT = FF // P
PAST, PAGE = 1024, 128
PAGES = PAST // PAGE
C = 64
CHUNKS = T // C
RMS_EPS, LNX_EPS = 1e-6, 64e-5
SLOT = 2048
SLOTS = 6
NEG = -1e30
DECAY = float(np.exp(-0.5))

F32 = mybir.dt.float32
I32 = mybir.dt.int32
ALU = mybir.AluOpType
ACT = mybir.ActivationFunctionType
AX = mybir.AxisListType

PARAMS = ["ffn_norm", "mix_norm", "rw_mu", "rw_w0", "rw_a0", "rw_k_k", "rw_k_a", "rw_r_k",
          "rw_lnx_w", "rw_lnx_b", "kv_norm"]
PARAM_ROWS = {"ffn_norm": 4, "mix_norm": 2, "rw_mu": 6}


def plan_tiles():
    first, owner = {}, []

    def add(name, n, who="d"):
        first[name] = len(owner)
        owner.extend(who * n if len(who) == 1 else who)

    def ffn(n):
        add(f"norm_ffn{n}", 1, "a")
        add(f"up{n}", 2 * FT)
        add(f"down{n}", DT)

    add("params", 2)
    add("shift_in", 1)
    add("x", DT)
    ffn(0)
    add("norm_mix0", 1, "a")
    add("shift_out", 2)
    for n in "rkv":
        add(n, DT)
    add("w1", 1, "a")
    add("w2", DT, "a")
    add("a1", 1)
    add("a2", DT, "a")
    add("g1", 1, "a")
    add("g2", DT)
    add("kk_norm", DT)
    add("bonus", DT)
    add("state_in", BS)
    for c in range(CHUNKS):
        last = c == CHUNKS - 1
        add(f"LT{c}", 2)
        add(f"KA{c}", 2)
        add(f"RG{c}", 2)
        add(f"tok{c}", 6, "a")
        add(f"D{c}", 2)
        for lv in levels(c):
            add(f"Z{c}_{lv}", 2, "a")
            if lv != levels(c)[-1]:
                add(f"DD{c}_{lv}", 2)
            add(f"DDT{c}_{lv}", 2)
        if last:
            add("own_state", 2)
        add(f"X{c}", 2, "a")
        add(f"U{c}", 2, "a")
        add(f"Y{c}", 2)
        if not last:
            add(f"S{c}", 2)
            if c == CHUNKS - 2:
                add("wkv_prompt", 2)
    for p in range(HP):
        add(f"SS{p}", 1)
        add(f"ST{p}", 2, "a")
    add("mean", DT)
    add("var", DT, "a")
    add("wo", DT)
    ffn(1)
    add("norm_kv", 1, "a")
    add("kk", DT)
    add("vv", DT)
    add("logf", 1)
    add("k_norm", DT, "a")
    add("logf_tok", 1)
    add("k_tok", 6)
    add("v_tok", 6)
    ffn(2)
    add("norm_mix1", 1, "a")
    add("q", DT)
    add("q_norm", DT, "a")
    add("fq_col", 1)
    add("fk_past", 4)
    add("fb", H)
    add("fox", 3 * H)
    add("fo", DT)
    ffn(3)
    add("y", 6)
    return first, owner


def levels(c):
    return [1, 2, 3, 4, 5] if c < CHUNKS - 1 else [1, 2]


def const_arrays():
    i = np.arange(P)
    head, tok = i // C, i % C
    same = (head[:, None] == head[None, :])
    s, t = tok[:, None], tok[None, :]
    m = {}
    m["ident"] = np.eye(P)
    m["ones"] = np.ones((P, P))
    m["pair"] = same
    for kind, seq in (("p", True), ("s", s // QS == t // QS)):
        m["strict_" + kind] = same & (s < t) & seq
        incl = ((s <= t) & seq)[:, :C]
        m["upto_" + kind] = np.concatenate([incl, incl], 1)
        m["first_" + kind] = same & (s + 1 == t) & (t % 2 == 1) & seq
    for lv in range(1, 6):
        b = 2 ** lv
        m[f"join{lv}"] = same & (s // (2 * b) == t // (2 * b)) & (s // b % 2 == 0) & (t // b % 2 == 1)
    m["later"] = i[:, None] > i[None, :]
    m["seq"] = tok[:, None] // QS == np.arange(BS)[None, :]
    chunk_mask = np.ones((P, T))
    chunk_mask[:, 0:TP:C] = 0
    chunk_mask[:, TP::QS] = 0
    m["chunk"] = chunk_mask
    seq_mask = np.ones((P, T))
    seq_mask[:, 0] = 0
    seq_mask[:, TP::QS] = 0
    m["seqscan"] = seq_mask
    causal = np.where(i[:, None] >= i[None, :], 0, NEG)
    m["causal"] = np.concatenate([causal, np.zeros((P, P)), causal], 1)
    m["new"] = np.where(np.arange(QS)[None, :] <= i[:, None] % QS, 0, NEG)
    m["quarter"] = i[:, None] // QS % 4 == np.arange(4)[None, :]
    m["selcol"] = (i[:, None] == i[None, :] // QS)
    m["qpick"] = (i[:, None] % QS == np.arange(QS)[None, :])
    at, out = {}, []
    n = 0
    for name, a in m.items():
        at[name] = (n, n + a.shape[1])
        n += a.shape[1]
        out.append(np.asarray(a, np.float32))
    return at, np.concatenate(out, 1)


def head_selectors():
    return np.repeat(np.eye(H, dtype=np.float32), P, 1)


def build(nc, A, O):
    first, owner = plan_tiles()
    at, const_np = const_arrays()
    N_CONST = const_np.shape[1]
    freed = {"d": [0], "a": [0]}
    for w in owner:
        for e in "da":
            freed[e].append(freed[e][-1] + (w == e))
    row_of, rows = {}, 0
    for name in PARAMS:
        row_of[name] = rows
        rows += PARAM_ROWS.get(name, 1) * DT
    row_of["head_norms"] = rows
    rows += 2
    norms = ["ffn0", "mix0", "ffn1", "kv", "ffn2", "mix1", "ffn3"]
    norm_src = dict(zip(norms, ["x", "down0", "wo", "down1", "down1", "down2", "fo"]))

    with ExitStack() as ctx:
        def sb(name, shape, dt=F32):
            return ctx.enter_context(nc.sbuf_tensor(name, shape, dt))

        sems = {}

        def S(name):
            if name not in sems:
                sems[name] = ctx.enter_context(nc.semaphore(name))
            return sems[name]

        TW = DT * T
        h_f = sb("h", [P, TW])
        xn_f = sb("xn", [P, TW])
        ring = sb("ring", [P, SLOTS, SLOT])
        arena = sb("arena", [P, 11 * TW])
        extra = sb("extra", [P, 2048])
        const = sb("const", [P, N_CONST])
        par = sb("par", [P, 2, P])
        small = sb("small", [P, 800])
        root = sb("root", [P, T])
        rs = sb("rs", [P, T])
        pt_sb = sb("pt_sb", [1, BS * PAGES], I32)
        ps = ctx.enter_context(nc.psum_tensor("ps", [P, 8, 512], F32))

        def feat(x):
            return x.rearrange("p (m t) -> p m t", m=DT)

        h, xn = feat(h_f[:, :]), feat(xn_f[:, :])

        def A_(n):
            return feat(arena[:, n * TW:(n + 1) * TW])

        def K(name):
            return const[:, at[name][0]:at[name][1]]

        def prm(name, m, row=0):
            r = row_of[name] + row * DT + m
            return par[:, r // P, r % P:r % P + 1]

        ident, ones, pair = K("ident"), K("ones"), K("pair")
        used = [0]

        def sm(n):
            used[0] += n
            assert used[0] <= 800, used
            return small[:, used[0] - n:used[0]]

        eps, eps_ln, b_f = sm(1), sm(1), sm(1)
        omka = sm(DT)
        w_f = sm(DT * H).rearrange("p (k n) -> p k n", k=DT)
        shT = sm(DT * BS).rearrange("p (m b) -> p m b", m=DT)
        shc = sm(DT * (BS + 1)).rearrange("p (m b) -> p m b", m=DT)
        lf_tok = sm(3 * H).rearrange("p (g h) -> p g h", g=3)
        F_tok = sm(3 * H).rearrange("p (g h) -> p g h", g=3)
        F_row = sm(TS)
        fq_all, tmp_fq = sm(BS), sm(TS)
        tmp_col = sm(16)
        hn_scale = sm(2)

        hid = arena[:, 0:FT * T].rearrange("p (f t) -> p f t", f=FT)
        sg = arena[:, 10 * TW:10 * TW + 4 * T].rearrange("p (g t) -> p g t", g=4)
        sq = A_(8)

        tile_done = S("tile_done")
        dve_freed = S("dve_freed_bank")
        act_freed = S("act_freed_bank")

        def bank(t, n=512, rows_=P):
            return ps[0:rows_, t % 8, 0:n]

        w_in = A["ffn_w_in"].rearrange("l s k m -> (l s) k m")
        w_out = A["ffn_w_out"].rearrange("l s k m -> (l s) k m")

        def cols(w, k0, k1, c0, n):
            return w[k0 * P:k1 * P, c0:c0 + n].rearrange("(k p) m -> p k m", p=P)

        def slab(slot, k, n=256):
            return ring[:, slot, 0:k * n].rearrange("p (k m) -> p k m", k=k)

        dense = {
            "r": A["rw_w_rkv"][0, 0], "k": A["rw_w_rkv"][0, 1], "v": A["rw_w_rkv"][0, 2],
            "wo": A["rw_w_o"][0], "kk": A["w_kv"][:, 0:D], "vv": A["w_kv"][:, D:2 * D],
            "q": A["fox_w_q"][0], "fo": A["fox_w_o"][0],
        }
        place = {"r": [0, 1, 2, 3], "k": [4, 5, 0, 1], "v": [2, 3, 4, 5], "wo": [4, 5, 4, 5],
                 "kk": [0, 1, 2, 3], "vv": [4, 5, 0, 1], "q": [2, 3, 4, 5], "fo": [2, 3, 4, 5]}
        LORA1, LORA2, LORA3 = 0, 1, 2
        lo1 = slab(LORA1, DT)

        def buf(j):
            if j < 2:
                x = xn_f[:, j * D:(j + 1) * D]
            elif j < 10:
                x = ring[:, (j - 2) // 2, (j - 2) % 2 * D:(j - 2) % 2 * D + D]
            elif j < 12:
                x = extra[:, (j - 10) * D:(j - 9) * D]
            else:
                x = arena[:, 6 * TW + 4096:6 * TW + 4096 + D]
            return x.rearrange("p (m c) -> p m c", m=HP)

        (A_bd, B_bd, K_bd, V_bd, LT_bd, KA_bd, RG_bd, V_tok, B_tok, K_tok, DT_bd, X_bd, S_bd) = (
            buf(j) for j in range(13))
        join_bd, Z_bd, D_bd = B_bd, K_bd, V_bd
        S0 = arena[:, 6 * TW:6 * TW + 4096].rearrange("p (b m i) -> p b m i", b=BS, m=HP)
        state_in = [x.rearrange("p m c -> p (m c)") for x in (LT_bd, KA_bd)]
        S0_bd = [B_bd, K_bd]
        XT_bd, Y0 = V_bd, LT_bd.rearrange("p m c -> p (m c)")[:, 0:512].rearrange("p (m c) -> p m c", m=HP)
        U_st = A_bd.rearrange("p m c -> p (m c)")[:, 0:512].rearrange("p (m c) -> p m c", m=HP)
        V_st = A_bd.rearrange("p m c -> p (m c)")[:, 512:1024].rearrange("p (m c) -> p m c", m=HP)
        UV = [x.rearrange("p m c -> p (m c)").rearrange("p (e b i) -> p e b i", e=2, b=BS) for x in (B_bd, K_bd)]
        SF = V_bd.rearrange("p m c -> p (m c)").rearrange("p (e b i) -> p e b i", e=2, b=BS)
        state_out = [x.rearrange("p m c -> p (m c)") for x in (LT_bd, KA_bd)]
        Yf = A_(9)
        Af, Bf, bonus, Rf, Kf, Vf, gf, Ef = A_(0), A_(1), A_(2), A_(3), A_(4), A_(5), A_(8), A_(10)

        kT, q_f = A_(3), A_(6)
        v_tok = arena[:, 4 * TW:4 * TW + 3 * D].rearrange("p (g d) -> p g d", g=3)
        k_tok = arena[:, 6 * TW:6 * TW + 3 * D].rearrange("p (g d) -> p g d", g=3)
        oT = xn
        fb = arena[:, 7 * TW:7 * TW + H * 384].rearrange("p (h c) -> p h c", h=H)
        head_sel = ring[0:H, 0, :].rearrange("p (h c) -> p h c", h=H)
        o10 = 10 * TW
        qp_bd = arena[:, o10:o10 + 1024].rearrange("p (j e t) -> p j e t", j=2, e=2)
        s_pr = arena[:, o10 + 1024:o10 + 1792].rearrange("p (j c) -> p j c", j=2)
        pT = arena[:, o10 + 1792:o10 + 2560].rearrange("p (j c) -> p j c", j=2)
        fstat = sb("fstat", [P, 2, 10])

        def v_page(j):
            return arena[:, j * D:(j + 1) * D] if j < 7 else arena[:, 4 * TW + 3 * D:4 * TW + 4 * D]

        def k_page(j):
            return ring[:, j // 2, j % 2 * D:j % 2 * D + D]

        o7 = 7 * TW
        k_feat = [arena[:, o7 + j * 2048:o7 + (j + 1) * 2048].rearrange("p (m t) -> p m t", m=HP) for j in range(2)]
        p_row = arena[:, o7 + 4096:o7 + 5184]
        p_T = arena[:, o7 + 5184:o7 + 6336].rearrange("p (g c) -> p g c", g=9)
        nfk_rep = arena[:, o7 + 6336:o7 + 7360]
        mask_new = arena[:, o7 + 7360:o7 + 7872].rearrange("p (b k) -> p b k", b=BS)
        o_two = arena[:, o7 + 7872:o7 + 8000]
        o_own = arena[:, o7 + 8000:o7 + 8256].rearrange("p (g d) -> p g d", g=4)
        s_new = arena[:, o7 + 8256:o7 + 8320]
        q_cur = arena[:, o7 + 8320:o7 + 8576]
        sst = arena[:, o7 + 8576:o7 + 8592]
        nfk = extra[:, 640:1664].rearrange("p (b j h) -> p b j h", b=BS, j=PAGES)
        lfp = arena[:, 7 * TW + 6144:7 * TW + 7168].rearrange("p (b j h) -> p b j h", b=BS, j=PAGES)    
        FT_, LF = extra[0:H, 0:T], extra[0:H, T:2 * T]
        lw = [extra[0:H, (2 + j) * T:(3 + j) * T] for j in range(4)]
        nF_dup = extra[0:H, 1664:2048]
        N_PARAM_DMAS = sum(2 if row_of[n] < P < row_of[n] + PARAM_ROWS.get(n, 1) * DT else 1 for n in PARAMS) + 4
        join_count, n_join = {}, 0
        for c in range(CHUNKS):
            for lv in levels(c):
                join_count[c, lv] = n_join
                n_join += 2
        fox_order = [(0, 0)]
        for hd in range(H):
            fox_order += ([(0, hd + 1)] if hd + 1 < H else []) + ([(2, hd - 1)] if hd else []) + [(1, hd)]
        fox_order.append((2, H - 1))

        def fox_tile(hd, kind):
            return fox_order.index((kind, hd))

        block = ctx.enter_context(nc.Block())

        @block.sync
        def _(sp):
            n_loads, free_at = [0] * SLOTS, [0] * SLOTS

            def load(slot, pieces, frees):
                if free_at[slot]:
                    sp.wait_ge(tile_done, free_at[slot])
                for dst, src in pieces:
                    sp.dma_start(dst, src).then_inc(S(f"slab{slot}"), 16)
                free_at[slot] = frees

            def load_dense(name):
                for q, slot in enumerate(place[name]):
                    load(slot, [(slab(slot, DT), cols(dense[name], 0, DT, 256 * q, 256))],
                         first[name] + 2 * q + 2)

            def load_ffn(n):
                base = first[f"up{n}"]
                w = w_in[n]
                for slot in range(4):
                    load(slot, [(slab(slot, DT), cols(w, 0, DT, slot // 2 * 256 + slot % 2 * FF, 256))], 0)
                with sp.Fori(1, 5) as i:
                    for slot in range(4):
                        sp.wait_ge(tile_done, i * 8 + (base - 8 + 4 * (slot // 2) + 4))
                        src = w[:, bass.ds(i * 512 + (slot // 2 * 256 + slot % 2 * FF), 256)]
                        sp.dma_start(slab(slot, DT), src.rearrange("(k p) m -> p k m", p=P)
                                     ).then_inc(S(f"slab{slot}"), 16)
                for slot in range(4):
                    free_at[slot] = base + 32 + 4 * (slot // 2) + 4
                for slot in (4, 5):
                    load(slot, [(slab(slot, DT), cols(w, 0, DT, 2560 + (slot - 4) * FF, 256))], base + 44)
                for mp in range(4):
                    for s3 in range(3):
                        slot = mp % 2 * 3 + s3
                        k0, k1 = 8 * s3, min(8 * s3 + 8, FT)
                        load(slot, [(slab(slot, k1 - k0), cols(w_out[n], k0, k1, 256 * mp, 256))],
                             first[f"down{n}"] + 2 * mp + 2)

            xt = arena[:, 3 * TW:3 * TW + 3 * D].rearrange("p (g d) -> p g d", g=3)
            sp.dma_start(const[:, :], A["const"]).then_inc(S("const_in"), 16)
            prow = arena[:, 5 * TW:5 * TW + 2 * P].rearrange("p (g d) -> p g d", g=2)
            for name in PARAMS:
                n = PARAM_ROWS.get(name, 1) * DT
                flat = A[name]
                dims = "abc"[:len(flat.shape)]
                if len(dims) > 1:
                    flat = flat.rearrange(" ".join(dims) + " -> (" + " ".join(dims) + ")")
                flat = flat.rearrange("(r c) -> r c", c=P)
                r0 = row_of[name]
                for a, b in ((r0, min(r0 + n, P)), (max(r0, P), r0 + n)):
                    if a < b:
                        sp.dma_start(prow[a % P:a % P + b - a, a // P, :], flat[a - r0:b - r0, :]
                                     ).then_inc(S("param_in"), 16)
            for j, src in enumerate((A["k_norm"], A["fox_q_norm"][0])):
                for e in range(2):
                    r = row_of["head_norms"] + j
                    sp.dma_start(prow[r % P:r % P + 1, 1, e * HD:(e + 1) * HD],
                                 src.rearrange("(a d) -> a d", a=1)).then_inc(S("param_in"), 16)
            sp.dma_start(arena[0:BS, 6 * TW:6 * TW + D], A["state_shift"][0]).then_inc(S("shift_in"), 16)
            for g in range(2):
                sp.dma_start(xt[:, g, :], A["x_prompt"][0, g * P:(g + 1) * P, :]).then_inc(S("x_in"), 16)
            sp.dma_start(xt[0:TS, 2, :], A["x_sample"].rearrange("b t d -> (b t) d")).then_inc(S("x_in"), 16)
            sp.dma_start(w_f, A["w_f"].rearrange("(k p) n -> p k n", p=P)).then_inc(S("wf_in"), 16)
            sp.dma_start(b_f[0:H, :], A["b_f"].rearrange("(h a) -> h a", a=1)).then_inc(S("wf_in"), 16)
            sp.dma_start(pt_sb[:, :], A["page_table"].rearrange("(a b) n -> a (b n)", a=1)).then_inc(S("pt_in"), 16)

            load_ffn(0)
            for name in "rkv":
                load_dense(name)
            load(LORA1, [(lo1[:, :, 0:64], A["rw_w1"][0].rearrange("(k p) m -> p k m", p=P)),
                         (lo1[:, :, 64:128], A["rw_a1"][0].rearrange("(k p) m -> p k m", p=P)),
                         (lo1[:, :, 128:256], A["rw_g1"][0].rearrange("(k p) m -> p k m", p=P))],
                 first["g1"] + 1)
            load(LORA2, [(ring[0:64, LORA2, 0:D], A["rw_w2"][0]),
                         (ring[0:64, LORA2, D:2 * D], A["rw_a2"][0])], first["a2"] + DT)
            load(LORA3, [(ring[:, LORA3, 0:D], A["rw_g2"][0])], first["g2"] + DT)
            load_dense("wo")
            for slot in range(4):
                free_at[slot] = first["wo"] + 1
            for j in range(2):
                sp.wait_ge(S(f"state_out{j}"), 16 * HP)
            load_ffn(1)
            load_dense("kk")
            load_dense("vv")
            load_ffn(2)
            load_dense("q")
            sp.wait_ge(tile_done, free_at[0])
            sp.dma_start(ring[0:H, 0, :], A["head_sel"]).then_inc(S("head_sel_in"), 16)
            load_dense("fo")
            sp.wait_ge(S("pt_in"), 16)
            sp.wait_ge(S("page_space"), 1)
            with sp.Fori(0, BS) as b:
                for j in range(PAGES):
                    page = sp.value_load(pt_sb[0:1, bass.ds(b * PAGES + j, 1)], min_val=0,
                                         max_val=A["cache_k"].shape[0] - 1)
                    sp.wait_ge(S("k_page_free"), b * PAGES + (j + 1))
                    sp.dma_start(k_page(j % 4), A["cache_k"][bass.ds(page, 1)].rearrange("a t h d -> (a t) (h d)")
                                 ).then_inc(S(f"k_page{j % 4}"), 16)
                for j in range(PAGES):
                    page = sp.value_load(pt_sb[0:1, bass.ds(b * PAGES + j, 1)], min_val=0,
                                         max_val=A["cache_k"].shape[0] - 1)
                    if j == 0:
                        sp.wait_ge(S("v_pages_free"), b + 1)
                    sp.dma_start(v_page(j), A["cache_v"][bass.ds(page, 1)].rearrange("a t h d -> (a t) (h d)")
                                 ).then_inc(S(f"v_page{j}"), 16)
            for slot in (0, 1):
                free_at[slot] = first["fo"] + 1
            load_ffn(3)
        @block.tensor
        def _(pe):
            loaded = [0] * SLOTS

            def begin(t):
                if t >= 8:
                    who = owner[t - 8]
                    pe.wait_ge({"d": dve_freed, "a": act_freed}[who], freed[who][t - 7])

            def end(mm):
                mm.then_inc(tile_done, 1)

            def slab_in(slot, pieces=1):
                loaded[slot] += 16 * pieces
                pe.wait_ge(S(f"slab{slot}"), loaded[slot])

            def dve_done(t):
                pe.wait_ge(dve_freed, freed["d"][t + 1])

            def act_done(t):
                pe.wait_ge(act_freed, freed["a"][t + 1])

            def norm(name):
                i, t = norms.index(name), first["norm_" + name]
                begin(t)
                for k in range(DT):
                    pe.wait_ge(S("sq_ready"), i * DT + k + 1)
                    mm = pe.matmul(bank(t, T), ones, sq[:, k, :], start=(k == 0), stop=(k == DT - 1))
                end(mm)

            def gemm(name, rhs, ready=None):
                for q, slot in enumerate(place[name]):
                    slab_in(slot)
                    for mt in range(2):
                        t = first[name] + 2 * q + mt
                        begin(t)
                        for k in range(DT):
                            if ready and q == mt == 0:
                                pe.wait_ge(ready[0], ready[1] + k + 1)
                            mm = pe.matmul(bank(t, T), slab(slot, DT)[:, k, mt * P:(mt + 1) * P], rhs[:, k, :],
                                           start=(k == 0), stop=(k == DT - 1))
                        end(mm)

            def xn_ready(name):
                return S("xn_ready"), norms.index(name) * DT

            def ffn(n):
                norm(f"ffn{n}")
                base = first[f"up{n}"]
                d0 = freed["d"][base]
                pe.wait_ge(act_freed, freed["a"][base])
                pe.wait_ge(S("xn_ready"), xn_ready(f"ffn{n}")[1] + DT)

                def up(pr, mt, e, slot):
                    b_ = (base + 4 * pr + 2 * mt + e) % 8
                    for k in range(DT):
                        mm = pe.matmul(ps[:, b_, 0:T], slab(slot, DT)[:, k, mt * P:(mt + 1) * P], xn[:, k, :],
                                       start=(k == 0), stop=(k == DT - 1))
                    end(mm)

                with pe.Fori(0, 5) as i:
                    for pr in range(2):
                        for e in range(2):
                            pe.wait_ge(S(f"slab{2 * pr + e}"), i * 16 + (loaded[2 * pr + e] + 16))
                        for mt in range(2):
                            for e in range(2):
                                j = 4 * pr + 2 * mt + e
                                pe.wait_ge(dve_freed, i * 8 + (d0 + j - 7))
                                up(pr, mt, e, 2 * pr + e)
                for slot in range(4):
                    loaded[slot] += 80
                for slot in (4, 5):
                    slab_in(slot)
                for mt in range(2):
                    for e in range(2):
                        begin(base + 40 + 2 * mt + e)
                        up(0, mt, e, 4 + e)
                down = first[f"down{n}"]
                for mp in range(4):
                    for s3 in range(3):
                        slot = mp % 2 * 3 + s3
                        k0, k1 = 8 * s3, min(8 * s3 + 8, FT)
                        slab_in(slot)
                        for mt in range(2):
                            t = down + 2 * mp + mt
                            if s3 == 0:
                                begin(t)
                            for k in range(k0, k1):
                                if mp == mt == 0:
                                    dve_done(base + 2 * k + 1)
                                mm = pe.matmul(bank(t, T), slab(slot, k1 - k0)[:, k - k0, mt * P:(mt + 1) * P],
                                               hid[:, k, :], start=(k == 0), stop=(k == FT - 1))
                            if s3 == 2:
                                end(mm)

            prow = arena[:, 5 * TW:5 * TW + 2 * P].rearrange("p (g d) -> p g d", g=2)
            xt = arena[:, 3 * TW:3 * TW + 3 * D].rearrange("p (g d) -> p g d", g=3)
            pe.sem_inc(S("k_page_free"), 4)
            pe.sem_inc(S("v_pages_free"), 1)
            pe.sem_inc(S("kT_act"), 2)
            pe.sem_inc(S("kT_dve"), 2)
            pe.sem_inc(S("s_done"), 1)
            pe.wait_ge(S("const_in"), 16)
            pe.wait_ge(S("param_in"), 16 * N_PARAM_DMAS)
            t = first["params"]
            end(pe.transpose(bank(t, P), prow[:, 0, :], ident))
            end(pe.transpose(bank(t + 1, rows - P), prow[0:rows - P, 1, :], ident[0:rows - P, 0:rows - P]))
            pe.wait_ge(S("shift_in"), 16)
            t = first["shift_in"]
            for m in range(DT):
                mm = pe.transpose(ps[:, t % 8, m * BS:(m + 1) * BS],
                                  arena[0:BS, 6 * TW + m * P:6 * TW + (m + 1) * P], ident[0:BS, 0:BS])
            end(mm)
            pe.wait_ge(S("x_in"), 48)
            for m in range(DT):
                t = first["x"] + m
                begin(t)
                for g, n in ((0, P), (1, P), (2, TS)):
                    mm = pe.transpose(ps[:, t % 8, g * P:g * P + n], xt[0:n, g, m * P:(m + 1) * P],
                                      ident[0:n, 0:n])
                end(mm)

            ffn(0)
            norm("mix0")

            pe.wait_ge(S("shift_cols"), 1)
            for j in range(2):
                t = first["shift_out"] + j
                begin(t)
                for m in range(4):
                    mm = pe.transpose(ps[0:BS + 1, t % 8, m * P:(m + 1) * P], shc[:, 4 * j + m, :], ident)
                end(mm)

            xs = [A_(1), A_(2)]
            for j, name in enumerate("rkv"):
                gemm(name, xs[j % 2], (S("xs_ready"), j * DT))
            slab_in(LORA1, 3)
            slab_in(LORA2, 2)
            slab_in(LORA3)
            for j, (name, c0, c1, w2, out) in enumerate((
                    ("w", 0, 64, ring[0:64, LORA2, 0:D], root[0:64, :]),
                    ("a", 64, 128, ring[0:64, LORA2, D:2 * D], rs[0:64, :]),
                    ("g", 128, 256, ring[:, LORA3, 0:D], root[:, :]))):
                t = first[name + "1"]
                begin(t)
                for k in range(DT):
                    pe.wait_ge(S("xs_ready"), (3 + j) * DT + k + 1)
                    mm = pe.matmul(ps[0:c1 - c0, t % 8, 0:T], lo1[:, k, c0:c1], xs[(3 + j) % 2][:, k, :],
                                   start=(k == 0), stop=(k == DT - 1))
                end(mm)
                (dve_done if name == "a" else act_done)(t)
                for m in range(DT):
                    t = first[name + "2"] + m
                    begin(t)
                    end(pe.matmul(bank(t, T), w2[:, m * P:(m + 1) * P], out, start=True, stop=True))

            def head_sums(name, src, ready):
                for m in range(DT):
                    t = first[name] + m
                    begin(t)
                    pe.wait_ge(ready, m + 1)
                    end(pe.matmul(bank(t, T), pair, src[:, m, :], start=True, stop=True))

            head_sums("kk_norm", A_(1), S("kk_sq"))
            head_sums("bonus", bonus, S("rk_ready"))

            for b in range(BS):
                t = first["state_in"] + b
                begin(t)
                pe.wait_ge(S(f"state_in{b % 2}"), 16 * (b // 2 + 1))
                for p in range(HP):
                    mm = pe.transpose(ps[:, t % 8, p * HD:(p + 1) * HD],
                                      state_in[b % 2][0:HD, p * P:(p + 1) * P], ident[0:HD, 0:HD])
                end(mm)

            def halves(name, body, *waits):
                for hf in range(2):
                    t = first[name] + hf
                    begin(t)
                    for w in waits:
                        w(hf)
                    for q in range(4):
                        mm = body(4 * hf + q, t % 8, q)
                    end(mm)

            def mmul(out, lhsT, rhs, start=True, stop=True):
                return pe.matmul(out, lhsT, rhs, start=start, stop=stop)

            for c in range(CHUNKS):
                sample = c == CHUNKS - 1

                def R_c(p):
                    return Rf[:, p, c * C:(c + 1) * C]

                def o(b_, q, n=P, off=0):
                    return ps[:, b_, q * P + off:q * P + off + n]

                halves(f"LT{c}", lambda p, b_, q: mmul(o(b_, q), B_bd[:, p, :], A_bd[:, p, :]),
                       lambda hf: pe.wait_ge(S("bd_ready"), 4 * (2 * c + hf) + 4))
                halves(f"KA{c}", lambda p, b_, q: mmul(o(b_, q), K_bd[:, p, :], A_bd[:, p, :]))

                def grams(p, b_, q):
                    mmul(o(b_, q, C), B_bd[:, p, :], R_c(p))
                    return mmul(o(b_, q, C, C), K_bd[:, p, :], R_c(p))
                halves(f"RG{c}", grams)
                for j, src in enumerate((V_bd, B_bd, K_bd)):
                    for hf in range(2):
                        t = first[f"tok{c}"] + 2 * j + hf
                        begin(t)
                        for q in range(4):
                            mm = pe.transpose(o(t % 8, q), src[:, 4 * hf + q, :], ident)
                        end(mm)
                halves(f"D{c}", lambda p, b_, q: pe.transpose(o(b_, q), DT_bd[:, p, :], ident),
                       lambda hf: pe.wait_ge(S("DT_ready"), 2 * c + hf + 1))
                lvs = levels(c)
                for n_lv, lv in enumerate(lvs):
                    prev = f"D{c}" if lv == lvs[0] else f"DD{c}_{lvs[n_lv - 1]}"
                    halves(f"Z{c}_{lv}", lambda p, b_, q: mmul(o(b_, q), join_bd[:, p, :], D_bd[:, p, :]),
                           lambda hf: pe.wait_ge(S("join_ready"), join_count[c, lv] + hf + 1),
                           lambda hf: dve_done(first[prev] + hf))
                    if lv != lvs[0]:
                        dve_done(first[f"DDT{c}_{lvs[n_lv - 1]}"] + 1)
                    if lv != lvs[-1]:
                        halves(f"DD{c}_{lv}", lambda p, b_, q: mmul(o(b_, q), DT_bd[:, p, :], Z_bd[:, p, :]),
                               lambda hf: act_done(first[f"Z{c}_{lv}"] + hf))
                    halves(f"DDT{c}_{lv}", lambda p, b_, q: mmul(o(b_, q), Z_bd[:, p, :], DT_bd[:, p, :]),
                           lambda hf: act_done(first[f"Z{c}_{lv}"] + hf))
                if sample:
                    for hf in range(2):
                        t = first["own_state"] + hf
                        begin(t)
                        for q in range(4):
                            p = 4 * hf + q
                            pe.wait_ge(S("S0_ready"), p + 1)
                            s0 = S0_bd[p % 2].rearrange("p m c -> p (m c)").rearrange("p (b c) -> p b c", b=BS)
                            for e, src in enumerate((Af, Rf)):
                                for b in range(BS):
                                    cc = TP + b * QS
                                    mm = mmul(ps[:, t % 8, q * P + e * C + b * QS:q * P + e * C + (b + 1) * QS],
                                              s0[:, b, :], src[:, p, cc:cc + QS])
                            if q < 3:
                                mm.then_inc(S("S0_used"), 1)
                            else:
                                end(mm)

                def solve_rhs(p, b_, q):
                    if c > 0:
                        mmul(o(b_, q), XT_bd[:, p, :] if sample else A_bd[:, p, :],
                             ident if sample else S_bd[:, p, :], True, False)
                    return mmul(o(b_, q), KA_bd[:, p, :], V_tok[:, p, :], c == 0, True)
                halves(f"X{c}", solve_rhs,
                       lambda hf: act_done(first[f"tok{c}"] + 1),
                       lambda hf: dve_done(first["own_state"] + hf if sample else
                                           first[f"S{c - 1}"] + hf if c else first[f"KA{c}"] + hf))
                halves(f"U{c}", lambda p, b_, q: mmul(o(b_, q), DT_bd[:, p, :], X_bd[:, p, :]),
                       lambda hf: act_done(first[f"X{c}"] + hf),
                       lambda hf: dve_done(first[f"DDT{c}_{lvs[-1]}"] + hf))

                def outputs(p, b_, q):
                    if c > 0 and not sample:
                        mmul(o(b_, q, C), S_bd[:, p, :], R_c(p), True, False)
                    mmul(o(b_, q, C), X_bd[:, p, :], RG_bd[:, p, 0:C], c == 0 or sample, False)
                    return mmul(o(b_, q, C), V_tok[:, p, :], RG_bd[:, p, C:2 * C], False, True)
                halves(f"Y{c}", outputs, lambda hf: act_done(first[f"U{c}"] + hf))
                if not sample:
                    def states(p, b_, q):
                        mmul(o(b_, q), B_tok[:, p, :], X_bd[:, p, :], True, False)
                        return mmul(o(b_, q), K_tok[:, p, :], V_tok[:, p, :], False, True)
                    halves(f"S{c}", states)
                    if c == CHUNKS - 2:
                        halves("wkv_prompt", lambda p, b_, q: pe.transpose(o(b_, q), S_bd[:, p, :], ident),
                               lambda hf: dve_done(first[f"S{c}"] + hf))
            for p in range(HP):
                t = first[f"SS{p}"]
                begin(t)
                pe.wait_ge(S("uv_ready"), 2 * p + 2)
                mmul(bank(t), B_tok[:, p, :], UV[p % 2][:, 0, :, :], True, False)
                end(mmul(bank(t), K_tok[:, p, :], UV[p % 2][:, 1, :, :], False, True))
                dve_done(t)
                for j in range(2):
                    t = first[f"ST{p}"] + j
                    begin(t)
                    for q in range(4):
                        mm = pe.transpose(ps[0:HD, t % 8, q * P:(q + 1) * P], SF[:, p % 2, 4 * j + q, :], ident)
                    end(mm)

            head_sums("mean", Yf, S("y_ready"))
            head_sums("var", A_(0), S("y_sq"))
            gemm("wo", Yf, (S("wo_in"), 0))
            ffn(1)

            norm("kv")
            gemm("kk", xn, xn_ready("kv"))
            gemm("vv", xn)
            t = first["logf"]
            begin(t)
            pe.wait_ge(S("wf_in"), 32)
            for k in range(DT):
                mm = mmul(ps[0:H, t % 8, 0:T], w_f[:, k, :], xn[:, k, :], k == 0, k == DT - 1)
            end(mm)
            head_sums("k_norm", A_(4), S("k_sq"))
            t = first["logf_tok"]
            begin(t)
            pe.wait_ge(S("logf_ready"), 2)
            for e, src in enumerate((LF, FT_)):
                for g, n in ((0, P), (1, P), (2, TS)):
                    mm = pe.transpose(ps[0:n, t % 8, (3 * e + g) * H:(3 * e + g + 1) * H],
                                      src[:, g * P:g * P + n], ident[0:H, 0:H])
            end(mm)

            def to_tokens(name, src, ready):
                for g, n in ((0, P), (1, P), (2, TS)):
                    for j in range(2):
                        t = first[name] + 2 * g + j
                        begin(t)
                        for m in range(4):
                            if g == 0:
                                ready(4 * j + m)
                            mm = pe.transpose(ps[0:n, t % 8, m * P:(m + 1) * P],
                                              src[:, 4 * j + m, g * P:g * P + n], ident)
                        end(mm)

            to_tokens("k_tok", kT, lambda m: pe.wait_ge(S("k_ready"), 1))
            to_tokens("v_tok", A_(9), lambda m: dve_done(first["vv"] + 7))
            ffn(2)

            norm("mix1")
            gemm("q", xn, xn_ready("mix1"))
            head_sums("q_norm", A_(7), S("q_sq"))
            t = first["fq_col"]
            begin(t)
            end(mmul(bank(t, TS), K("selcol")[0:H, :], FT_[:, TP:T]))
            pe.wait_ge(S("lfp_in"), 16 * BS * PAGES)
            for j in range(4):
                t = first["fk_past"] + j
                begin(t)
                end(mmul(bank(t), K("later") if j < 2 else ones,
                         lfp.rearrange("p b j h -> p (b j h)")[:, j % 2 * 512:j % 2 * 512 + 512]))
            pe.wait_ge(S("head_sel_in"), 16)
            pe.wait_ge(S("nF_ready"), 1)
            for hd in range(H):
                t = first["fb"] + hd
                begin(t)
                end(mmul(bank(t, 384), head_sel[:, hd, :], nF_dup))

            def scores(hd):
                t = first["fox"] + fox_tile(hd, 0)
                begin(t)
                pe.wait_ge(S("qp_ready"), hd // 2 + 1)
                qp = qp_bd[:, hd // 2 % 2, hd % 2, :]
                mmul(ps[:, t % 8, 0:P], qp[:, 0:P], kT[:, hd // 2, 0:P])
                end(mmul(ps[:, t % 8, P:3 * P], qp[:, P:2 * P], kT[:, hd // 2, 0:2 * P]))

            def turn(hd):
                t = first["fox"] + fox_tile(hd, 1)
                begin(t)
                pe.wait_ge(S("p_ready"), 2 * hd + 2)
                for j in range(3):
                    mm = pe.transpose(ps[:, t % 8, j * P:(j + 1) * P], s_pr[:, hd % 2, j * P:(j + 1) * P], ident)
                end(mm)

            def values(hd):
                t = first["fox"] + fox_tile(hd, 2)
                begin(t)
                dve_done(first["fox"] + fox_tile(hd, 1))
                vc = slice(hd // 2 * P, (hd // 2 + 1) * P)
                mmul(ps[:, t % 8, 0:P], v_tok[:, 0, vc], pT[:, hd % 2, 0:P])
                mmul(ps[:, t % 8, P:2 * P], v_tok[:, 0, vc], pT[:, hd % 2, P:2 * P], True, False)
                end(mmul(ps[:, t % 8, P:2 * P], v_tok[:, 1, vc], pT[:, hd % 2, 2 * P:3 * P], False, True))

            for kind, hd in fox_order:
                (scores, turn, values)[kind](hd)

            def unit_scores(b, u):
                pe.wait_ge(S("kT_act"), b * PAGES + (2 * u + 4))
                pe.wait_ge(S("kT_dve"), b * PAGES + (2 * u + 4))
                bk, c0 = u // 2, u % 2 * 256
                for j in range(2):
                    pe.matmul(ps[:, bk, c0 + j * P:c0 + (j + 1) * P],
                              nfk_rep[:, (2 * u + j) * P:(2 * u + j + 1) * P], ident,
                              start=(j == 0), stop=False, skip_group_check=True)
                for r in range(2):
                    for g in range(4):
                        mm = pe.matmul(ps[32 * g:32 * g + 32, bk, c0:c0 + 256],
                                       q_cur[:, (2 * g + r) * 32:(2 * g + r + 1) * 32],
                                       k_feat[u % 2][:, 2 * g + r, :],
                                       start=False, stop=(r == 1), skip_group_check=True)
                return mm

            dve_done(first["fox"] + 3 * H - 1)
            with pe.Fori(0, BS) as b:
                for j in range(PAGES):
                    kb = 3 + j % 2 * 2
                    pe.wait_ge(S(f"k_page{j % 4}"), b * 32 + (16 * (j // 4 + 1)))
                    pe.wait_ge(S("kT_act"), b * PAGES + (j + 1))
                    pe.wait_ge(S("kT_dve"), b * PAGES + (j + 1))
                    for m in range(DT):
                        mm = pe.transpose(ps[:, kb + m // 4, m % 4 * P:(m % 4 + 1) * P],
                                          k_page(j % 4)[:, m * P:(m + 1) * P], ident)
                    mm.then_inc(S("k_page_free"), 1)
                    if j == 2:
                        pe.wait_ge(S("q_cur"), b * 4 + 4)
                        pe.wait_ge(S("nfk_rep"), b + 1)
                    if j >= 2 and j % 2 == 1:
                        unit_scores(b, j // 2 - 1)
                unit_scores(b, 3)
                for r in range(2):
                    for g in range(4):
                        mm = mmul(ps[32 * g:32 * g + 32, 2, 0:TS], q_cur[:, (2 * g + r) * 32:(2 * g + r + 1) * 32],
                                  kT[:, 2 * g + r, TP:T], r == 0, r == 1)
                mm.then_inc(S("s_done"), 1)
                pe.wait_ge(S("p_row"), b * 2 + 2)
                for j in range(PAGES):
                    pe.transpose(ps[:, j // 4, j % 4 * P:(j % 4 + 1) * P], p_row[:, j * P:(j + 1) * P], ident)
                pe.transpose(ps[0:TS, 2, P:2 * P], p_row[:, PAST:PAST + TS], ident).then_inc(S("p_turned"), 1)
                pe.wait_ge(S("pT_act"), b + 1)
                pe.wait_ge(S("pT_dve"), b * 2 + 2)
                for j in range(PAGES + 1):
                    if j < PAGES:
                        pe.wait_ge(S(f"v_page{j}"), b * 16 + 16)
                    for g in range(4):
                        v = v_page(j) if j < PAGES else v_tok[0:TS, 2, :]
                        mm = mmul(ps[32 * g:32 * g + 32, 7, 0:256], p_T[0:v.shape[0], j, 32 * g:32 * g + 32],
                                  v[:, 256 * g:256 * g + 256], j == 0, j == PAGES)
                mm.then_inc(S("v_pages_free"), 1)
                pe.wait_ge(S("o_own"), b * 2 + 2)
                pe.transpose(ps[:, 7, 256:384], o_two, ident).then_inc(S("o_turned"), 1)
            pe.wait_ge(S("fox_out"), 2 * BS)
            gemm("fo", oT)
            ffn(3)
            to_tokens("y", h, lambda m: dve_done(first["down3"] + m))
        @block.scalar
        def _(act):
            def filled(t):
                act.wait_ge(tile_done, t + 1)

            def squares(name):
                i, src = norms.index(name), first[norm_src[name]]
                for m in range(DT):
                    act.wait_ge(dve_freed, freed["d"][src + m + 1])
                    act.activation(sq[:, m, :], h[:, m, :], ACT.Square).then_inc(S("sq_ready"), 1)

            def norm(name):
                squares(name)
                i, t = norms.index(name), first["norm_" + name]
                filled(t)
                if i:
                    act.wait_ge(S("rs_ready"), i)
                if name == "mix0":
                    pass
                act.activation(root[:, :], bank(t, T), ACT.Sqrt, bias=eps, scale=1.0 / D).then_inc(act_freed, 1)

            def ffn(n):
                norm(f"ffn{n}")
                base = first[f"up{n}"]
                with act.Fori(0, 5) as i:
                    for g in range(4):
                        act.wait_ge(tile_done, i * 8 + (base + 2 * g + 1))
                        act.activation(sg[:, g, :], ps[:, (base + 2 * g) % 8, 0:T], ACT.Silu
                                       ).then_inc(S("silu_ready"), 1)
                for g in range(2):
                    filled(base + 40 + 2 * g)
                    act.activation(sg[:, g, :], bank(base + 40 + 2 * g, T), ACT.Silu).then_inc(S("silu_ready"), 1)

            act.wait_ge(S("eps_ready"), 2)
            ffn(0)
            norm("mix0")
            def lora(name, func, mid, out, bias):
                t = first[name + "1"]
                if name != "a":
                    filled(t)
                    n = HD if name == "w" else P
                    if name == "w":
                        act.wait_ge(S("rs_ready"), 2)
                    else:
                        filled(first["w2"] + 7)
                    act.activation(mid, ps[0:n, t % 8, 0:T], func).then_inc(act_freed, 1)
                if bias:
                    for m in range(DT):
                        filled(first[name + "2"] + m)
                        act.activation(out[:, m, :], bank(first[name + "2"] + m, T), ACT.Sigmoid,
                                       bias=prm(bias, m)).then_inc(act_freed, 1)

            lora("w", ACT.Tanh, root[0:HD, :], A_(6), "rw_w0")
            lora("a", None, None, A_(7), "rw_a0")
            lora("g", ACT.Sigmoid, root[:, :], None, None)
            for m in range(DT):
                act.wait_ge(S("kk_raw"), m + 1)
                act.activation(A_(1)[:, m, :], A_(0)[:, m, :], ACT.Square).then_inc(S("kk_sq"), 1)
            act.wait_ge(dve_freed, freed["d"][first["kk_norm"] + DT])
            act.activation(A_(1), A_(1), ACT.Sqrt).then_inc(S("kk_root"), 1)
            act.wait_ge(S("decay_sums"), 1)
            act.activation(A_(10), A_(9), ACT.Exp, scale=-DECAY).then_inc(S("decays"), 1)
            act.wait_ge(S("a_used"), 1)
            act.activation(A_(7), A_(9), ACT.Exp, scale=DECAY).then_inc(S("decays"), 1)
            act.activation(A_(6), A_(6), ACT.Exp, scale=-DECAY).then_inc(S("decays"), 1)

            def copy_halves(name, dst):
                for hf in range(2):
                    filled(first[name] + hf)
                    act.activation(dst[:, 4 * hf:4 * hf + 4, :], bank(first[name] + hf), ACT.Copy
                                   ).then_inc(act_freed, 1)

            for c in range(CHUNKS):
                for j, dst in enumerate((V_tok, B_tok, K_tok)):
                    for hf in range(2):
                        t = first[f"tok{c}"] + 2 * j + hf
                        filled(t)
                        act.activation(dst[:, 4 * hf:4 * hf + 4, :], bank(t), ACT.Copy).then_inc(act_freed, 1)
                for lv in levels(c):
                    copy_halves(f"Z{c}_{lv}", Z_bd)
                copy_halves(f"X{c}", X_bd)
                copy_halves(f"U{c}", X_bd)
            for p in range(HP):
                if p >= 2:
                    act.wait_ge(S(f"state_out{p % 2}"), 32 * (p // 2))
                for j in range(2):
                    filled(first[f"ST{p}"] + j)
                    act.activation(state_out[p % 2][0:HD, j * 512:(j + 1) * 512], bank(first[f"ST{p}"] + j, 512, HD),
                                   ACT.Copy).then_inc(act_freed, 1)
            for m in range(DT):
                act.wait_ge(dve_freed, freed["d"][first["mean"] + m + 1])
                act.activation(A_(0)[:, m, :], Yf[:, m, :], ACT.Square).then_inc(S("y_sq"), 1)
            for m in range(DT):
                filled(first["var"] + m)
                act.activation(A_(1)[:, m, :], bank(first["var"] + m, T), ACT.Sqrt, bias=eps_ln, scale=1.0 / HD
                               ).then_inc(act_freed, 1)
            ffn(1)
            norm("kv")

            def head_roots(name, src_name, src, dst, sq_sem):
                for m in range(DT):
                    act.wait_ge(dve_freed, freed["d"][first[src_name] + m + 1])
                    act.activation(dst[:, m, :], src[:, m, :], ACT.Square).then_inc(S(sq_sem), 1)
                for m in range(DT):
                    filled(first[name] + m)
                    act.activation(dst[:, m, :], bank(first[name] + m, T), ACT.Sqrt, bias=eps, scale=1.0 / HD
                                   ).then_inc(act_freed, 1)

            head_roots("k_norm", "kk", kT, A_(4), "k_sq")
            act.wait_ge(S("logf_arg"), 1)
            act.activation(lw[1], lw[1], ACT.Exp).then_inc(S("logf_exp"), 1)
            ffn(2)
            norm("mix1")
            head_roots("q_norm", "q", q_f, A_(7), "q_sq")
            for hd in range(H):
                act.wait_ge(S("s_ready"), 2 * hd + 2)
                s = s_pr[:, hd % 2, :]
                st = fstat[:, hd % 2, :]
                act.activation(s[:, 0:P], s[:, 0:P], ACT.Exp, bias=st[:, 4:5], accum_out=st[:, 6:7]
                               ).then_inc(S("e_ready"), 1)
                act.activation(s[:, P:3 * P], s[:, P:3 * P], ACT.Exp, bias=st[:, 5:6], accum_out=st[:, 7:8]
                               ).then_inc(S("e_ready"), 1)
            with act.Fori(0, BS) as b:
                if True:
                    act.wait_ge(S("s_done"), b + 1)
                    nf = nfk[:, bass.ds(b, 1), :, :].rearrange("p b j h -> p (b j h)")
                    act.activation(nfk_rep.rearrange("p (n q) -> p n q", q=QS),
                                   nf.unsqueeze(2).to_broadcast([P, PAGES * H, QS]), ACT.Copy
                                   ).then_inc(S("nfk_rep"), 1)
                for j in range(PAGES):
                    act.wait_ge(S("k_page_free"), b * PAGES + (j + 5))
                    act.activation(k_feat[j // 2 % 2][:, 0:4, j % 2 * P:(j % 2 + 1) * P],
                                   ps[:, 3 + j % 2 * 2, :].rearrange("p (m t) -> p m t", m=4), ACT.Copy
                                   ).then_inc(S("kT_act"), 1)
                act.wait_ge(S("less_max"), b + 1)
                act.activation(p_row[:, 0:PAST], ps[:, 0:2, :].rearrange("p g c -> p (g c)"), ACT.Exp,
                               bias=sst[:, 4:5], accum_out=sst[:, 6:7]).then_inc(S("p_row"), 1)
                act.activation(p_row[:, PAST:PAST + TS], s_new, ACT.Exp,
                               bias=sst[:, 4:5], accum_out=sst[:, 7:8]).then_inc(S("p_row"), 1)
                act.wait_ge(S("p_turned"), b + 1)
                act.activation(p_T[:, 0:4, :], ps[:, 0, :].rearrange("p (g c) -> p g c", g=4), ACT.Copy
                               ).then_inc(S("pT_act"), 1)
            ffn(3)

        @block.vector
        def _(dve):
            steps = [0]

            def link(ins):
                steps[0] += 1
                ins.then_inc(S("dve_step"), 1)
                dve.wait_ge(S("dve_step"), steps[0])

            def filled(t):
                dve.wait_ge(tile_done, t + 1)

            def free(ins, n=1):
                ins.then_inc(dve_freed, n)

            TT, TS_, STT, CP = dve.tensor_tensor, dve.tensor_scalar, dve.scalar_tensor_tensor, dve.tensor_copy

            def norm(name, param, row):
                i, t = norms.index(name), first["norm_" + name]
                dve.wait_ge(act_freed, freed["a"][t + 1])
                dve.reciprocal(rs[:, :], root[:, :]).then_inc(S("rs_ready"), 1)
                dve.wait_ge(S("rs_ready"), i + 1)
                for m in range(DT):
                    STT(xn[:, m, :], h[:, m, :], prm(param, m, row), rs[:, :], ALU.mult, ALU.mult
                        ).then_inc(S("xn_ready"), 1)

            def ffn(n):
                norm(f"ffn{n}", "ffn_norm", n)
                base = first[f"up{n}"]
                with dve.Fori(0, 5) as i:
                    for g in range(4):
                        dve.wait_ge(S("silu_ready"), i * 4 + (n * FT + g + 1))
                        dve.wait_ge(tile_done, i * 8 + (base + 2 * g + 2))
                        free(TT(hid[:, bass.ds(i * 4 + g, 1), :], sg[:, g:g + 1, :],
                                ps[:, (base + 2 * g + 1) % 8:(base + 2 * g + 1) % 8 + 1, 0:T], ALU.mult), 2)
                for g in range(2):
                    dve.wait_ge(S("silu_ready"), n * FT + 20 + g + 1)
                    filled(base + 41 + 2 * g)
                    free(TT(hid[:, 20 + g, :], sg[:, g, :], bank(base + 41 + 2 * g, T), ALU.mult), 2)
                for m in range(DT):
                    filled(first[f"down{n}"] + m)
                    free(STT(h[:, m, :], bank(first[f"down{n}"] + m, T), 0.5, h[:, m, :], ALU.mult, ALU.add))

            dve.memset(eps, RMS_EPS).then_inc(S("eps_ready"), 1)
            dve.memset(eps_ln, LNX_EPS).then_inc(S("eps_ready"), 1)
            t = first["params"]
            filled(t)
            free(CP(par[:, 0, :], bank(t, P)))
            filled(t + 1)
            free(CP(par[:, 1, 0:rows - P], bank(t + 1, rows - P)))
            dve.wait_ge(dve_freed, 2)
            link(TS_(omka, par[:, row_of["rw_k_a"] // P, row_of["rw_k_a"] % P:row_of["rw_k_a"] % P + DT],
                     -1.0, 1.0, ALU.mult, ALU.add))
            filled(first["shift_in"])
            free(CP(shT.rearrange("p m b -> p (m b)"), bank(first["shift_in"], DT * BS)))
            for m in range(DT):
                filled(first["x"] + m)
                free(CP(h[:, m, :], bank(first["x"] + m, T)))
            dve.wait_ge(dve_freed, freed["d"][first["x"] + DT])
            ffn(0)
            dve.wait_ge(dve_freed, freed["d"][first["down0"] + DT])
            norm("mix0", "mix_norm", 0)
            dve.wait_ge(S("xn_ready"), 2 * DT)
            CP(shc[:, :, 0:1], xn[:, :, TP - 1:TP])
            xs_sample = xn[:, :, TP:T].rearrange("p m (b t) -> p m b t", b=BS)
            link(CP(shc[:, :, 1:BS + 1], xs_sample[:, :, :, QS - 1]))
            dve.sem_inc(S("shift_cols"), 1)
            df = A_(0)
            df_s = df[:, :, TP:T].rearrange("p m (b t) -> p m b t", b=BS)
            TT(df[:, :, 1:TP], xn[:, :, 0:TP - 1], xn[:, :, 1:TP], ALU.subtract)
            TS_(df[:, :, 0:1], xn[:, :, 0:1], -1.0, None, ALU.mult)
            TT(df_s[:, :, :, 1:QS], xs_sample[:, :, :, 0:QS - 1], xs_sample[:, :, :, 1:QS], ALU.subtract)
            link(TT(df_s[:, :, :, 0], shT, xs_sample[:, :, :, 0], ALU.subtract))

            def mixed(j):
                if j >= 2:
                    filled(first[["r", "k", "v", "w1", "a1", "g1"][j - 2]] + (7 if j < 5 else 0))
                for m in range(DT):
                    STT(A_(1 + j % 2)[:, m, :], df[:, m, :], prm("rw_mu", m, j), xn[:, m, :], ALU.mult, ALU.add
                        ).then_inc(S("xs_ready"), 1)

            def copy_out(name, dst):
                for m in range(DT):
                    filled(first[name] + m)
                    free(CP(dst[:, m, :], bank(first[name] + m, T)))

            for j in range(2):
                t = first["shift_out"] + j
                filled(t)
                free(CP(A_(9)[0:BS + 1, :, :].rearrange("p m t -> p (m t)")[:, j * 512:(j + 1) * 512],
                        bank(t, 512, BS + 1)))
            mixed(0)
            mixed(1)
            copy_out("r", Rf)
            mixed(2)
            copy_out("k", Kf)
            mixed(3)
            copy_out("v", Vf)
            mixed(4)
            mixed(5)
            filled(first["a1"])
            free(CP(rs[0:HD, :], bank(first["a1"], T, HD)))
            copy_out("g2", gf)
            dve.wait_ge(dve_freed, freed["d"][first["g2"] + DT])
            kk, b_, aa = A_(0), A_(1), A_(7)
            for m in range(DT):
                TS_(kk[:, m, :], Kf[:, m, :], prm("rw_k_k", m), None, ALU.mult).then_inc(S("kk_raw"), 1)
            dve.wait_ge(act_freed, freed["a"][first["a2"] + DT])
            tmp = A_(2)
            for m in range(DT):
                ins = TS_(tmp[:, m, :], aa[:, m, :], prm("rw_k_a", m), omka[:, m:m + 1], ALU.mult, ALU.add)
            link(ins)
            link(TT(Kf, Kf, tmp, ALU.mult))
            for m in range(DT):
                STT(bonus[:, m, :], Rf[:, m, :], prm("rw_r_k", m), Kf[:, m, :], ALU.mult, ALU.mult
                    ).then_inc(S("rk_ready"), 1)
            sig, cum = A_(6), A_(9)
            dve.wait_ge(S("shift_stored"), 32)
            for m in range(DT):
                ins = dve.tensor_tensor_scan(cum[:, m, :], K("chunk"), sig[:, m, :], 0.0, ALU.mult, ALU.add)
            link(ins)
            link(TT(sig, cum, sig, ALU.subtract))
            dve.sem_inc(S("decay_sums"), 1)
            for m in range(DT):
                filled(first["kk_norm"] + m)
                free(TS_(b_[:, m, :], bank(first["kk_norm"] + m, T), 1e-24, None, ALU.max))
            dve.wait_ge(S("kk_root"), 1)
            link(dve.reciprocal(b_, b_))
            link(TT(kk, kk, b_, ALU.mult))
            link(TT(b_, kk, aa, ALU.mult))
            dve.sem_inc(S("a_used"), 1)
            for m in range(DT):
                filled(first["bonus"] + m)
                free(TT(bonus[:, m, :], bank(first["bonus"] + m, T), Vf[:, m, :], ALU.mult))
            dve.wait_ge(S("decays"), 3)
            Em, Ep = A_(7), A_(6)
            TT(Rf, Rf, Ef, ALU.mult)
            TT(Kf, Kf, Em, ALU.mult)
            TT(Bf, b_, Em, ALU.mult)
            link(STT(Af, kk, -1.0, Ep, ALU.mult, ALU.mult))
            dve.sem_inc(S("scan_in"), 1)
            for b in range(BS):
                filled(first["state_in"] + b)
                free(CP(S0[:, b, :, :], bank(first["state_in"] + b).rearrange("p (m i) -> p m i", m=HP)))

            def quad(t):
                return bank(t).rearrange("p (q c) -> p q c", q=4)

            def over(x, n=4):
                return x.unsqueeze(1).to_broadcast([P, n, x.shape[1]])

            def masked(name, dst, mask, hf):
                t = first[name] + hf
                filled(t)
                free(TT(dst[:, 4 * hf:4 * hf + 4, :], quad(t), over(K(mask)), ALU.mult))

            for c in range(CHUNKS):
                sample = c == CHUNKS - 1
                kind = "s" if sample else "p"
                for hf in range(2):
                    masked(f"LT{c}", LT_bd, "strict_" + kind, hf)
                dve.wait_ge(dve_freed, freed["d"][first[f"LT{c}"] + 2])
                for hf in range(2):
                    hs = slice(4 * hf, 4 * hf + 4)
                    link(TT(DT_bd[:, hs, :], LT_bd[:, hs, :], over(K("first_" + kind)), ALU.mult))
                    TT(DT_bd[:, hs, :], DT_bd[:, hs, :], over(ident), ALU.add).then_inc(S("DT_ready"), 1)
                for hf in range(2):
                    masked(f"KA{c}", KA_bd, "strict_" + kind, hf)
                for hf in range(2):
                    masked(f"RG{c}", RG_bd, "upto_" + kind, hf)
                for hf in range(2):
                    filled(first[f"D{c}"] + hf)
                    free(CP(D_bd[:, 4 * hf:4 * hf + 4, :], quad(first[f"D{c}"] + hf)))
                dve.wait_ge(dve_freed, freed["d"][first[f"D{c}"] + 2])
                dve.wait_ge(S("DT_ready"), 2 * c + 2)
                lvs = levels(c)
                for lv in lvs:
                    for nm, dst in (("DD", D_bd), ("DDT", DT_bd)):
                        if nm == "DD" and lv == lvs[-1]:
                            continue
                        for hf in range(2):
                            t = first[f"{nm}{c}_{lv}"] + hf
                            filled(t)
                            hs = slice(4 * hf, 4 * hf + 4)
                            free(TT(dst[:, hs, :], quad(t), dst[:, hs, :], ALU.add))
                    dve.wait_ge(dve_freed, freed["d"][first[f"DDT{c}_{lv}"] + 2])
                if sample:
                    for hf in range(2):
                        t = first["own_state"] + hf
                        filled(t)
                        hs = slice(4 * hf, 4 * hf + 4)
                        xt0 = quad(t)[:, :, 0:C].unsqueeze(2).to_broadcast([P, 4, 2, C])
                        out = XT_bd[:, hs, :].rearrange("p m (e c) -> p m e c", e=2)
                        mk = pair.rearrange("p (e c) -> p e c", e=2).unsqueeze(1).to_broadcast([P, 4, 2, C])
                        link(TT(out, xt0, mk, ALU.mult))
                        free(CP(Y0[:, hs, :], quad(t)[:, :, C:2 * C]))
                for hf in range(2):
                    t = first[f"Y{c}"] + hf
                    filled(t)
                    hs = slice(4 * hf, 4 * hf + 4)
                    dst = Yf[:, hs, c * C:(c + 1) * C]
                    if sample:
                        dve.wait_ge(dve_freed, freed["d"][first["own_state"] + 2])
                        free(TT(dst, quad(t)[:, :, 0:C], Y0[:, hs, :], ALU.add))
                    else:
                        free(CP(dst, quad(t)[:, :, 0:C]))
                if not sample:
                    for hf in range(2):
                        t = first[f"S{c}"] + hf
                        filled(t)
                        hs = slice(4 * hf, 4 * hf + 4)
                        wc = Ef[:, hs, (c + 1) * C - 1:(c + 1) * C].to_broadcast([P, 4, P])
                        if c == 0:
                            free(TT(S_bd[:, hs, :], quad(t), wc, ALU.mult))
                        else:
                            link(TT(S_bd[:, hs, :], quad(t), S_bd[:, hs, :], ALU.add))
                            free(TT(S_bd[:, hs, :], S_bd[:, hs, :], wc, ALU.mult))
                    dve.wait_ge(dve_freed, freed["d"][first[f"S{c}"] + 2])
                    if c == CHUNKS - 2:
                        for hf in range(2):
                            t = first["wkv_prompt"] + hf
                            filled(t)
                            free(CP(S_bd[:, 4 * hf:4 * hf + 4, :], quad(t)))
            for p in range(HP):
                t = first[f"SS{p}"]
                filled(t)
                sf = SF[:, p % 2, :, :]
                if p >= 2:
                    filled(first[f"ST{p - 2}"] + 1)
                wc = Ef[:, p, TP + QS - 1:T:QS].unsqueeze(2).to_broadcast([P, BS, C])
                link(TT(sf, bank(t).rearrange("p (b i) -> p b i", b=BS), S0[:, :, p, :], ALU.add))
                free(TT(sf, sf, wc, ALU.mult))
            dve.sem_inc(S("y_ready"), DT)
            for m in range(DT):
                t = first["mean"] + m
                filled(t)
                free(STT(Yf[:, m, :], bank(t, T), -1.0 / HD, Yf[:, m, :], ALU.mult, ALU.add))
            for m in range(DT):
                dve.wait_ge(act_freed, freed["a"][first["var"] + m + 1])
                link(dve.reciprocal(A_(1)[:, m, :], A_(1)[:, m, :]))
                link(TT(Yf[:, m, :], Yf[:, m, :], A_(1)[:, m, :], ALU.mult))
                link(TS_(Yf[:, m, :], Yf[:, m, :], prm("rw_lnx_w", m), prm("rw_lnx_b", m), ALU.mult, ALU.add))
                link(TT(Yf[:, m, :], Yf[:, m, :], bonus[:, m, :], ALU.add))
                TT(Yf[:, m, :], Yf[:, m, :], gf[:, m, :], ALU.mult).then_inc(S("wo_in"), 1)

            def residual(name):
                for m in range(DT):
                    filled(first[name] + m)
                    free(TT(h[:, m, :], bank(first[name] + m, T), h[:, m, :], ALU.add))
                dve.wait_ge(dve_freed, freed["d"][first[name] + DT])

            residual("wo")
            ffn(1)
            dve.wait_ge(dve_freed, freed["d"][first["down1"] + DT])

            norm("kv", "kv_norm", 0)
            copy_out("kk", kT)
            copy_out("vv", A_(9))
            for j in range(2):
                r = row_of["head_norms"] + j - P
                TS_(hn_scale[:, j:j + 1], par[:, 1, r:r + 1], HD ** -0.5 if j else 1.0, None, ALU.mult)
            t = first["logf"]
            filled(t)
            x, e, z, z2 = lw
            w = root[0:H, :]
            free(TS_(x, bank(t, T, H), b_f[0:H, :], None, ALU.add))
            dve.wait_ge(dve_freed, freed["d"][t + 1])
            link(TS_(e, x, -1.0, None, ALU.mult))
            link(TT(e, e, x, ALU.min))
            dve.sem_inc(S("logf_arg"), 1)
            for m in range(DT):
                dve.wait_ge(act_freed, freed["a"][first["k_norm"] + m + 1])
            link(dve.reciprocal(A_(4), A_(4)))
            STT(kT, kT, hn_scale[:, 0:1], A_(4), ALU.mult, ALU.mult).then_inc(S("k_ready"), 1)
            dve.wait_ge(S("logf_exp"), 1)
            link(TS_(z, e, 2.0, None, ALU.add))
            link(dve.reciprocal(z, z))
            link(TT(z, z, e, ALU.mult))
            link(TT(z2, z, z, ALU.mult))
            link(TS_(e, z2, 1.0 / 19, None, ALU.mult))
            for n in range(8, 0, -1):
                link(STT(e, e, 1.0 / (2 * n + 1), z2, ALU.add, ALU.mult))
            link(STT(z, e, 1.0, z, ALU.add, ALU.mult))
            link(TS_(x, x, 0.0, None, ALU.min))
            link(STT(LF, z, -2.0, x, ALU.mult, ALU.add))
            link(dve.tensor_tensor_scan(FT_, K("seqscan")[0:H, :], LF, 0.0, ALU.mult, ALU.add))
            dve.sem_inc(S("logf_ready"), 2)
            t = first["logf_tok"]
            filled(t)
            both = bank(t, 6 * H).rearrange("p (e g h) -> p e g h", e=2, g=3)
            CP(lf_tok[:, 0:2, :], both[:, 0, 0:2, :])
            CP(F_tok[:, 0:2, :], both[:, 1, 0:2, :])
            CP(lf_tok[0:TS, 2, :], both[0:TS, 0, 2, :])
            free(CP(F_tok[0:TS, 2, :], both[0:TS, 1, 2, :]))
            dve.wait_ge(dve_freed, freed["d"][t + 1])
            dve.sem_inc(S("logf_tok_ready"), 1)
            dve.wait_ge(S("wkv_prompt_out"), 32)
            for name, dst in (("k_tok", k_tok), ("v_tok", v_tok)):
                for g, n in ((0, P), (1, P), (2, TS)):
                    for j in range(2):
                        t = first[name] + 2 * g + j
                        filled(t)
                        free(CP(dst[0:n, g, j * 512:(j + 1) * 512], bank(t, 512, n)))
            dve.wait_ge(dve_freed, freed["d"][first["v_tok"] + 6])
            ffn(2)
            dve.wait_ge(dve_freed, freed["d"][first["down2"] + DT])

            norm("mix1", "mix_norm", 1)
            dve.wait_ge(S("k_stored"), 48)
            copy_out("q", q_f)
            for m in range(DT):
                dve.wait_ge(act_freed, freed["a"][first["q_norm"] + m + 1])
            link(dve.reciprocal(A_(7), A_(7)))
            link(STT(q_f, q_f, hn_scale[:, 1:2], A_(7), ALU.mult, ALU.mult))
            dve.sem_inc(S("q_ready"), 1)
            t = first["fq_col"]
            filled(t)
            free(CP(F_row, bank(t, TS)))
            dve.wait_ge(dve_freed, freed["d"][t + 1])
            fq = tmp_fq.rearrange("p (b q) -> p b q", b=BS)
            link(TT(fq, F_row.rearrange("p (b q) -> p b q", b=BS),
                    K("qpick").unsqueeze(1).to_broadcast([P, BS, QS]), ALU.mult))
            link(dve.tensor_reduce(fq_all, fq, AX.X, ALU.add))
            for j in range(2):
                filled(first["fk_past"] + j)
                free(CP(nfk.rearrange("p b j h -> p (b j h)")[:, j * 512:(j + 1) * 512],
                        bank(first["fk_past"] + j)))
            tot = [s_pr.rearrange("p j c -> p (j c)")[:, 0:512].rearrange("p (b j h) -> p b j h", b=4, j=PAGES),
                   qp_bd.rearrange("p j e t -> p (j e t)")[:, 0:512].rearrange("p (b j h) -> p b j h", b=4, j=PAGES)]
            for hb in range(2):
                t = first["fk_past"] + 2 + hb
                filled(t)
                free(CP(tot[hb], bank(t).rearrange("p (b j h) -> p b j h", b=4, j=PAGES)))
            dve.wait_ge(dve_freed, freed["d"][first["fk_past"] + 4])
            for hb in range(2):
                bs = slice(4 * hb, 4 * hb + 4)
                for j in range(PAGES - 2, -1, -1):
                    if j < PAGES - 2:
                        link(TT(tot[hb][:, :, j + 1, :], tot[hb][:, :, j + 1, :], tot[hb][:, :, j + 2, :], ALU.add))
                    link(TT(nfk[:, bs, j, :], nfk[:, bs, j, :], tot[hb][:, :, j + 1, :], ALU.add))
            for dst, src in ((slice(0, P), slice(0, P)), (slice(P, 3 * P), slice(0, 2 * P))):
                ins = TS_(nF_dup[:, dst], FT_[:, src], -1.0, None, ALU.mult)
            link(ins)
            dve.sem_inc(S("nF_ready"), 1)
            for hd in range(H):
                t = first["fb"] + hd
                filled(t)
                free(TT(fb[:, hd, :], bank(t, 384), K("causal"), ALU.add))
            dve.wait_ge(dve_freed, freed["d"][first["fb"] + H])
            dve.sem_inc(S("page_space"), 1)

            def queries_of(p):
                if p >= 2:
                    filled(first["fox"] + fox_tile(2 * p - 3, 0))
                for e_ in range(2):
                    ins = TS_(qp_bd[:, p % 2, e_, :], q_f[:, p, 0:TP], pair[:, e_ * C:e_ * C + 1], None, ALU.mult)
                link(ins)
                dve.sem_inc(S("qp_ready"), 1)

            queries_of(0)
            for kind, hd in fox_order:
                t = first["fox"] + fox_tile(hd, kind)
                s, st = s_pr[:, hd % 2, :], fstat[:, hd % 2, :]
                if kind == 0:
                    if hd % 2 == 0 and hd // 2 + 1 < HP:
                        queries_of(hd // 2 + 1)
                    if hd >= 2:
                        filled(first["fox"] + fox_tile(hd - 2, 1))
                    filled(t)
                    TT(s, bank(t, 384), fb[:, hd, :], ALU.add).then_inc(dve_freed, 1)
                    dve.wait_ge(dve_freed, freed["d"][t + 1])
                    dve.tensor_reduce(st[:, 0:1], s[:, 0:P], AX.X, ALU.max)
                    link(dve.tensor_reduce(st[:, 1:2], s[:, P:3 * P], AX.X, ALU.max))
                    link(TT(st[:, 2:4], st[:, 0:2], F_tok[:, 0:2, hd], ALU.add))
                    link(TT(st[:, 4:6], F_tok[:, 0:2, hd], st[:, 2:4], ALU.subtract))
                    dve.sem_inc(S("s_ready"), 2)
                elif kind == 1:
                    filled(t)
                    free(CP(pT[:, hd % 2, :], bank(t, 384)))
                else:
                    filled(t)
                    e_ = hd % 2
                    free(CP(oT[e_ * HD:(e_ + 1) * HD, hd // 2, 0:TP], ps[e_ * HD:(e_ + 1) * HD, t % 8, 0:TP]))
                nxt = fox_order[fox_order.index((kind, hd)) + 1] if (kind, hd) != fox_order[-1] else (None, 0)
                if nxt[0] == 1:
                    h1 = nxt[1]
                    s, st = s_pr[:, h1 % 2, :], fstat[:, h1 % 2, :]
                    dve.wait_ge(S("e_ready"), 2 * h1 + 2)
                    link(dve.reciprocal(st[:, 8:10], st[:, 6:8]))
                    TS_(s[:, 0:P], s[:, 0:P], st[:, 8:9], None, ALU.mult).then_inc(S("p_ready"), 1)
                    TS_(s[:, P:3 * P], s[:, P:3 * P], st[:, 9:10], None, ALU.mult).then_inc(S("p_ready"), 1)
            dve.wait_ge(dve_freed, freed["d"][first["fox"] + 3 * H])

            link(dve.memset(mask_new.rearrange("p b k -> p (b k)"), NEG))
            for b in range(BS):
                ins = CP(mask_new[:, b, b * QS:(b + 1) * QS], K("new"))
            link(ins)
            link(TT(mask_new, mask_new, F_row.unsqueeze(1).to_broadcast([P, BS, TS]), ALU.subtract))
            link(dve.memset(q_cur, 0.0))
            base, PER = steps[0], 9
            n_link = [0]

            with dve.Fori(0, BS) as b:
                def lk(ins):
                    n_link[0] += 1
                    ins.then_inc(S("dve_step"), 1)
                    dve.wait_ge(S("dve_step"), b * PER + (base + n_link[0]))

                dve.wait_ge(S("s_done"), b + 1)
                for r in range(2):
                    for e_ in range(2):
                        off = 48 * r + QS * e_
                        TS_(q_cur.rearrange("p (g c) -> p g c", g=4)[:, :, off:off + QS],
                            q_f[:, r:HP:2, bass.ds(b * QS + TP, QS)], pair[:, e_ * C:e_ * C + 1], None, ALU.mult
                            ).then_inc(S("q_cur"), 1)
                for j in range(PAGES):
                    dve.wait_ge(S("k_page_free"), b * PAGES + (j + 5))
                    CP(k_feat[j // 2 % 2][:, 4:8, j % 2 * P:(j % 2 + 1) * P],
                       ps[:, 4 + j % 2 * 2, :].rearrange("p (m t) -> p m t", m=4)).then_inc(S("kT_dve"), 1)
                dve.wait_ge(S("s_done"), b + 2)
                lk(TT(s_new, ps[:, 2, 0:TS], mask_new[:, bass.ds(b, 1), :].rearrange("p b k -> p (b k)"), ALU.add))
                dve.tensor_reduce(sst[:, 0:1], ps[:, 0:2, :].rearrange("p g c -> p (g c)"), AX.X, ALU.max)
                lk(dve.tensor_reduce(sst[:, 1:2], s_new, AX.X, ALU.max))
                lk(TT(sst[:, 2:3], sst[:, 0:1], sst[:, 1:2], ALU.max))
                lk(TT(sst[:, 3:4], sst[:, 2:3], fq_all[:, bass.ds(b, 1)], ALU.add))
                TT(sst[:, 4:5], fq_all[:, bass.ds(b, 1)], sst[:, 3:4], ALU.subtract).then_inc(S("less_max"), 1)
                dve.wait_ge(S("p_turned"), b + 1)
                CP(p_T[:, 4:8, :], ps[:, 1, :].rearrange("p (g c) -> p g c", g=4)).then_inc(S("pT_dve"), 1)
                CP(p_T[0:TS, 8, :], ps[0:TS, 2, P:2 * P]).then_inc(S("pT_dve"), 1)
                lk(TT(sst[:, 8:9], sst[:, 6:7], sst[:, 7:8], ALU.add))
                lk(dve.reciprocal(sst[:, 9:10], sst[:, 8:9]))
                dve.wait_ge(S("v_pages_free"), b + 2)
                lk(STT(o_own, ps[:, 7, 0:256].rearrange("p (g d) -> p g d", g=4), sst[:, 9:10],
                       K("quarter").unsqueeze(2).to_broadcast([P, 4, HD]), ALU.mult, ALU.mult))
                for e_ in range(2):
                    dve.tensor_reduce(o_two[:, e_ * HD:(e_ + 1) * HD], o_own.rearrange("p g d -> p d g"), AX.X,
                                      ALU.add).then_inc(S("o_own"), 1)
                dve.wait_ge(S("o_turned"), b + 1)
                for e_ in range(2):
                    pr = slice(e_ * HD, (e_ + 1) * HD)
                    CP(oT[pr, :, bass.ds(b * QS + TP, QS)],
                       ps[pr, 7, 256:384].rearrange("p (m e q) -> p m e q", m=HP, e=2)[:, :, e_, :]
                       ).then_inc(S("fox_out"), 1)
                for _ in range(PER - n_link[0]):
                    dve.sem_inc(S("dve_step"), 1)
                assert n_link[0] <= PER
            steps[0] = base + PER * BS
            dve.wait_ge(S("fox_out"), 2 * BS)
            residual("fo")
            ffn(3)
            dve.wait_ge(dve_freed, freed["d"][first["down3"] + DT])
            y_tok = [arena[:, 3 * TW + j * D:3 * TW + (j + 1) * D] for j in range(3)]
            for g, n in ((0, P), (1, P), (2, TS)):
                for j in range(2):
                    t = first["y"] + 2 * g + j
                    filled(t)
                    free(CP(y_tok[g][0:n, j * 512:(j + 1) * 512], bank(t, 512, n)))

        @block.gpsimd
        def _(pool):
            pool.wait_ge(dve_freed, freed["d"][first["shift_out"] + 2])
            rows_sh = A_(9)[0:BS + 1, :, :].rearrange("p m t -> p (m t)")[:, 0:D]
            pool.dma_start(O["shift_prompt"].rearrange("n b d -> (n b) d"), rows_sh[0:1, :]).then_inc(S("shift_stored"), 16)
            pool.dma_start(O["shift_sample"].rearrange("n b d -> (n b) d"), rows_sh[1:BS + 1, :]).then_inc(S("shift_stored"), 16)
            pool.wait_ge(S("scan_in"), 1)
            for b in range(BS):
                if b >= 2:
                    pool.wait_ge(tile_done, first["state_in"] + b - 1)
                pool.dma_start(state_in[b % 2][0:HD, :].rearrange("p (g j) -> p g j", g=H),
                               A["state_wkv"][0, b].rearrange("g i j -> i g j")).then_inc(S(f"state_in{b % 2}"), 16)

            def pairs(dst, src, hf, c):
                hs = slice(4 * hf, 4 * hf + 4)
                pool.tensor_tensor(dst[:, hs, :].rearrange("p m (e c) -> p m e c", e=2),
                                   src[:, hs, c * C:(c + 1) * C].unsqueeze(2).to_broadcast([P, 4, 2, C]),
                                   pair.rearrange("p (e c) -> p e c", e=2).unsqueeze(1).to_broadcast([P, 4, 2, C]),
                                   ALU.mult).then_inc(S("bd_ready"), 1)

            for c in range(CHUNKS):
                if c:
                    pool.wait_ge(tile_done, first[f"X{c - 1}"] + 2)
                for hf in range(2):
                    for dst, src in ((A_bd, Af), (B_bd, Bf), (K_bd, Kf), (V_bd, Vf)):
                        pairs(dst, src, hf, c)
                lvs = levels(c)
                for n_lv, lv in enumerate(lvs):
                    for hf in range(2):
                        hs = slice(4 * hf, 4 * hf + 4)
                        if lv == lvs[0]:
                            pool.wait_ge(tile_done, first[f"tok{c}"] + 4)
                            pool.wait_ge(dve_freed, freed["d"][first[f"LT{c}"] + 2])
                        else:
                            pool.wait_ge(tile_done, first[f"Z{c}_{lvs[n_lv - 1]}"] + hf + 1)
                        pool.tensor_tensor(join_bd[:, hs, :], LT_bd[:, hs, :],
                                           K(f"join{lv}").unsqueeze(1).to_broadcast([P, 4, P]), ALU.mult
                                           ).then_inc(S("join_ready"), 1)
                if c == CHUNKS - 2:
                    pool.wait_ge(dve_freed, freed["d"][first["wkv_prompt"] + 2])
                    for e in range(2):
                        pool.dma_start(
                            O["wkv_prompt"][0, 0].rearrange("(m e) i j -> e i m j", e=2)[e],
                            S_bd[e * HD:(e + 1) * HD, :, e * HD:(e + 1) * HD]).then_inc(S("wkv_prompt_out"), 16)
            pool.wait_ge(tile_done, first[f"DDT{CHUNKS - 1}_2"] + 2)
            for p in range(HP):
                if p >= 2:
                    n = p - 2
                    if n % 4 == 3:
                        pool.wait_ge(tile_done, first["own_state"] + n // 4 + 1)
                    else:
                        pool.wait_ge(S("S0_used"), n - n // 4 + 1)
                pool.tensor_tensor(
                    S0_bd[p % 2].rearrange("p m c -> p (m c)").rearrange("p (b e i) -> p b e i", b=BS, e=2),
                    S0[:, :, p, :].unsqueeze(2).to_broadcast([P, BS, 2, C]),
                    pair.rearrange("p (e c) -> p e c", e=2).unsqueeze(1).to_broadcast([P, BS, 2, C]),
                    ALU.mult).then_inc(S("S0_ready"), 1)
            c = CHUNKS - 1
            pool.wait_ge(act_freed, freed["a"][first[f"U{c}"] + 2])
            pool.wait_ge(tile_done, first[f"Y{c}"] + 2)
            pool.tensor_tensor(U_st, X_bd[:, :, 0:C], X_bd[:, :, C:2 * C], ALU.add).then_inc(S("st_ready"), 1)
            pool.tensor_tensor(V_st, V_tok[:, :, 0:C], V_tok[:, :, C:2 * C], ALU.add).then_inc(S("st_ready"), 1)
            pool.wait_ge(S("st_ready"), 2)

            def store_states(p):
                pool.wait_ge(act_freed, freed["a"][first[f"ST{p}"] + 2])
                for e in range(2):
                    pool.dma_start(O["wkv_sample"][0, :, 2 * p + e, :, :].rearrange("b i j -> i b j"),
                                   state_out[p % 2][0:HD, :].rearrange("p (b e j) -> p b e j", b=BS, e=2)[:, :, e, :]
                                   ).then_inc(S(f"state_out{p % 2}"), 16)

            for p in range(HP):
                if p >= 2:
                    pool.wait_ge(tile_done, first[f"SS{p - 2}"] + 1)
                for e, src in enumerate((U_st, V_st)):
                    pool.tensor_tensor(UV[p % 2][:, e, :, :], src[:, p, :].unsqueeze(1).to_broadcast([P, BS, C]),
                                       K("seq").unsqueeze(2).to_broadcast([P, BS, C]), ALU.mult
                                       ).then_inc(S("uv_ready"), 1)
                if p >= 1:
                    store_states(p - 1)
            store_states(HP - 1)
            pool.wait_ge(S("logf_tok_ready"), 1)
            pool.dma_start(O["logf_prompt"][0].rearrange("(g p) h -> p g h", p=P), lf_tok[:, 0:2, :]).then_inc(S("logf_stored"), 16)
            pool.dma_start(O["logf_sample"].rearrange("b t h -> (b t) h"), lf_tok[0:TS, 2, :]).then_inc(S("logf_stored"), 16)
            for name, src in (("k", k_tok), ("v", v_tok)):
                for g in range(3):
                    pool.wait_ge(dve_freed, freed["d"][first[name + "_tok"] + 2 * g + 2])
                    if g < 2:
                        dst = O[name + "_prompt"][0, g * P:(g + 1) * P].rearrange("t h d -> t (h d)")
                    else:
                        dst = O[name + "_sample"].rearrange("b t h d -> (b t) (h d)")
                    pool.dma_start(dst, src[0:P if g < 2 else TS, g, :]).then_inc(S(name + "_stored"), 16)
            pool.wait_ge(tile_done, first["down2"] + DT)
            pool.wait_ge(S("pt_in"), 16)
            with pool.Fori(0, BS) as b:
                for j in range(PAGES):
                    page = pool.value_load(pt_sb[0:1, bass.ds(b * PAGES + j, 1)], min_val=0,
                                           max_val=A["cache_k"].shape[0] - 1)
                    pool.dma_start(lfp[:, bass.ds(b, 1), j, :].rearrange("p b h -> p (b h)"),
                                   A["cache_logf"][bass.ds(page, 1)].rearrange("a t h -> (a t) h")
                                   ).then_inc(S("lfp_in"), 16)
            for g in range(3):
                pool.wait_ge(dve_freed, freed["d"][first["y"] + 2 * g + 2])
                dst = (O["y_prompt"][0, g * P:(g + 1) * P] if g < 2 else O["y_sample"].rearrange("b t d -> (b t) d"))
                pool.dma_start(dst, arena[0:P if g < 2 else TS, 3 * TW + g * D:3 * TW + (g + 1) * D]
                               ).then_inc(S("y_stored"), 16)
            pool.wait_ge(S("shift_stored"), 32)
            pool.wait_ge(S("wkv_prompt_out"), 32)
            pool.wait_ge(S("state_out0"), 16 * HP)
            pool.wait_ge(S("state_out1"), 16 * HP)
            pool.wait_ge(S("logf_stored"), 32)
            pool.wait_ge(S("k_stored"), 48)
            pool.wait_ge(S("v_stored"), 48)
            pool.wait_ge(S("y_stored"), 48)


_INS = ["x_prompt", "x_sample", "cache_k", "cache_v", "cache_logf", "state_wkv", "state_shift", "page_table",
        "ffn_norm", "ffn_w_in", "ffn_w_out", "mix_norm", "rw_mu", "rw_w_rkv", "rw_w0", "rw_w1", "rw_w2",
        "rw_a0", "rw_a1", "rw_a2", "rw_g1", "rw_g2", "rw_k_k", "rw_k_a", "rw_r_k", "rw_lnx_w", "rw_lnx_b",
        "rw_w_o", "kv_norm", "w_kv", "k_norm", "w_f", "b_f", "fox_w_q", "fox_q_norm", "fox_w_o"]
_OUTS = [("y_prompt", (1, TP, D)), ("y_sample", (BS, QS, D)), ("k_prompt", (1, TP, H, HD)),
         ("v_prompt", (1, TP, H, HD)), ("logf_prompt", (1, TP, H)), ("wkv_prompt", (1, 1, H, HD, HD)),
         ("shift_prompt", (1, 1, D)), ("k_sample", (BS, QS, H, HD)), ("v_sample", (BS, QS, H, HD)),
         ("logf_sample", (BS, QS, H)), ("wkv_sample", (1, BS, H, HD, HD)), ("shift_sample", (1, BS, D))]


def kernel(**inputs):
    import concourse.bacc as bacc
    from concourse.bass_utils import run_bass_kernel_spmd

    nc = bacc.Bacc("TRN2", target_bir_lowering=False, num_devices=1)
    arrays, A, O = {}, {}, {}
    given = {name: np.ascontiguousarray(inputs[name]) for name in _INS}
    given["const"] = const_arrays()[1]
    given["head_sel"] = head_selectors()
    for name, a in given.items():
        arrays["in_" + name] = a
        A[name] = nc.dram_tensor("in_" + name, a.shape, mybir.dt.from_np(a.dtype), kind="ExternalInput").ap()
    for name, shape in _OUTS:
        O[name] = nc.dram_tensor("out_" + name, shape, F32, kind="ExternalOutput").ap()
    build(nc, A, O)
    r = run_bass_kernel_spmd(nc, [arrays], core_ids=[0])
    return tuple(r.results[0]["out_" + name] for name, _ in _OUTS)
```

```python
from contextlib import ExitStack

import numpy as np

import concourse.bass as bass
from concourse import mybir

P = 128
D = 1024
DT = D // P
TP, BS, TS = 256, 8, 64
T = TP + TS
QS = TS // BS
H, HD = 16, 64
HP = H // 2
FF = 2816
FT = FF // P
PAST, PAGE = 1024, 128
PAGES = PAST // PAGE
C = 64
CHUNKS = T // C
RMS_EPS, LNX_EPS = 1e-6, 64e-5
SLAB = 2048
SLOTS = 4
NEG = -1e30
DECAY = float(np.exp(-0.5))

F32 = mybir.dt.float32
F32R = mybir.dt.float32r
I32 = mybir.dt.int32
ALU = mybir.AluOpType
ACT = mybir.ActivationFunctionType
AX = mybir.AxisListType

PARAMS = ["ffn_norm", "mix_norm", "rw_mu", "rw_w0", "rw_a0", "rw_k_k", "rw_k_a", "rw_r_k",
          "rw_lnx_w", "rw_lnx_b", "kv_norm"]
PARAM_ROWS = {"ffn_norm": 4, "mix_norm": 2, "rw_mu": 6}


def plan_tiles():
    first, owner = {}, []

    def add(name, n, who="d"):
        first[name] = len(owner)
        owner.extend(who * n if len(who) == 1 else who)

    def ffn(n):
        if n != 2:
            add(f"norm_ffn{n}", 1, "a")
        add(f"up{n}", 2 * FT)
        add(f"down{n}", DT)

    add("params", 2)
    add("shift_in", 1)
    add("x", DT)
    ffn(0)
    add("norm_mix0", 1, "a")
    add("shift_out", 2)
    for n in "rkv":
        add(n, DT)
    add("w1", 1, "a")
    add("w2", DT, "a")
    add("a1", 1)
    add("a2", DT, "a")
    add("g1", 1, "a")
    add("g2", DT)
    add("kk_norm", DT)
    add("bonus", DT)
    add("state_in", BS)
    for c in range(CHUNKS):
        last = c == CHUNKS - 1
        add(f"LT{c}", 2)
        add(f"KA{c}", 2)
        add(f"RG{c}", 2)
        add(f"tok{c}", 6, "a")
        add(f"D{c}", 2)
        for lv in levels(c):
            add(f"Z{c}_{lv}", 2, "a")
            if lv != levels(c)[-1]:
                add(f"DD{c}_{lv}", 2)
            add(f"DDT{c}_{lv}", 2)
        if last:
            add("own_state", 2)
        add(f"X{c}", 2, "a")
        add(f"U{c}", 2, "a")
        add(f"Y{c}", 2)
        if not last:
            add(f"S{c}", 2)
            if c == CHUNKS - 2:
                add("wkv_prompt", 2)
    for p in range(HP):
        add(f"SS{p}", 1)
        add(f"ST{p}", 2, "a")
    add("mean", DT)
    add("var", DT, "a")
    add("wo", DT)
    ffn(1)
    add("norm_kv", 1, "a")
    add("kk", DT)
    add("vv", DT)
    add("logf", 1)
    add("k_norm", DT, "a")
    add("logf_tok", 1)
    add("k_tok", 6)
    add("v_tok", 6)
    ffn(2)
    add("norm_mix1", 1, "a")
    add("q", DT)
    add("q_norm", DT, "a")
    add("fq_col", 1)
    add("fk_past", 4)
    add("fb", H)
    add("fox", 3 * H)
    add("fo", DT)
    ffn(3)
    add("y", 6)
    return first, owner


def plan_slabs():
    slabs, first_slab, low_rank, count = [], {}, {}, [0] * SLOTS

    def take(slot, pieces=1):
        count[slot] += 16 * pieces
        return count[slot]

    def dense(name, slots):
        first_slab[name] = len(slabs)
        for slot in slots:
            slabs.append((slot, DT, take(slot)))

    def ffn(n, slot):
        first_slab[f"up{n}"] = len(slabs)
        for j in range(FT + 12):
            slabs.append(((slot + j) % SLOTS, DT if j < FT or (j - FT) % 3 < 2 else FT - 2 * DT,
                          take((slot + j) % SLOTS)))
            if j == FT - 1:
                first_slab[f"down{n}"] = len(slabs)

    ffn(0, 0)
    for name in "rkv":
        dense(name, [2, 3, 0, 1])
    low_rank[1], low_rank[2], low_rank[3] = take(2, 3), take(3, 2), take(0)
    dense("wo", [2, 0, 1, 2])
    ffn(1, 0)
    for name in ("kk", "vv"):
        dense(name, [2, 3, 0, 1])
    ffn(2, 2)
    dense("q", [0, 1, 2, 3])
    dense("fo", [1, 2, 3, 0])
    ffn(3, 1)
    return slabs, first_slab, low_rank


def levels(c):
    return [1, 2, 3, 4, 5] if c < CHUNKS - 1 else [1, 2]


def const_arrays():
    i = np.arange(P)
    head, tok = i // C, i % C
    same = (head[:, None] == head[None, :])
    s, t = tok[:, None], tok[None, :]
    m = {}
    m["ident"] = np.eye(P)
    m["ones"] = np.ones((P, P))
    m["pair"] = same
    for kind, seq in (("p", True), ("s", s // QS == t // QS)):
        m["strict_" + kind] = same & (s < t) & seq
        incl = ((s <= t) & seq)[:, :C]
        m["upto_" + kind] = np.concatenate([incl, incl], 1)
        m["first_" + kind] = same & (s + 1 == t) & (t % 2 == 1) & seq
    for lv in range(1, 6):
        b = 2 ** lv
        m[f"join{lv}"] = same & (s // (2 * b) == t // (2 * b)) & (s // b % 2 == 0) & (t // b % 2 == 1)
    m["later"] = i[:, None] > i[None, :]
    m["seq"] = tok[:, None] // QS == np.arange(BS)[None, :]
    chunk_mask = np.ones((P, T))
    chunk_mask[:, 0:TP:C] = 0
    chunk_mask[:, TP::QS] = 0
    m["chunk"] = chunk_mask
    seq_mask = np.ones((P, T))
    seq_mask[:, 0] = 0
    seq_mask[:, TP::QS] = 0
    m["seqscan"] = seq_mask
    causal = np.where(i[:, None] >= i[None, :], 0, NEG)
    m["causal"] = np.concatenate([causal, np.zeros((P, P)), causal], 1)
    m["new"] = np.where(np.arange(QS)[None, :] <= i[:, None] % QS, 0, NEG)
    m["quarter"] = i[:, None] // QS % 4 == np.arange(4)[None, :]
    m["selcol"] = (i[:, None] == i[None, :] // QS)
    m["qpick"] = (i[:, None] % QS == np.arange(QS)[None, :])
    at, out = {}, []
    n = 0
    for name, a in m.items():
        at[name] = (n, n + a.shape[1])
        n += a.shape[1]
        out.append(np.asarray(a, np.float32))
    return at, np.concatenate(out, 1)


def head_selectors():
    return np.repeat(np.eye(H, dtype=np.float32), P, 1)


def build(nc, A, O):
    first, owner = plan_tiles()
    at, const_np = const_arrays()
    N_CONST = const_np.shape[1]
    freed = {"d": [0], "a": [0]}
    for w in owner:
        for e in "da":
            freed[e].append(freed[e][-1] + (w == e))
    row_of, rows = {}, 0
    for name in PARAMS:
        row_of[name] = rows
        rows += PARAM_ROWS.get(name, 1) * DT
    row_of["head_norms"] = rows
    rows += 2
    slabs, first_slab, low_rank = plan_slabs()
    norms = ["ffn0", "mix0", "ffn1", "kv", "mix1", "ffn3"]
    normed = ["ffn0", "mix0", "ffn1", "kv", "ffn2", "mix1", "ffn3"]
    split_norms = ["ffn0", "ffn1", "kv", "ffn2", "mix1", "ffn3"]

    with ExitStack() as ctx:
        def sb(name, shape, dt=F32):
            return ctx.enter_context(nc.sbuf_tensor(name, shape, dt))

        sems = {}

        def S(name):
            if name not in sems:
                sems[name] = ctx.enter_context(nc.semaphore(name))
            return sems[name]

        TW = DT * T
        h_f = sb("h", [P, TW])
        with nc.sbuf_tensor("xn", [P, TW], F32) as xn_f, nc.sbuf_tensor("ring", [P, 3, 2 * SLAB], F32) as ring, \
                nc.sbuf_tensor("arena", [P, 11 * TW], F32) as arena:
            pass
        xn_r, ring_r, arena_r = sb("xn_r", [P, TW], F32R), sb("ring_r", [P, 3, 2 * SLAB], F32R), \
            sb("arena_r", [P, 11 * TW], F32R)
        extra = sb("extra", [P, 2048])
        const = sb("const", [P, N_CONST])
        par = sb("par", [P, 2, P])
        small = sb("small", [P, 800])
        root = sb("root", [P, T])
        rs = sb("rs", [P, T])
        pt_sb = sb("pt_sb", [1, BS * PAGES], I32)
        ps = ctx.enter_context(nc.psum_tensor("ps", [P, 8, 512], F32))

        def feat(x):
            return x.rearrange("p (m t) -> p m t", m=DT)

        h, xn = feat(h_f[:, :]), feat(xn_f[:, :])

        def A_(n):
            return feat(arena[:, n * TW:(n + 1) * TW])

        def AR_(n):
            return feat(arena_r[:, n * TW:(n + 1) * TW])

        def K(name):
            return const[:, at[name][0]:at[name][1]]

        def prm(name, m, row=0):
            r = row_of[name] + row * DT + m
            return par[:, r // P, r % P:r % P + 1]

        ident, ones, pair = K("ident"), K("ones"), K("pair")
        used = [0]

        def sm(n):
            used[0] += n
            assert used[0] <= 800, used
            return small[:, used[0] - n:used[0]]

        eps, eps_ln, b_f = sm(1), sm(1), sm(1)
        omka = sm(DT)
        w_f = sm(DT * H).rearrange("p (k n) -> p k n", k=DT)
        shT = sm(DT * BS).rearrange("p (m b) -> p m b", m=DT)
        shc = sm(DT * (BS + 1)).rearrange("p (m b) -> p m b", m=DT)
        lf_tok = sm(3 * H).rearrange("p (g h) -> p g h", g=3)
        F_tok = sm(3 * H).rearrange("p (g h) -> p g h", g=3)
        F_row = sm(TS)
        fq_all, tmp_fq = sm(BS), sm(TS)
        hn_scale = sm(2)

        o_kT = 2 * FT * T
        o_v, o_xh = o_kT + TW, o_kT + TW + 3 * D
        o_sg, o_slot = o_xh + TW, o_xh + TW + 4 * T
        assert o_slot + 2 * SLAB <= 11 * TW
        hid = arena[:, 0:FT * T].rearrange("p (f t) -> p f t", f=FT)
        hid_lo = arena_r[:, 0:FT * T].rearrange("p (f t) -> p f t", f=FT)
        hid_hi = arena_r[:, FT * T:2 * FT * T].rearrange("p (f t) -> p f t", f=FT)
        sg = arena[:, o_sg:o_sg + 4 * T].rearrange("p (g t) -> p g t", g=4)
        sq = feat(arena[:, o_xh:o_xh + TW])
        xn_hi, xn_lo = feat(arena_r[:, o_xh:o_xh + TW]), feat(xn_r[:, :])

        tile_done = S("tile_done")
        dve_freed = S("dve_freed_bank")
        act_freed = S("act_freed_bank")

        def bank(t, n=512, rows_=P):
            return ps[0:rows_, t % 8, 0:n]

        w_in = A["ffn_w_in"].rearrange("l s k m -> (l s) k m")
        w_out = A["ffn_w_out"].rearrange("l s k m -> (l s) k m")

        def cols(w, k0, k1, c0, n):
            return w[k0 * P:k1 * P, c0:c0 + n].rearrange("(k p) m -> p k m", p=P)

        def slot_(slot, r=False):
            if slot < 3:
                return (ring_r if r else ring)[:, slot, :]
            return (arena_r if r else arena)[:, o_slot:o_slot + 2 * SLAB]

        def slab(slot, k, n=256):
            return slot_(slot)[:, 0:k * n].rearrange("p (k m) -> p k m", k=k)

        def part(s, hi):
            slot, k, _ = slabs[s]
            return slot_(slot, True)[:, hi * SLAB:hi * SLAB + k * 256].rearrange("p (k m) -> p k m", k=k)

        def raw(s):
            return slab(slabs[s][0], slabs[s][1])

        dense = {
            "r": A["rw_w_rkv"][0, 0], "k": A["rw_w_rkv"][0, 1], "v": A["rw_w_rkv"][0, 2],
            "wo": A["rw_w_o"][0], "kk": A["w_kv"][:, 0:D], "vv": A["w_kv"][:, D:2 * D],
            "q": A["fox_w_q"][0], "fo": A["fox_w_o"][0],
        }
        LORA1, LORA2, LORA3 = 2, 3, 0
        lo1 = slab(LORA1, DT)
        lora2 = slot_(LORA2)

        def buf(j):
            if j < 2:
                x = xn_f[:, j * D:(j + 1) * D]
            elif j < 10:
                x = ring[:, (j - 2) // 4, (j - 2) % 4 * D:(j - 2) % 4 * D + D]
            elif j < 12:
                x = extra[:, (j - 10) * D:(j - 9) * D]
            else:
                x = arena[:, 6 * TW + 4096:6 * TW + 4096 + D]
            return x.rearrange("p (m c) -> p m c", m=HP)

        (A_bd, B_bd, K_bd, V_bd, LT_bd, KA_bd, RG_bd, V_tok, B_tok, K_tok, DT_bd, X_bd, S_bd) = (
            buf(j) for j in range(13))
        join_bd, Z_bd, D_bd = B_bd, K_bd, V_bd
        S0 = arena[:, 6 * TW:6 * TW + 4096].rearrange("p (b m i) -> p b m i", b=BS, m=HP)
        state_in = [x.rearrange("p m c -> p (m c)") for x in (LT_bd, KA_bd)]
        S0_bd = [B_bd, K_bd]
        XT_bd, Y0 = V_bd, LT_bd.rearrange("p m c -> p (m c)")[:, 0:512].rearrange("p (m c) -> p m c", m=HP)
        U_st = A_bd.rearrange("p m c -> p (m c)")[:, 0:512].rearrange("p (m c) -> p m c", m=HP)
        V_st = A_bd.rearrange("p m c -> p (m c)")[:, 512:1024].rearrange("p (m c) -> p m c", m=HP)
        UV = [x.rearrange("p m c -> p (m c)").rearrange("p (e b i) -> p e b i", e=2, b=BS) for x in (B_bd, K_bd)]
        SF = V_bd.rearrange("p m c -> p (m c)").rearrange("p (e b i) -> p e b i", e=2, b=BS)
        state_out = [x.rearrange("p m c -> p (m c)") for x in (LT_bd, KA_bd)]
        Yf = A_(9)
        Af, Bf, bonus, Rf, Kf, Vf, gf, Ef = A_(0), A_(1), A_(2), A_(3), A_(4), A_(5), A_(8), A_(10)

        kT = feat(arena[:, o_kT:o_kT + TW])
        v_tok = arena[:, o_v:o_v + 3 * D].rearrange("p (g d) -> p g d", g=3)
        k_tok = arena[:, o_kT - 3 * D:o_kT].rearrange("p (g d) -> p g d", g=3)
        o_q = PAGES * D
        q_f = feat(arena[:, o_q:o_q + TW])
        q_sq = feat(arena[:, o_q + TW:o_q + 2 * TW])
        oT, oT_lo, oT_hi = xn, xn_lo, feat(arena_r[:, o_q + TW:o_q + 2 * TW])
        fb = arena[:, o_xh:o_xh + H * 384].rearrange("p (h c) -> p h c", h=H)
        head_sel = ring[0:H, 0, 0:H * P].rearrange("p (h c) -> p h c", h=H)
        o10 = o_xh + H * 384
        assert o_q + 2 * TW + 3 * 256 <= o_kT and o10 + 1792 <= 11 * TW
        qp_bd = arena[:, o10:o10 + 1024].rearrange("p (j e t) -> p j e t", j=2, e=2)
        s_pr = arena[:, o10 + 1024:o10 + 1792].rearrange("p (j c) -> p j c", j=2)
        o_pT = o_q + 2 * TW
        pT = arena[:, o_pT:o_pT + 768].rearrange("p (j c) -> p j c", j=2)
        fstat = sb("fstat", [P, 2, 10])

        def v_page(j):
            return arena[:, j * D:(j + 1) * D]

        def k_page(j):
            return ring[:, 0, j * D:j * D + D]

        o7 = o_xh
        k_feat = [arena[:, o7 + j * 2048:o7 + (j + 1) * 2048].rearrange("p (m t) -> p m t", m=HP) for j in range(2)]
        p_row = arena[:, o7 + 4096:o7 + 5184]
        p_T = arena[:, o7 + 5184:o7 + 6336].rearrange("p (g c) -> p g c", g=9)
        nfk_rep = arena[:, o7 + 6336:o7 + 7360]
        mask_new = arena[:, o7 + 7360:o7 + 7872].rearrange("p (b k) -> p b k", b=BS)
        o_two = arena[:, o7 + 7872:o7 + 8000]
        o_own = arena[:, o7 + 8000:o7 + 8256].rearrange("p (g d) -> p g d", g=4)
        s_new = arena[:, o_pT:o_pT + 64]
        q_cur = arena[:, o_pT + 64:o_pT + 320]
        sst = arena[:, o_pT + 320:o_pT + 336]
        nfk = extra[:, 640:1664].rearrange("p (b j h) -> p b j h", b=BS, j=PAGES)
        lfp = arena[:, 0:1024].rearrange("p (b j h) -> p b j h", b=BS, j=PAGES)    
        FT_, LF = extra[0:H, 0:T], extra[0:H, T:2 * T]
        lw = [extra[0:H, (2 + j) * T:(3 + j) * T] for j in range(4)]
        nF_dup = extra[0:H, 1664:2048]
        N_PARAM_DMAS = sum(2 if row_of[n] < P < row_of[n] + PARAM_ROWS.get(n, 1) * DT else 1 for n in PARAMS) + 4
        join_count, n_join = {}, 0
        for c in range(CHUNKS):
            for lv in levels(c):
                join_count[c, lv] = n_join
                n_join += 2
        fox_order = [(0, 0)]
        for hd in range(H):
            fox_order += ([(0, hd + 1)] if hd + 1 < H else []) + ([(2, hd - 1)] if hd else []) + [(1, hd)]
        fox_order.append((2, H - 1))

        def fox_tile(hd, kind):
            return fox_order.index((kind, hd))

        block = ctx.enter_context(nc.Block())

        @block.sync
        def _(sp):
            free_at = [None] * SLOTS

            def load(slot, pieces, frees):
                if free_at[slot]:
                    sp.wait_ge(*free_at[slot])
                for dst, src in pieces:
                    sp.dma_start(dst, src).then_inc(S(f"slab{slot}"), 16)
                free_at[slot] = frees

            def free_after(s, sem, value):
                free_at[slabs[s][0]] = (sem, value)

            def load_slab(s, src):
                load(slabs[s][0], [(raw(s), src)], None)

            def load_dense(name):
                for q in range(4):
                    s = first_slab[name] + q
                    load_slab(s, cols(dense[name], 0, DT, 256 * q, 256))
                    free_after(s, tile_done, first[name] + 2 * q + 2)

            def load_ffn(n):
                base, s0 = first[f"up{n}"], first_slab[f"up{n}"]
                w = w_in[n]
                for j in range(4):
                    load_slab(s0 + j, cols(w, 0, DT, j // 2 * 256 + j % 2 * FF, 256))
                with sp.Fori(1, 5) as i:
                    for j in range(4):
                        sp.wait_ge(tile_done, i * 8 + (base - 8 + 2 * j + 2))
                        src = w[:, bass.ds(i * 512 + (j // 2 * 256 + j % 2 * FF), 256)]
                        slot = slabs[s0 + j][0]
                        sp.dma_start(slab(slot, DT), src.rearrange("(k p) m -> p k m", p=P)
                                     ).then_inc(S(f"slab{slot}"), 16)
                for j in range(4):
                    free_after(s0 + j, tile_done, base + 32 + 2 * j + 2)
                for j in range(2):
                    load_slab(s0 + 20 + j, cols(w, 0, DT, 2560 + j * FF, 256))
                    free_after(s0 + 20 + j, tile_done, base + 40 + 2 * j + 2)
                for mp in range(4):
                    for s3 in range(3):
                        s = first_slab[f"down{n}"] + 3 * mp + s3
                        k0, k1 = 8 * s3, min(8 * s3 + 8, FT)
                        load_slab(s, cols(w_out[n], k0, k1, 256 * mp, 256))
                        if s3 < 2:
                            free_after(s, S("down_slab_used"), 8 * n + 2 * mp + s3 + 1)
                        else:
                            free_after(s, tile_done, first[f"down{n}"] + 2 * mp + 2)

            xt = arena[:, 3 * TW:3 * TW + 3 * D].rearrange("p (g d) -> p g d", g=3)
            sp.dma_start(const[:, :], A["const"]).then_inc(S("const_in"), 16)
            prow = arena[:, 5 * TW:5 * TW + 2 * P].rearrange("p (g d) -> p g d", g=2)
            for name in PARAMS:
                n = PARAM_ROWS.get(name, 1) * DT
                flat = A[name]
                dims = "abc"[:len(flat.shape)]
                if len(dims) > 1:
                    flat = flat.rearrange(" ".join(dims) + " -> (" + " ".join(dims) + ")")
                flat = flat.rearrange("(r c) -> r c", c=P)
                r0 = row_of[name]
                for a, b in ((r0, min(r0 + n, P)), (max(r0, P), r0 + n)):
                    if a < b:
                        sp.dma_start(prow[a % P:a % P + b - a, a // P, :], flat[a - r0:b - r0, :]
                                     ).then_inc(S("param_in"), 16)
            for j, src in enumerate((A["k_norm"], A["fox_q_norm"][0])):
                for e in range(2):
                    r = row_of["head_norms"] + j
                    sp.dma_start(prow[r % P:r % P + 1, 1, e * HD:(e + 1) * HD],
                                 src.rearrange("(a d) -> a d", a=1)).then_inc(S("param_in"), 16)
            sp.dma_start(arena[0:BS, 6 * TW:6 * TW + D], A["state_shift"][0]).then_inc(S("shift_in"), 16)
            for g in range(2):
                sp.dma_start(xt[:, g, :], A["x_prompt"][0, g * P:(g + 1) * P, :]).then_inc(S("x_in"), 16)
            sp.dma_start(xt[0:TS, 2, :], A["x_sample"].rearrange("b t d -> (b t) d")).then_inc(S("x_in"), 16)
            sp.dma_start(w_f, A["w_f"].rearrange("(k p) n -> p k n", p=P)).then_inc(S("wf_in"), 16)
            sp.dma_start(b_f[0:H, :], A["b_f"].rearrange("(h a) -> h a", a=1)).then_inc(S("wf_in"), 16)
            sp.dma_start(pt_sb[:, :], A["page_table"].rearrange("(a b) n -> a (b n)", a=1)).then_inc(S("pt_in"), 16)

            load_ffn(0)
            for name in "rkv":
                load_dense(name)
            load(LORA1, [(lo1[:, :, 0:64], A["rw_w1"][0].rearrange("(k p) m -> p k m", p=P)),
                         (lo1[:, :, 64:128], A["rw_a1"][0].rearrange("(k p) m -> p k m", p=P)),
                         (lo1[:, :, 128:256], A["rw_g1"][0].rearrange("(k p) m -> p k m", p=P))],
                 (tile_done, first["g1"] + 1))
            load(LORA2, [(lora2[0:64, 0:D], A["rw_w2"][0]),
                         (lora2[0:64, D:2 * D], A["rw_a2"][0])], None)
            load(LORA3, [(slot_(LORA3)[:, 0:D], A["rw_g2"][0])], None)
            load_slab(first_slab["wo"], cols(dense["wo"], 0, DT, 0, 256))
            free_at[0] = free_at[1] = (tile_done, first[f"ST{HP - 1}"] + 2)
            free_at[2] = (tile_done, first["wo"] + 2)
            free_at[3] = (tile_done, first["wo"] + DT)
            for j in range(2):
                sp.wait_ge(S(f"state_out{j}"), 16 * HP)
            for q in range(1, 4):
                s = first_slab["wo"] + q
                load_slab(s, cols(dense["wo"], 0, DT, 256 * q, 256))
                free_after(s, tile_done, first["wo"] + 2 * q + 2)
            load_ffn(1)
            load_dense("kk")
            load_dense("vv")
            load_ffn(2)
            load_dense("q")
            sp.wait_ge(*free_at[0])
            sp.dma_start(ring[0:H, 0, 0:H * P], A["head_sel"]).then_inc(S("head_sel_in"), 16)
            for q in range(2):
                s = first_slab["fo"] + q
                load_slab(s, cols(dense["fo"], 0, DT, 256 * q, 256))
                free_after(s, tile_done, first["fo"] + 2 * q + 2)
            sp.wait_ge(S("pt_in"), 16)
            sp.wait_ge(S("page_space"), 1)
            with sp.Fori(0, BS) as b:
                for j in range(PAGES):
                    page = sp.value_load(pt_sb[0:1, bass.ds(b * PAGES + j, 1)], min_val=0,
                                         max_val=A["cache_k"].shape[0] - 1)
                    sp.wait_ge(S("k_page_free"), b * PAGES + (j + 1))
                    sp.dma_start(k_page(j % 4), A["cache_k"][bass.ds(page, 1)].rearrange("a t h d -> (a t) (h d)")
                                 ).then_inc(S(f"k_page{j % 4}"), 16)
                for j in range(PAGES):
                    page = sp.value_load(pt_sb[0:1, bass.ds(b * PAGES + j, 1)], min_val=0,
                                         max_val=A["cache_k"].shape[0] - 1)
                    if j == 0:
                        sp.wait_ge(S("v_pages_free"), b + 1)
                    sp.dma_start(v_page(j), A["cache_v"][bass.ds(page, 1)].rearrange("a t h d -> (a t) (h d)")
                                 ).then_inc(S(f"v_page{j}"), 16)
            free_at[0] = free_at[3] = (S("fox_out"), 2 * BS)
            for q in range(2, 4):
                s = first_slab["fo"] + q
                load_slab(s, cols(dense["fo"], 0, DT, 256 * q, 256))
                free_after(s, tile_done, first["fo"] + 2 * q + 2)
            load_ffn(3)
        @block.tensor
        def _(pe):
            def begin(t):
                if t >= 8:
                    who = owner[t - 8]
                    pe.wait_ge({"d": dve_freed, "a": act_freed}[who], freed[who][t - 7])

            def end(mm):
                mm.then_inc(tile_done, 1)

            def split(s):
                pe.wait_ge(S("w_lo"), s + 1)

            def mm3(out, s, k, mt, x_hi, x_lo, first_, last):
                cs = slice(mt * P, (mt + 1) * P)
                pe.matmul(out, part(s, 1)[:, k, cs], x_hi, start=first_, stop=False)
                pe.matmul(out, part(s, 1)[:, k, cs], x_lo, start=False, stop=False)
                return pe.matmul(out, part(s, 0)[:, k, cs], x_hi, start=False, stop=last)

            def dve_done(t):
                pe.wait_ge(dve_freed, freed["d"][t + 1])

            def act_done(t):
                pe.wait_ge(act_freed, freed["a"][t + 1])

            def norm(name):
                i, t = norms.index(name), first["norm_" + name]
                begin(t)
                for k in range(DT):
                    pe.wait_ge(S("sq_ready"), i * DT + k + 1)
                    mm = pe.matmul(bank(t, T), ones, sq[:, k, :], start=(k == 0), stop=(k == DT - 1))
                end(mm)

            def gemm(name, x_hi, x_lo, ready=None):
                for q in range(4):
                    s = first_slab[name] + q
                    split(s)
                    for mt in range(2):
                        t = first[name] + 2 * q + mt
                        begin(t)
                        for k in range(DT):
                            if ready and q == mt == 0:
                                pe.wait_ge(ready[0], ready[1] + k + 1)
                            mm = mm3(bank(t, T), s, k, mt, x_hi[:, k, :], x_lo[:, k, :], k == 0, k == DT - 1)
                        end(mm)

            def xn_ready(name):
                return S("xn_split"), split_norms.index(name) * DT

            def ffn(n):
                if n != 2:
                    norm(f"ffn{n}")
                base, s0 = first[f"up{n}"], first_slab[f"up{n}"]
                d0 = freed["d"][base]
                pe.wait_ge(act_freed, freed["a"][base])
                pe.wait_ge(dve_freed, d0)
                xr = xn_ready(f"ffn{n}")

                def up(j, mt, check=False):
                    for k in range(DT):
                        if check:
                            pe.wait_ge(xr[0], xr[1] + k + 1)
                        mm = mm3(ps[:, (base + 2 * j + mt) % 8, 0:T], s0 + j % 4, k, mt, xn_hi[:, k, :], xn_lo[:, k, :],
                                 k == 0, k == DT - 1)
                    end(mm)

                pe.wait_ge(xr[0], xr[1] + DT)
                with pe.Fori(0, 5) as i:
                    for j in range(4):
                        pe.wait_ge(S("w_lo"), i * 4 + (s0 + j + 1))
                        for mt in range(2):
                            pe.wait_ge(dve_freed, i * 8 + (d0 + 2 * j + mt - 7))
                            up(j, mt)
                for j in (20, 21):
                    split(s0 + j)
                    for mt in range(2):
                        begin(base + 2 * j + mt)
                        up(j, mt)
                down = first[f"down{n}"]
                for mp in range(4):
                    for s3 in range(3):
                        s = first_slab[f"down{n}"] + 3 * mp + s3
                        k0, k1 = 8 * s3, min(8 * s3 + 8, FT)
                        split(s)
                        for mt in range(2):
                            t = down + 2 * mp + mt
                            if s3 == 0:
                                begin(t)
                            for k in range(k0, k1):
                                if mp == mt == 0:
                                    pe.wait_ge(S("hid_split"), FT * n + k + 1)
                                mm = mm3(bank(t, T), s, k - k0, mt, hid_hi[:, k, :], hid_lo[:, k, :],
                                         k == 0, k == FT - 1)
                            if s3 == 2:
                                end(mm)
                        if s3 < 2:
                            mm.then_inc(S("down_slab_used"), 1)

            prow = arena[:, 5 * TW:5 * TW + 2 * P].rearrange("p (g d) -> p g d", g=2)
            xt = arena[:, 3 * TW:3 * TW + 3 * D].rearrange("p (g d) -> p g d", g=3)
            pe.sem_inc(S("k_page_free"), 4)
            pe.sem_inc(S("v_pages_free"), 1)
            pe.sem_inc(S("kT_act"), 2)
            pe.sem_inc(S("kT_dve"), 2)
            pe.sem_inc(S("s_done"), 1)
            pe.wait_ge(S("const_in"), 16)
            pe.wait_ge(S("param_in"), 16 * N_PARAM_DMAS)
            t = first["params"]
            end(pe.transpose(bank(t, P), prow[:, 0, :], ident))
            end(pe.transpose(bank(t + 1, rows - P), prow[0:rows - P, 1, :], ident[0:rows - P, 0:rows - P]))
            pe.wait_ge(S("shift_in"), 16)
            t = first["shift_in"]
            for m in range(DT):
                mm = pe.transpose(ps[:, t % 8, m * BS:(m + 1) * BS],
                                  arena[0:BS, 6 * TW + m * P:6 * TW + (m + 1) * P], ident[0:BS, 0:BS])
            end(mm)
            pe.wait_ge(S("x_in"), 48)
            for m in range(DT):
                t = first["x"] + m
                begin(t)
                for g, n in ((0, P), (1, P), (2, TS)):
                    mm = pe.transpose(ps[:, t % 8, g * P:g * P + n], xt[0:n, g, m * P:(m + 1) * P],
                                      ident[0:n, 0:n])
                end(mm)

            ffn(0)
            norm("mix0")

            pe.wait_ge(S("shift_cols"), 1)
            for j in range(2):
                t = first["shift_out"] + j
                begin(t)
                for m in range(4):
                    mm = pe.transpose(ps[0:BS + 1, t % 8, m * P:(m + 1) * P], shc[:, 4 * j + m, :], ident)
                end(mm)

            xs = [A_(1), A_(2)]
            for j, name in enumerate("rkv"):
                gemm(name, AR_(6 + j % 2), AR_(1 + j % 2), (S("xs_split"), j * DT))
            for slot, j in ((LORA1, 1), (LORA2, 2), (LORA3, 3)):
                pe.wait_ge(S(f"slab{slot}"), low_rank[j])
            for j, (name, c0, c1, w2, out) in enumerate((
                    ("w", 0, 64, lora2[0:64, 0:D], root[0:64, :]),
                    ("a", 64, 128, lora2[0:64, D:2 * D], rs[0:64, :]),
                    ("g", 128, 256, slot_(LORA3)[:, 0:D], root[:, :]))):
                t = first[name + "1"]
                begin(t)
                for k in range(DT):
                    pe.wait_ge(S("xs_raw"), (3 + j) * DT + k + 1)
                    mm = pe.matmul(ps[0:c1 - c0, t % 8, 0:T], lo1[:, k, c0:c1], xs[(3 + j) % 2][:, k, :],
                                   start=(k == 0), stop=(k == DT - 1))
                end(mm)
                (dve_done if name == "a" else act_done)(t)
                for m in range(DT):
                    t = first[name + "2"] + m
                    begin(t)
                    end(pe.matmul(bank(t, T), w2[:, m * P:(m + 1) * P], out, start=True, stop=True))

            def head_sums(name, src, ready):
                for m in range(DT):
                    t = first[name] + m
                    begin(t)
                    pe.wait_ge(ready, m + 1)
                    end(pe.matmul(bank(t, T), pair, src[:, m, :], start=True, stop=True))

            head_sums("kk_norm", A_(1), S("kk_sq"))
            head_sums("bonus", bonus, S("rk_ready"))

            for b in range(BS):
                t = first["state_in"] + b
                begin(t)
                pe.wait_ge(S(f"state_in{b % 2}"), 16 * (b // 2 + 1))
                for p in range(HP):
                    mm = pe.transpose(ps[:, t % 8, p * HD:(p + 1) * HD],
                                      state_in[b % 2][0:HD, p * P:(p + 1) * P], ident[0:HD, 0:HD])
                end(mm)

            def halves(name, body, *waits):
                for hf in range(2):
                    t = first[name] + hf
                    begin(t)
                    for w in waits:
                        w(hf)
                    for q in range(4):
                        mm = body(4 * hf + q, t % 8, q)
                    end(mm)

            def mmul(out, lhsT, rhs, start=True, stop=True):
                return pe.matmul(out, lhsT, rhs, start=start, stop=stop)

            for c in range(CHUNKS):
                sample = c == CHUNKS - 1

                def R_c(p):
                    return Rf[:, p, c * C:(c + 1) * C]

                def o(b_, q, n=P, off=0):
                    return ps[:, b_, q * P + off:q * P + off + n]

                halves(f"LT{c}", lambda p, b_, q: mmul(o(b_, q), B_bd[:, p, :], A_bd[:, p, :]),
                       lambda hf: pe.wait_ge(S("bd_ready"), 4 * (2 * c + hf) + 4))
                halves(f"KA{c}", lambda p, b_, q: mmul(o(b_, q), K_bd[:, p, :], A_bd[:, p, :]))

                def grams(p, b_, q):
                    mmul(o(b_, q, C), B_bd[:, p, :], R_c(p))
                    return mmul(o(b_, q, C, C), K_bd[:, p, :], R_c(p))
                halves(f"RG{c}", grams)
                for j, src in enumerate((V_bd, B_bd, K_bd)):
                    for hf in range(2):
                        t = first[f"tok{c}"] + 2 * j + hf
                        begin(t)
                        for q in range(4):
                            mm = pe.transpose(o(t % 8, q), src[:, 4 * hf + q, :], ident)
                        end(mm)
                halves(f"D{c}", lambda p, b_, q: pe.transpose(o(b_, q), DT_bd[:, p, :], ident),
                       lambda hf: pe.wait_ge(S("DT_ready"), 2 * c + hf + 1))
                lvs = levels(c)
                for n_lv, lv in enumerate(lvs):
                    prev = f"D{c}" if lv == lvs[0] else f"DD{c}_{lvs[n_lv - 1]}"
                    halves(f"Z{c}_{lv}", lambda p, b_, q: mmul(o(b_, q), join_bd[:, p, :], D_bd[:, p, :]),
                           lambda hf: pe.wait_ge(S("join_ready"), join_count[c, lv] + hf + 1),
                           lambda hf: dve_done(first[prev] + hf))
                    if lv != lvs[0]:
                        dve_done(first[f"DDT{c}_{lvs[n_lv - 1]}"] + 1)
                    if lv != lvs[-1]:
                        halves(f"DD{c}_{lv}", lambda p, b_, q: mmul(o(b_, q), DT_bd[:, p, :], Z_bd[:, p, :]),
                               lambda hf: act_done(first[f"Z{c}_{lv}"] + hf))
                    halves(f"DDT{c}_{lv}", lambda p, b_, q: mmul(o(b_, q), Z_bd[:, p, :], DT_bd[:, p, :]),
                           lambda hf: act_done(first[f"Z{c}_{lv}"] + hf))
                if sample:
                    for hf in range(2):
                        t = first["own_state"] + hf
                        begin(t)
                        for q in range(4):
                            p = 4 * hf + q
                            pe.wait_ge(S("S0_ready"), p + 1)
                            s0 = S0_bd[p % 2].rearrange("p m c -> p (m c)").rearrange("p (b c) -> p b c", b=BS)
                            for e, src in enumerate((Af, Rf)):
                                for b in range(BS):
                                    cc = TP + b * QS
                                    mm = mmul(ps[:, t % 8, q * P + e * C + b * QS:q * P + e * C + (b + 1) * QS],
                                              s0[:, b, :], src[:, p, cc:cc + QS])
                            if q < 3:
                                mm.then_inc(S("S0_used"), 1)
                            else:
                                end(mm)

                def solve_rhs(p, b_, q):
                    if c > 0:
                        mmul(o(b_, q), XT_bd[:, p, :] if sample else A_bd[:, p, :],
                             ident if sample else S_bd[:, p, :], True, False)
                    return mmul(o(b_, q), KA_bd[:, p, :], V_tok[:, p, :], c == 0, True)
                halves(f"X{c}", solve_rhs,
                       lambda hf: act_done(first[f"tok{c}"] + 1),
                       lambda hf: dve_done(first["own_state"] + hf if sample else
                                           first[f"S{c - 1}"] + hf if c else first[f"KA{c}"] + hf))
                halves(f"U{c}", lambda p, b_, q: mmul(o(b_, q), DT_bd[:, p, :], X_bd[:, p, :]),
                       lambda hf: act_done(first[f"X{c}"] + hf),
                       lambda hf: dve_done(first[f"DDT{c}_{lvs[-1]}"] + hf))

                def outputs(p, b_, q):
                    if c > 0 and not sample:
                        mmul(o(b_, q, C), S_bd[:, p, :], R_c(p), True, False)
                    mmul(o(b_, q, C), X_bd[:, p, :], RG_bd[:, p, 0:C], c == 0 or sample, False)
                    return mmul(o(b_, q, C), V_tok[:, p, :], RG_bd[:, p, C:2 * C], False, True)
                halves(f"Y{c}", outputs, lambda hf: act_done(first[f"U{c}"] + hf))
                if not sample:
                    def states(p, b_, q):
                        mmul(o(b_, q), B_tok[:, p, :], X_bd[:, p, :], True, False)
                        return mmul(o(b_, q), K_tok[:, p, :], V_tok[:, p, :], False, True)
                    halves(f"S{c}", states)
                    if c == CHUNKS - 2:
                        halves("wkv_prompt", lambda p, b_, q: pe.transpose(o(b_, q), S_bd[:, p, :], ident),
                               lambda hf: dve_done(first[f"S{c}"] + hf))
            for p in range(HP):
                t = first[f"SS{p}"]
                begin(t)
                pe.wait_ge(S("uv_ready"), 2 * p + 2)
                mmul(bank(t), B_tok[:, p, :], UV[p % 2][:, 0, :, :], True, False)
                end(mmul(bank(t), K_tok[:, p, :], UV[p % 2][:, 1, :, :], False, True))
                dve_done(t)
                for j in range(2):
                    t = first[f"ST{p}"] + j
                    begin(t)
                    for q in range(4):
                        mm = pe.transpose(ps[0:HD, t % 8, q * P:(q + 1) * P], SF[:, p % 2, 4 * j + q, :], ident)
                    end(mm)

            head_sums("mean", Yf, S("y_ready"))
            head_sums("var", A_(0), S("y_sq"))
            gemm("wo", AR_(3), AR_(9), (S("wo_split"), 0))
            ffn(1)

            norm("kv")
            gemm("kk", xn_hi, xn_lo, xn_ready("kv"))
            gemm("vv", xn_hi, xn_lo)
            t = first["logf"]
            begin(t)
            pe.wait_ge(S("wf_in"), 32)
            for k in range(DT):
                mmul(ps[0:H, t % 8, 0:T], w_f[:, k, :], xn_hi[:, k, :].bitcast(F32), k == 0, False)
                mm = mmul(ps[0:H, t % 8, 0:T], w_f[:, k, :], xn_lo[:, k, :].bitcast(F32), False, k == DT - 1)
            end(mm)
            head_sums("k_norm", A_(1), S("k_sq"))
            t = first["logf_tok"]
            begin(t)
            pe.wait_ge(S("logf_ready"), 2)
            for e, src in enumerate((LF, FT_)):
                for g, n in ((0, P), (1, P), (2, TS)):
                    mm = pe.transpose(ps[0:n, t % 8, (3 * e + g) * H:(3 * e + g + 1) * H],
                                      src[:, g * P:g * P + n], ident[0:H, 0:H])
            end(mm)

            def to_tokens(name, src, ready):
                for g, n in ((0, P), (1, P), (2, TS)):
                    for j in range(2):
                        t = first[name] + 2 * g + j
                        begin(t)
                        for m in range(4):
                            if g == 0:
                                ready(4 * j + m)
                            mm = pe.transpose(ps[0:n, t % 8, m * P:(m + 1) * P],
                                              src[:, 4 * j + m, g * P:g * P + n], ident)
                        end(mm)

            to_tokens("k_tok", kT, lambda m: pe.wait_ge(S("k_ready"), 1))
            to_tokens("v_tok", A_(0), lambda m: dve_done(first["vv"] + 7))
            ffn(2)

            norm("mix1")
            gemm("q", xn_hi, xn_lo, xn_ready("mix1"))
            head_sums("q_norm", q_sq, S("q_sq"))
            t = first["fq_col"]
            begin(t)
            end(mmul(bank(t, TS), K("selcol")[0:H, :], FT_[:, TP:T]))
            pe.wait_ge(S("lfp_in"), 16 * BS * PAGES)
            for j in range(4):
                t = first["fk_past"] + j
                begin(t)
                end(mmul(bank(t), K("later") if j < 2 else ones,
                         lfp.rearrange("p b j h -> p (b j h)")[:, j % 2 * 512:j % 2 * 512 + 512]))
            pe.wait_ge(S("head_sel_in"), 16)
            pe.wait_ge(S("nF_ready"), 1)
            for hd in range(H):
                t = first["fb"] + hd
                begin(t)
                end(mmul(bank(t, 384), head_sel[:, hd, :], nF_dup))

            def scores(hd):
                t = first["fox"] + fox_tile(hd, 0)
                begin(t)
                pe.wait_ge(S("qp_ready"), hd // 2 + 1)
                qp = qp_bd[:, hd // 2 % 2, hd % 2, :]
                mmul(ps[:, t % 8, 0:P], qp[:, 0:P], kT[:, hd // 2, 0:P])
                end(mmul(ps[:, t % 8, P:3 * P], qp[:, P:2 * P], kT[:, hd // 2, 0:2 * P]))

            def turn(hd):
                t = first["fox"] + fox_tile(hd, 1)
                begin(t)
                pe.wait_ge(S("p_ready"), 2 * hd + 2)
                for j in range(3):
                    mm = pe.transpose(ps[:, t % 8, j * P:(j + 1) * P], s_pr[:, hd % 2, j * P:(j + 1) * P], ident)
                end(mm)

            def values(hd):
                t = first["fox"] + fox_tile(hd, 2)
                begin(t)
                dve_done(first["fox"] + fox_tile(hd, 1))
                vc = slice(hd // 2 * P, (hd // 2 + 1) * P)
                mmul(ps[:, t % 8, 0:P], v_tok[:, 0, vc], pT[:, hd % 2, 0:P])
                mmul(ps[:, t % 8, P:2 * P], v_tok[:, 0, vc], pT[:, hd % 2, P:2 * P], True, False)
                end(mmul(ps[:, t % 8, P:2 * P], v_tok[:, 1, vc], pT[:, hd % 2, 2 * P:3 * P], False, True))

            for kind, hd in fox_order:
                (scores, turn, values)[kind](hd)

            def unit_scores(b, u):
                pe.wait_ge(S("kT_act"), b * PAGES + (2 * u + 4))
                pe.wait_ge(S("kT_dve"), b * PAGES + (2 * u + 4))
                bk, c0 = u // 2, u % 2 * 256
                for j in range(2):
                    pe.matmul(ps[:, bk, c0 + j * P:c0 + (j + 1) * P],
                              nfk_rep[:, (2 * u + j) * P:(2 * u + j + 1) * P], ident,
                              start=(j == 0), stop=False, skip_group_check=True)
                for r in range(2):
                    for g in range(4):
                        mm = pe.matmul(ps[32 * g:32 * g + 32, bk, c0:c0 + 256],
                                       q_cur[:, (2 * g + r) * 32:(2 * g + r + 1) * 32],
                                       k_feat[u % 2][:, 2 * g + r, :],
                                       start=False, stop=(r == 1), skip_group_check=True)
                return mm

            dve_done(first["fox"] + 3 * H - 1)
            with pe.Fori(0, BS) as b:
                for j in range(PAGES):
                    kb = 3 + j % 2 * 2
                    pe.wait_ge(S(f"k_page{j % 4}"), b * 32 + (16 * (j // 4 + 1)))
                    pe.wait_ge(S("kT_act"), b * PAGES + (j + 1))
                    pe.wait_ge(S("kT_dve"), b * PAGES + (j + 1))
                    for m in range(DT):
                        mm = pe.transpose(ps[:, kb + m // 4, m % 4 * P:(m % 4 + 1) * P],
                                          k_page(j % 4)[:, m * P:(m + 1) * P], ident)
                    mm.then_inc(S("k_page_free"), 1)
                    if j == 2:
                        pe.wait_ge(S("q_cur"), b * 4 + 4)
                        pe.wait_ge(S("nfk_rep"), b + 1)
                    if j >= 2 and j % 2 == 1:
                        unit_scores(b, j // 2 - 1)
                unit_scores(b, 3)
                for r in range(2):
                    for g in range(4):
                        mm = mmul(ps[32 * g:32 * g + 32, 2, 0:TS], q_cur[:, (2 * g + r) * 32:(2 * g + r + 1) * 32],
                                  kT[:, 2 * g + r, TP:T], r == 0, r == 1)
                mm.then_inc(S("s_done"), 1)
                pe.wait_ge(S("p_row"), b * 2 + 2)
                for j in range(PAGES):
                    pe.transpose(ps[:, j // 4, j % 4 * P:(j % 4 + 1) * P], p_row[:, j * P:(j + 1) * P], ident)
                pe.transpose(ps[0:TS, 2, P:2 * P], p_row[:, PAST:PAST + TS], ident).then_inc(S("p_turned"), 1)
                pe.wait_ge(S("pT_act"), b + 1)
                pe.wait_ge(S("pT_dve"), b * 2 + 2)
                for j in range(PAGES + 1):
                    if j < PAGES:
                        pe.wait_ge(S(f"v_page{j}"), b * 16 + 16)
                    for g in range(4):
                        v = v_page(j) if j < PAGES else v_tok[0:TS, 2, :]
                        mm = mmul(ps[32 * g:32 * g + 32, 7, 0:256], p_T[0:v.shape[0], j, 32 * g:32 * g + 32],
                                  v[:, 256 * g:256 * g + 256], j == 0, j == PAGES)
                mm.then_inc(S("v_pages_free"), 1)
                pe.wait_ge(S("o_own"), b * 2 + 2)
                pe.transpose(ps[:, 7, 256:384], o_two, ident).then_inc(S("o_turned"), 1)
            pe.wait_ge(S("o_split"), 2)
            gemm("fo", oT_hi, oT_lo)
            ffn(3)
            to_tokens("y", h, lambda m: dve_done(first["down3"] + m))
        @block.scalar
        def _(act):
            def filled(t):
                act.wait_ge(tile_done, t + 1)

            def hi(s):
                slot, k, value = slabs[s]
                act.wait_ge(S(f"slab{slot}"), value)
                act.activation(part(s, 1), raw(s), ACT.Copy).then_inc(S("w_hi"), 1)

            def square(src, m):
                act.wait_ge(dve_freed, freed["d"][first[src] + m + 1])
                act.activation(sq[:, m, :], h[:, m, :], ACT.Square).then_inc(S("sq_ready"), 1)

            def root_mean(name):
                i, t = norms.index(name), first["norm_" + name]
                filled(t)
                if i:
                    act.wait_ge(S("rs_ready"), i)
                act.activation(root[:, :], bank(t, T), ACT.Sqrt, bias=eps, scale=1.0 / D).then_inc(act_freed, 1)

            def xn_high(name):
                for m in range(DT):
                    act.wait_ge(S("xn_raw"), normed.index(name) * DT + m + 1)
                    act.activation(xn_hi[:, m, :], xn[:, m, :], ACT.Copy).then_inc(S("xn_hi"), 1)

            def gemm(name, ahead=True, norm_next=False):
                for q in range(4):
                    if ahead:
                        hi(first_slab[name] + q + 2)
                    if norm_next:
                        square(name, 2 * q)
                        square(name, 2 * q + 1)

            def ffn(n):
                if n != 2:
                    root_mean(f"ffn{n}")
                xn_high(f"ffn{n}")
                base, s0 = first[f"up{n}"], first_slab[f"up{n}"]
                d0 = freed["d"][base]
                if n == 2:
                    act.wait_ge(S("k_stored"), 48)
                with act.Fori(0, 5) as i:
                    for j in range(4):
                        slot, _, value = slabs[s0 + j + 2]
                        act.wait_ge(S(f"slab{slot}"), i * 16 + value)
                        act.activation(part(s0 + j + 2, 1), raw(s0 + j + 2), ACT.Copy).then_inc(S("w_hi"), 1)
                        for mt in range(2):
                            if j % 2 == 0:
                                act.wait_ge(tile_done, i * 8 + (base + 2 * j + mt + 1))
                                act.activation(sg[:, j + mt, :], ps[:, (base + 2 * j + mt) % 8, 0:T], ACT.Silu
                                               ).then_inc(S("silu_ready"), 1)
                            else:
                                act.wait_ge(dve_freed, i * 8 + (d0 + 2 * j - 2 + (4 if mt else 1)))
                                f = 2 * (j // 2) + mt
                                act.activation(hid_hi[:, bass.ds(i * 4 + f, 1), :], hid[:, bass.ds(i * 4 + f, 1), :],
                                               ACT.Copy).then_inc(S("hid_hi"), 1)
                for j in range(2):
                    hi(s0 + 22 + j)
                    for mt in range(2):
                        if j == 0:
                            filled(base + 40 + mt)
                            act.activation(sg[:, mt, :], bank(base + 40 + mt, T), ACT.Silu).then_inc(S("silu_ready"), 1)
                        else:
                            act.wait_ge(dve_freed, d0 + 40 + (4 if mt else 1))
                            act.activation(hid_hi[:, 20 + mt, :], hid[:, 20 + mt, :], ACT.Copy
                                           ).then_inc(S("hid_hi"), 1)
                for mp in range(4):
                    for s3 in range(3):
                        s = first_slab[f"down{n}"] + 3 * mp + s3 + 2
                        if s < len(slabs):
                            hi(s)
                    if n < 3:
                        square(f"down{n}", 2 * mp)
                        square(f"down{n}", 2 * mp + 1)

            act.wait_ge(S("eps_ready"), 2)
            hi(0)
            hi(1)
            for m in range(DT):
                square("x", m)
            ffn(0)
            root_mean("mix0")
            for j, name in enumerate("rkv"):
                for m in range(DT):
                    act.wait_ge(S("xs_raw"), j * DT + m + 1)
                    act.activation(AR_(6 + j % 2)[:, m, :], A_(1 + j % 2)[:, m, :], ACT.Copy).then_inc(S("xs_hi"), 1)
                if j:
                    gemm("rk"[j - 1])
            hi(first_slab["v"] + 2)
            hi(first_slab["v"] + 3)
            def lora(name, func, mid, out, bias):
                t = first[name + "1"]
                if name != "a":
                    filled(t)
                    n = HD if name == "w" else P
                    if name == "w":
                        act.wait_ge(S("rs_ready"), 2)
                    else:
                        filled(first["w2"] + 7)
                    act.activation(mid, ps[0:n, t % 8, 0:T], func).then_inc(act_freed, 1)
                if bias:
                    for m in range(DT):
                        filled(first[name + "2"] + m)
                        act.activation(out[:, m, :], bank(first[name + "2"] + m, T), ACT.Sigmoid,
                                       bias=prm(bias, m)).then_inc(act_freed, 1)

            lora("w", ACT.Tanh, root[0:HD, :], A_(6), "rw_w0")
            lora("a", None, None, A_(7), "rw_a0")
            lora("g", ACT.Sigmoid, root[:, :], None, None)
            for m in range(DT):
                act.wait_ge(S("kk_raw"), m + 1)
                act.activation(A_(1)[:, m, :], A_(0)[:, m, :], ACT.Square).then_inc(S("kk_sq"), 1)
            act.wait_ge(dve_freed, freed["d"][first["kk_norm"] + DT])
            act.activation(A_(1), A_(1), ACT.Sqrt).then_inc(S("kk_root"), 1)
            act.wait_ge(S("decay_sums"), 1)
            act.activation(A_(10), A_(9), ACT.Exp, scale=-DECAY).then_inc(S("decays"), 1)
            act.wait_ge(S("a_used"), 1)
            act.activation(A_(7), A_(9), ACT.Exp, scale=DECAY).then_inc(S("decays"), 1)
            act.activation(A_(6), A_(6), ACT.Exp, scale=-DECAY).then_inc(S("decays"), 1)

            def copy_halves(name, dst):
                for hf in range(2):
                    filled(first[name] + hf)
                    act.activation(dst[:, 4 * hf:4 * hf + 4, :], bank(first[name] + hf), ACT.Copy
                                   ).then_inc(act_freed, 1)

            for c in range(CHUNKS):
                for j, dst in enumerate((V_tok, B_tok, K_tok)):
                    for hf in range(2):
                        t = first[f"tok{c}"] + 2 * j + hf
                        filled(t)
                        act.activation(dst[:, 4 * hf:4 * hf + 4, :], bank(t), ACT.Copy).then_inc(act_freed, 1)
                for lv in levels(c):
                    copy_halves(f"Z{c}_{lv}", Z_bd)
                copy_halves(f"X{c}", X_bd)
                copy_halves(f"U{c}", X_bd)
            for p in range(HP):
                if p >= 2:
                    act.wait_ge(S(f"state_out{p % 2}"), 32 * (p // 2))
                for j in range(2):
                    filled(first[f"ST{p}"] + j)
                    act.activation(state_out[p % 2][0:HD, j * 512:(j + 1) * 512], bank(first[f"ST{p}"] + j, 512, HD),
                                   ACT.Copy).then_inc(act_freed, 1)
            hi(first_slab["wo"])
            for m in range(DT):
                act.wait_ge(dve_freed, freed["d"][first["mean"] + m + 1])
                act.activation(A_(0)[:, m, :], Yf[:, m, :], ACT.Square).then_inc(S("y_sq"), 1)
            for m in range(DT):
                filled(first["var"] + m)
                act.activation(A_(1)[:, m, :], bank(first["var"] + m, T), ACT.Sqrt, bias=eps_ln, scale=1.0 / HD
                               ).then_inc(act_freed, 1)
            hi(first_slab["wo"] + 1)
            for m in range(DT):
                act.wait_ge(S("wo_raw"), m + 1)
                act.activation(AR_(3)[:, m, :], Yf[:, m, :], ACT.Copy).then_inc(S("wo_hi"), 1)
            act.wait_ge(S("wkv_prompt_out"), 32)
            gemm("wo", norm_next=True)
            ffn(1)
            root_mean("kv")
            xn_high("kv")

            def head_roots(name, src_name, src, dst, sq_sem):
                for q in range(4):
                    hi(first_slab[src_name] + q + 2)
                    for m in (2 * q, 2 * q + 1):
                        act.wait_ge(dve_freed, freed["d"][first[src_name] + m + 1])
                        act.activation(dst[:, m, :], src[:, m, :], ACT.Square).then_inc(S(sq_sem), 1)
                if name == "k_norm":
                    gemm("vv")
                for m in range(DT):
                    filled(first[name] + m)
                    act.activation(dst[:, m, :], bank(first[name] + m, T), ACT.Sqrt, bias=eps, scale=1.0 / HD
                                   ).then_inc(act_freed, 1)

            head_roots("k_norm", "kk", kT, A_(1), "k_sq")
            act.wait_ge(S("logf_arg"), 1)
            act.activation(lw[1], lw[1], ACT.Exp).then_inc(S("logf_exp"), 1)
            ffn(2)
            root_mean("mix1")
            xn_high("mix1")
            head_roots("q_norm", "q", q_f, q_sq, "q_sq")
            for hd in range(H):
                act.wait_ge(S("s_ready"), 2 * hd + 2)
                s = s_pr[:, hd % 2, :]
                st = fstat[:, hd % 2, :]
                act.activation(s[:, 0:P], s[:, 0:P], ACT.Exp, bias=st[:, 4:5], accum_out=st[:, 6:7]
                               ).then_inc(S("e_ready"), 1)
                act.activation(s[:, P:3 * P], s[:, P:3 * P], ACT.Exp, bias=st[:, 5:6], accum_out=st[:, 7:8]
                               ).then_inc(S("e_ready"), 1)
            act.wait_ge(dve_freed, freed["d"][first["fox"] + 3 * H])
            act.activation(oT_hi[:, :, 0:TP], oT[:, :, 0:TP], ACT.Copy).then_inc(S("o_hi"), 1)
            with act.Fori(0, BS) as b:
                if True:
                    act.wait_ge(S("s_done"), b + 1)
                    nf = nfk[:, bass.ds(b, 1), :, :].rearrange("p b j h -> p (b j h)")
                    act.activation(nfk_rep.rearrange("p (n q) -> p n q", q=QS),
                                   nf.unsqueeze(2).to_broadcast([P, PAGES * H, QS]), ACT.Copy
                                   ).then_inc(S("nfk_rep"), 1)
                for j in range(PAGES):
                    act.wait_ge(S("k_page_free"), b * PAGES + (j + 5))
                    act.activation(k_feat[j // 2 % 2][:, 0:4, j % 2 * P:(j % 2 + 1) * P],
                                   ps[:, 3 + j % 2 * 2, :].rearrange("p (m t) -> p m t", m=4), ACT.Copy
                                   ).then_inc(S("kT_act"), 1)
                act.wait_ge(S("less_max"), b + 1)
                act.activation(p_row[:, 0:PAST], ps[:, 0:2, :].rearrange("p g c -> p (g c)"), ACT.Exp,
                               bias=sst[:, 4:5], accum_out=sst[:, 6:7]).then_inc(S("p_row"), 1)
                act.activation(p_row[:, PAST:PAST + TS], s_new, ACT.Exp,
                               bias=sst[:, 4:5], accum_out=sst[:, 7:8]).then_inc(S("p_row"), 1)
                act.wait_ge(S("p_turned"), b + 1)
                act.activation(p_T[:, 0:4, :], ps[:, 0, :].rearrange("p (g c) -> p g c", g=4), ACT.Copy
                               ).then_inc(S("pT_act"), 1)
            act.wait_ge(S("fox_out"), 2 * BS)
            act.activation(oT_hi[:, :, TP:T], oT[:, :, TP:T], ACT.Copy).then_inc(S("o_hi"), 1)
            gemm("fo", norm_next=True)
            ffn(3)

        @block.vector
        def _(dve):
            steps = [0]

            def link(ins):
                steps[0] += 1
                ins.then_inc(S("dve_step"), 1)
                dve.wait_ge(S("dve_step"), steps[0])

            def filled(t):
                dve.wait_ge(tile_done, t + 1)

            def free(ins, n=1):
                ins.then_inc(dve_freed, n)

            TT, TS_, STT, CP = dve.tensor_tensor, dve.tensor_scalar, dve.scalar_tensor_tensor, dve.tensor_copy

            def low(out, x, high):
                return TT(out, x, high.bitcast(F32), ALU.subtract)

            def lo(s):
                dve.wait_ge(S("w_hi"), s + 1)
                low(part(s, 0), raw(s), part(s, 1)).then_inc(S("w_lo"), 1)

            def norm(name, param, row):
                if name != "ffn2":
                    i, t = norms.index(name), first["norm_" + name]
                    dve.wait_ge(act_freed, freed["a"][t + 1])
                    dve.reciprocal(rs[:, :], root[:, :]).then_inc(S("rs_ready"), 1)
                    dve.wait_ge(S("rs_ready"), i + 1)

                def xn_low(m):
                    dve.wait_ge(S("xn_hi"), split_norms.index(name) * DT + m + 1)
                    low(xn_lo[:, m, :], xn[:, m, :], xn_hi[:, m, :]).then_inc(S("xn_split"), 1)

                for m in range(DT):
                    STT(xn[:, m, :], h[:, m, :], prm(param, m, row), rs[:, :], ALU.mult, ALU.mult
                        ).then_inc(S("xn_raw"), 1)
                    if m >= 2 and name != "mix0":
                        xn_low(m - 2)
                if name != "mix0":
                    xn_low(DT - 2)
                    xn_low(DT - 1)

            def ffn(n):
                norm(f"ffn{n}", "ffn_norm", n)
                base, s0 = first[f"up{n}"], first_slab[f"up{n}"]
                with dve.Fori(0, 5) as i:
                    for j in range(4):
                        dve.wait_ge(S("w_hi"), i * 4 + (s0 + j + 3))
                        low(part(s0 + j + 2, 0), raw(s0 + j + 2), part(s0 + j + 2, 1)).then_inc(S("w_lo"), 1)
                        if j % 2 == 0:
                            continue
                        dve.wait_ge(S("silu_ready"), i * 4 + (n * FT + j + 1))
                        for mt in range(2):
                            f = 2 * (j // 2) + mt
                            dve.wait_ge(tile_done, i * 8 + (base + 2 * j + mt + 1))
                            b_ = (base + 2 * j + mt) % 8
                            free(TT(hid[:, bass.ds(i * 4 + f, 1), :], sg[:, f:f + 1, :],
                                    ps[:, b_:b_ + 1, 0:T], ALU.mult), 3 if mt else 1)
                        for mt in range(2):
                            f = 2 * (j // 2) + mt
                            dve.wait_ge(S("hid_hi"), i * 4 + (n * FT + f + 1))
                            low(hid_lo[:, bass.ds(i * 4 + f, 1), :], hid[:, bass.ds(i * 4 + f, 1), :],
                                hid_hi[:, bass.ds(i * 4 + f, 1), :]).then_inc(S("hid_split"), 1)
                lo(s0 + 22)
                lo(s0 + 23)
                dve.wait_ge(S("silu_ready"), n * FT + FT)
                for mt in range(2):
                    filled(base + 42 + mt)
                    free(TT(hid[:, 20 + mt, :], sg[:, mt, :], bank(base + 42 + mt, T), ALU.mult), 3 if mt else 1)
                for mt in range(2):
                    dve.wait_ge(S("hid_hi"), n * FT + 20 + mt + 1)
                    low(hid_lo[:, 20 + mt, :], hid[:, 20 + mt, :], hid_hi[:, 20 + mt, :]).then_inc(S("hid_split"), 1)
                for mp in range(4):
                    for s3 in range(3):
                        s = first_slab[f"down{n}"] + 3 * mp + s3 + 2
                        if s < len(slabs):
                            lo(s)
                    for m in (2 * mp, 2 * mp + 1):
                        filled(first[f"down{n}"] + m)
                        free(STT(h[:, m, :], bank(first[f"down{n}"] + m, T), 0.5, h[:, m, :], ALU.mult, ALU.add))

            dve.memset(eps, RMS_EPS).then_inc(S("eps_ready"), 1)
            dve.memset(eps_ln, LNX_EPS).then_inc(S("eps_ready"), 1)
            t = first["params"]
            filled(t)
            free(CP(par[:, 0, :], bank(t, P)))
            filled(t + 1)
            free(CP(par[:, 1, 0:rows - P], bank(t + 1, rows - P)))
            dve.wait_ge(dve_freed, 2)
            link(TS_(omka, par[:, row_of["rw_k_a"] // P, row_of["rw_k_a"] % P:row_of["rw_k_a"] % P + DT],
                     -1.0, 1.0, ALU.mult, ALU.add))
            filled(first["shift_in"])
            free(CP(shT.rearrange("p m b -> p (m b)"), bank(first["shift_in"], DT * BS)))
            for m in range(DT):
                filled(first["x"] + m)
                free(CP(h[:, m, :], bank(first["x"] + m, T)))
            dve.wait_ge(dve_freed, freed["d"][first["x"] + DT])
            lo(0)
            lo(1)
            ffn(0)
            dve.wait_ge(dve_freed, freed["d"][first["down0"] + DT])
            norm("mix0", "mix_norm", 0)
            dve.wait_ge(S("xn_raw"), 2 * DT)
            CP(shc[:, :, 0:1], xn[:, :, TP - 1:TP])
            xs_sample = xn[:, :, TP:T].rearrange("p m (b t) -> p m b t", b=BS)
            link(CP(shc[:, :, 1:BS + 1], xs_sample[:, :, :, QS - 1]))
            dve.sem_inc(S("shift_cols"), 1)
            df = A_(0)
            df_s = df[:, :, TP:T].rearrange("p m (b t) -> p m b t", b=BS)
            TT(df[:, :, 1:TP], xn[:, :, 0:TP - 1], xn[:, :, 1:TP], ALU.subtract)
            TS_(df[:, :, 0:1], xn[:, :, 0:1], -1.0, None, ALU.mult)
            TT(df_s[:, :, :, 1:QS], xs_sample[:, :, :, 0:QS - 1], xs_sample[:, :, :, 1:QS], ALU.subtract)
            link(TT(df_s[:, :, :, 0], shT, xs_sample[:, :, :, 0], ALU.subtract))

            def mixed(j):
                if j >= 2:
                    filled(first[["r", "k", "v", "w1", "a1", "g1"][j - 2]] + (7 if j < 5 else 0))
                for m in range(DT):
                    STT(A_(1 + j % 2)[:, m, :], df[:, m, :], prm("rw_mu", m, j), xn[:, m, :], ALU.mult, ALU.add
                        ).then_inc(S("xs_raw"), 1)
                if j < 3:
                    for m in range(DT):
                        dve.wait_ge(S("xs_hi"), j * DT + m + 1)
                        low(AR_(1 + j % 2)[:, m, :], A_(1 + j % 2)[:, m, :], AR_(6 + j % 2)[:, m, :]
                            ).then_inc(S("xs_split"), 1)

            def copy_out(name, dst, ahead=4):
                for q in range(4):
                    if name in first_slab and q < ahead:
                        lo(first_slab[name] + q + 2)
                    for m in (2 * q, 2 * q + 1):
                        filled(first[name] + m)
                        free(CP(dst[:, m, :], bank(first[name] + m, T)))

            for j in range(2):
                t = first["shift_out"] + j
                filled(t)
                free(CP(arena[0:BS + 1, 8 * TW + j * 512:8 * TW + (j + 1) * 512],
                        bank(t, 512, BS + 1)))
            mixed(0)
            mixed(1)
            copy_out("r", Rf)
            mixed(2)
            copy_out("k", Kf)
            mixed(3)
            copy_out("v", Vf, 2)
            mixed(4)
            mixed(5)
            filled(first["a1"])
            free(CP(rs[0:HD, :], bank(first["a1"], T, HD)))
            dve.wait_ge(S("shift_stored"), 32)
            copy_out("g2", gf)
            dve.wait_ge(dve_freed, freed["d"][first["g2"] + DT])
            kk, b_, aa = A_(0), A_(1), A_(7)
            for m in range(DT):
                TS_(kk[:, m, :], Kf[:, m, :], prm("rw_k_k", m), None, ALU.mult).then_inc(S("kk_raw"), 1)
            dve.wait_ge(act_freed, freed["a"][first["a2"] + DT])
            tmp = A_(2)
            for m in range(DT):
                ins = TS_(tmp[:, m, :], aa[:, m, :], prm("rw_k_a", m), omka[:, m:m + 1], ALU.mult, ALU.add)
            link(ins)
            link(TT(Kf, Kf, tmp, ALU.mult))
            for m in range(DT):
                STT(bonus[:, m, :], Rf[:, m, :], prm("rw_r_k", m), Kf[:, m, :], ALU.mult, ALU.mult
                    ).then_inc(S("rk_ready"), 1)
            sig, cum = A_(6), A_(9)
            for m in range(DT):
                ins = dve.tensor_tensor_scan(cum[:, m, :], K("chunk"), sig[:, m, :], 0.0, ALU.mult, ALU.add)
            link(ins)
            link(TT(sig, cum, sig, ALU.subtract))
            dve.sem_inc(S("decay_sums"), 1)
            for m in range(DT):
                filled(first["kk_norm"] + m)
                free(TS_(b_[:, m, :], bank(first["kk_norm"] + m, T), 1e-24, None, ALU.max))
            dve.wait_ge(S("kk_root"), 1)
            link(dve.reciprocal(b_, b_))
            link(TT(kk, kk, b_, ALU.mult))
            link(TT(b_, kk, aa, ALU.mult))
            dve.sem_inc(S("a_used"), 1)
            for m in range(DT):
                filled(first["bonus"] + m)
                free(TT(bonus[:, m, :], bank(first["bonus"] + m, T), Vf[:, m, :], ALU.mult))
            dve.wait_ge(S("decays"), 3)
            Em, Ep = A_(7), A_(6)
            TT(Rf, Rf, Ef, ALU.mult)
            TT(Kf, Kf, Em, ALU.mult)
            TT(Bf, b_, Em, ALU.mult)
            link(STT(Af, kk, -1.0, Ep, ALU.mult, ALU.mult))
            dve.sem_inc(S("scan_in"), 1)
            for b in range(BS):
                filled(first["state_in"] + b)
                free(CP(S0[:, b, :, :], bank(first["state_in"] + b).rearrange("p (m i) -> p m i", m=HP)))

            def quad(t):
                return bank(t).rearrange("p (q c) -> p q c", q=4)

            def over(x, n=4):
                return x.unsqueeze(1).to_broadcast([P, n, x.shape[1]])

            def masked(name, dst, mask, hf):
                t = first[name] + hf
                filled(t)
                free(TT(dst[:, 4 * hf:4 * hf + 4, :], quad(t), over(K(mask)), ALU.mult))

            for c in range(CHUNKS):
                sample = c == CHUNKS - 1
                kind = "s" if sample else "p"
                for hf in range(2):
                    masked(f"LT{c}", LT_bd, "strict_" + kind, hf)
                dve.wait_ge(dve_freed, freed["d"][first[f"LT{c}"] + 2])
                for hf in range(2):
                    hs = slice(4 * hf, 4 * hf + 4)
                    link(TT(DT_bd[:, hs, :], LT_bd[:, hs, :], over(K("first_" + kind)), ALU.mult))
                    TT(DT_bd[:, hs, :], DT_bd[:, hs, :], over(ident), ALU.add).then_inc(S("DT_ready"), 1)
                for hf in range(2):
                    masked(f"KA{c}", KA_bd, "strict_" + kind, hf)
                for hf in range(2):
                    masked(f"RG{c}", RG_bd, "upto_" + kind, hf)
                for hf in range(2):
                    filled(first[f"D{c}"] + hf)
                    free(CP(D_bd[:, 4 * hf:4 * hf + 4, :], quad(first[f"D{c}"] + hf)))
                dve.wait_ge(dve_freed, freed["d"][first[f"D{c}"] + 2])
                dve.wait_ge(S("DT_ready"), 2 * c + 2)
                lvs = levels(c)
                for lv in lvs:
                    for nm, dst in (("DD", D_bd), ("DDT", DT_bd)):
                        if nm == "DD" and lv == lvs[-1]:
                            continue
                        for hf in range(2):
                            t = first[f"{nm}{c}_{lv}"] + hf
                            filled(t)
                            hs = slice(4 * hf, 4 * hf + 4)
                            free(TT(dst[:, hs, :], quad(t), dst[:, hs, :], ALU.add))
                    dve.wait_ge(dve_freed, freed["d"][first[f"DDT{c}_{lv}"] + 2])
                if sample:
                    for hf in range(2):
                        t = first["own_state"] + hf
                        filled(t)
                        hs = slice(4 * hf, 4 * hf + 4)
                        xt0 = quad(t)[:, :, 0:C].unsqueeze(2).to_broadcast([P, 4, 2, C])
                        out = XT_bd[:, hs, :].rearrange("p m (e c) -> p m e c", e=2)
                        mk = pair.rearrange("p (e c) -> p e c", e=2).unsqueeze(1).to_broadcast([P, 4, 2, C])
                        link(TT(out, xt0, mk, ALU.mult))
                        free(CP(Y0[:, hs, :], quad(t)[:, :, C:2 * C]))
                for hf in range(2):
                    t = first[f"Y{c}"] + hf
                    filled(t)
                    hs = slice(4 * hf, 4 * hf + 4)
                    dst = Yf[:, hs, c * C:(c + 1) * C]
                    if sample:
                        dve.wait_ge(dve_freed, freed["d"][first["own_state"] + 2])
                        free(TT(dst, quad(t)[:, :, 0:C], Y0[:, hs, :], ALU.add))
                    else:
                        free(CP(dst, quad(t)[:, :, 0:C]))
                if not sample:
                    for hf in range(2):
                        t = first[f"S{c}"] + hf
                        filled(t)
                        hs = slice(4 * hf, 4 * hf + 4)
                        wc = Ef[:, hs, (c + 1) * C - 1:(c + 1) * C].to_broadcast([P, 4, P])
                        if c == 0:
                            free(TT(S_bd[:, hs, :], quad(t), wc, ALU.mult))
                        else:
                            link(TT(S_bd[:, hs, :], quad(t), S_bd[:, hs, :], ALU.add))
                            free(TT(S_bd[:, hs, :], S_bd[:, hs, :], wc, ALU.mult))
                    dve.wait_ge(dve_freed, freed["d"][first[f"S{c}"] + 2])
                    if c == CHUNKS - 2:
                        for hf in range(2):
                            t = first["wkv_prompt"] + hf
                            filled(t)
                            free(CP(S_bd[:, 4 * hf:4 * hf + 4, :], quad(t)))
            for p in range(HP):
                t = first[f"SS{p}"]
                filled(t)
                sf = SF[:, p % 2, :, :]
                if p >= 2:
                    filled(first[f"ST{p - 2}"] + 1)
                wc = Ef[:, p, TP + QS - 1:T:QS].unsqueeze(2).to_broadcast([P, BS, C])
                link(TT(sf, bank(t).rearrange("p (b i) -> p b i", b=BS), S0[:, :, p, :], ALU.add))
                free(TT(sf, sf, wc, ALU.mult))
            dve.sem_inc(S("y_ready"), DT)
            lo(first_slab["wo"])
            for m in range(DT):
                t = first["mean"] + m
                filled(t)
                free(STT(Yf[:, m, :], bank(t, T), -1.0 / HD, Yf[:, m, :], ALU.mult, ALU.add))

            def wo_low(m):
                dve.wait_ge(S("wo_hi"), m + 1)
                low(AR_(9)[:, m, :], Yf[:, m, :], AR_(3)[:, m, :]).then_inc(S("wo_split"), 1)

            for m in range(DT):
                dve.wait_ge(act_freed, freed["a"][first["var"] + m + 1])
                link(dve.reciprocal(A_(1)[:, m, :], A_(1)[:, m, :]))
                link(TT(Yf[:, m, :], Yf[:, m, :], A_(1)[:, m, :], ALU.mult))
                link(TS_(Yf[:, m, :], Yf[:, m, :], prm("rw_lnx_w", m), prm("rw_lnx_b", m), ALU.mult, ALU.add))
                link(TT(Yf[:, m, :], Yf[:, m, :], bonus[:, m, :], ALU.add))
                TT(Yf[:, m, :], Yf[:, m, :], gf[:, m, :], ALU.mult).then_inc(S("wo_raw"), 1)
                if m:
                    wo_low(m - 1)
            wo_low(DT - 1)
            lo(first_slab["wo"] + 1)

            def residual(name):
                for q in range(4):
                    lo(first_slab[name] + q + 2)
                    for m in (2 * q, 2 * q + 1):
                        filled(first[name] + m)
                        free(TT(h[:, m, :], bank(first[name] + m, T), h[:, m, :], ALU.add))
                dve.wait_ge(dve_freed, freed["d"][first[name] + DT])

            residual("wo")
            ffn(1)
            dve.wait_ge(dve_freed, freed["d"][first["down1"] + DT])

            norm("kv", "kv_norm", 0)
            copy_out("kk", kT)
            copy_out("vv", A_(0))
            for j in range(2):
                r = row_of["head_norms"] + j - P
                TS_(hn_scale[:, j:j + 1], par[:, 1, r:r + 1], HD ** -0.5 if j else 1.0, None, ALU.mult)
            t = first["logf"]
            filled(t)
            x, e, z, z2 = lw
            w = root[0:H, :]
            free(TS_(x, bank(t, T, H), b_f[0:H, :], None, ALU.add))
            dve.wait_ge(dve_freed, freed["d"][t + 1])
            link(TS_(e, x, -1.0, None, ALU.mult))
            link(TT(e, e, x, ALU.min))
            dve.sem_inc(S("logf_arg"), 1)
            for m in range(DT):
                dve.wait_ge(act_freed, freed["a"][first["k_norm"] + m + 1])
            link(dve.reciprocal(A_(1), A_(1)))
            STT(kT, kT, hn_scale[:, 0:1], A_(1), ALU.mult, ALU.mult).then_inc(S("k_ready"), 1)
            dve.wait_ge(S("logf_exp"), 1)
            link(TS_(z, e, 2.0, None, ALU.add))
            link(dve.reciprocal(z, z))
            link(TT(z, z, e, ALU.mult))
            link(TT(z2, z, z, ALU.mult))
            link(TS_(e, z2, 1.0 / 19, None, ALU.mult))
            for n in range(8, 0, -1):
                link(STT(e, e, 1.0 / (2 * n + 1), z2, ALU.add, ALU.mult))
            link(STT(z, e, 1.0, z, ALU.add, ALU.mult))
            link(TS_(x, x, 0.0, None, ALU.min))
            link(STT(LF, z, -2.0, x, ALU.mult, ALU.add))
            link(dve.tensor_tensor_scan(FT_, K("seqscan")[0:H, :], LF, 0.0, ALU.mult, ALU.add))
            dve.sem_inc(S("logf_ready"), 2)
            t = first["logf_tok"]
            filled(t)
            both = bank(t, 6 * H).rearrange("p (e g h) -> p e g h", e=2, g=3)
            CP(lf_tok[:, 0:2, :], both[:, 0, 0:2, :])
            CP(F_tok[:, 0:2, :], both[:, 1, 0:2, :])
            CP(lf_tok[0:TS, 2, :], both[0:TS, 0, 2, :])
            free(CP(F_tok[0:TS, 2, :], both[0:TS, 1, 2, :]))
            dve.wait_ge(dve_freed, freed["d"][t + 1])
            dve.sem_inc(S("logf_tok_ready"), 1)
            dve.wait_ge(S("wkv_prompt_out"), 32)
            for name, dst in (("k_tok", k_tok), ("v_tok", v_tok)):
                for g, n in ((0, P), (1, P), (2, TS)):
                    for j in range(2):
                        t = first[name] + 2 * g + j
                        filled(t)
                        free(CP(dst[0:n, g, j * 512:(j + 1) * 512], bank(t, 512, n)))
            dve.wait_ge(dve_freed, freed["d"][first["v_tok"] + 6])
            ffn(2)
            dve.wait_ge(dve_freed, freed["d"][first["down2"] + DT])

            norm("mix1", "mix_norm", 1)
            copy_out("q", q_f)
            for m in range(DT):
                dve.wait_ge(act_freed, freed["a"][first["q_norm"] + m + 1])
            link(dve.reciprocal(q_sq, q_sq))
            link(STT(q_f, q_f, hn_scale[:, 1:2], q_sq, ALU.mult, ALU.mult))
            dve.sem_inc(S("q_ready"), 1)
            t = first["fq_col"]
            filled(t)
            free(CP(F_row, bank(t, TS)))
            dve.wait_ge(dve_freed, freed["d"][t + 1])
            fq = tmp_fq.rearrange("p (b q) -> p b q", b=BS)
            link(TT(fq, F_row.rearrange("p (b q) -> p b q", b=BS),
                    K("qpick").unsqueeze(1).to_broadcast([P, BS, QS]), ALU.mult))
            link(dve.tensor_reduce(fq_all, fq, AX.X, ALU.add))
            for j in range(2):
                filled(first["fk_past"] + j)
                free(CP(nfk.rearrange("p b j h -> p (b j h)")[:, j * 512:(j + 1) * 512],
                        bank(first["fk_past"] + j)))
            tot = [s_pr.rearrange("p j c -> p (j c)")[:, 0:512].rearrange("p (b j h) -> p b j h", b=4, j=PAGES),
                   qp_bd.rearrange("p j e t -> p (j e t)")[:, 0:512].rearrange("p (b j h) -> p b j h", b=4, j=PAGES)]
            for hb in range(2):
                t = first["fk_past"] + 2 + hb
                filled(t)
                free(CP(tot[hb], bank(t).rearrange("p (b j h) -> p b j h", b=4, j=PAGES)))
            dve.wait_ge(dve_freed, freed["d"][first["fk_past"] + 4])
            for hb in range(2):
                bs = slice(4 * hb, 4 * hb + 4)
                for j in range(PAGES - 2, -1, -1):
                    if j < PAGES - 2:
                        link(TT(tot[hb][:, :, j + 1, :], tot[hb][:, :, j + 1, :], tot[hb][:, :, j + 2, :], ALU.add))
                    link(TT(nfk[:, bs, j, :], nfk[:, bs, j, :], tot[hb][:, :, j + 1, :], ALU.add))
            for dst, src in ((slice(0, P), slice(0, P)), (slice(P, 3 * P), slice(0, 2 * P))):
                ins = TS_(nF_dup[:, dst], FT_[:, src], -1.0, None, ALU.mult)
            link(ins)
            dve.sem_inc(S("nF_ready"), 1)
            for hd in range(H):
                t = first["fb"] + hd
                filled(t)
                free(TT(fb[:, hd, :], bank(t, 384), K("causal"), ALU.add))
            dve.wait_ge(dve_freed, freed["d"][first["fb"] + H])
            dve.sem_inc(S("page_space"), 1)

            def queries_of(p):
                if p >= 2:
                    filled(first["fox"] + fox_tile(2 * p - 3, 0))
                for e_ in range(2):
                    ins = TS_(qp_bd[:, p % 2, e_, :], q_f[:, p, 0:TP], pair[:, e_ * C:e_ * C + 1], None, ALU.mult)
                link(ins)
                dve.sem_inc(S("qp_ready"), 1)

            queries_of(0)
            for kind, hd in fox_order:
                t = first["fox"] + fox_tile(hd, kind)
                s, st = s_pr[:, hd % 2, :], fstat[:, hd % 2, :]
                if kind == 0:
                    if hd % 2 == 0 and hd // 2 + 1 < HP:
                        queries_of(hd // 2 + 1)
                    if hd >= 2:
                        filled(first["fox"] + fox_tile(hd - 2, 1))
                    filled(t)
                    TT(s, bank(t, 384), fb[:, hd, :], ALU.add).then_inc(dve_freed, 1)
                    dve.wait_ge(dve_freed, freed["d"][t + 1])
                    dve.tensor_reduce(st[:, 0:1], s[:, 0:P], AX.X, ALU.max)
                    link(dve.tensor_reduce(st[:, 1:2], s[:, P:3 * P], AX.X, ALU.max))
                    link(TT(st[:, 2:4], st[:, 0:2], F_tok[:, 0:2, hd], ALU.add))
                    link(TT(st[:, 4:6], F_tok[:, 0:2, hd], st[:, 2:4], ALU.subtract))
                    dve.sem_inc(S("s_ready"), 2)
                elif kind == 1:
                    filled(t)
                    free(CP(pT[:, hd % 2, :], bank(t, 384)))
                else:
                    filled(t)
                    e_ = hd % 2
                    free(CP(oT[e_ * HD:(e_ + 1) * HD, hd // 2, 0:TP], ps[e_ * HD:(e_ + 1) * HD, t % 8, 0:TP]))
                nxt = fox_order[fox_order.index((kind, hd)) + 1] if (kind, hd) != fox_order[-1] else (None, 0)
                if nxt[0] == 1:
                    h1 = nxt[1]
                    s, st = s_pr[:, h1 % 2, :], fstat[:, h1 % 2, :]
                    dve.wait_ge(S("e_ready"), 2 * h1 + 2)
                    link(dve.reciprocal(st[:, 8:10], st[:, 6:8]))
                    TS_(s[:, 0:P], s[:, 0:P], st[:, 8:9], None, ALU.mult).then_inc(S("p_ready"), 1)
                    TS_(s[:, P:3 * P], s[:, P:3 * P], st[:, 9:10], None, ALU.mult).then_inc(S("p_ready"), 1)
            dve.wait_ge(dve_freed, freed["d"][first["fox"] + 3 * H])

            dve.wait_ge(S("o_hi"), 1)
            low(oT_lo[:, :, 0:TP], oT[:, :, 0:TP], oT_hi[:, :, 0:TP]).then_inc(S("o_split"), 1)
            link(dve.memset(mask_new.rearrange("p b k -> p (b k)"), NEG))
            for b in range(BS):
                ins = CP(mask_new[:, b, b * QS:(b + 1) * QS], K("new"))
            link(ins)
            link(TT(mask_new, mask_new, F_row.unsqueeze(1).to_broadcast([P, BS, TS]), ALU.subtract))
            link(dve.memset(q_cur, 0.0))
            base, PER = steps[0], 9
            n_link = [0]

            with dve.Fori(0, BS) as b:
                def lk(ins):
                    n_link[0] += 1
                    ins.then_inc(S("dve_step"), 1)
                    dve.wait_ge(S("dve_step"), b * PER + (base + n_link[0]))

                dve.wait_ge(S("s_done"), b + 1)
                for r in range(2):
                    for e_ in range(2):
                        off = 48 * r + QS * e_
                        TS_(q_cur.rearrange("p (g c) -> p g c", g=4)[:, :, off:off + QS],
                            q_f[:, r:HP:2, bass.ds(b * QS + TP, QS)], pair[:, e_ * C:e_ * C + 1], None, ALU.mult
                            ).then_inc(S("q_cur"), 1)
                for j in range(PAGES):
                    dve.wait_ge(S("k_page_free"), b * PAGES + (j + 5))
                    CP(k_feat[j // 2 % 2][:, 4:8, j % 2 * P:(j % 2 + 1) * P],
                       ps[:, 4 + j % 2 * 2, :].rearrange("p (m t) -> p m t", m=4)).then_inc(S("kT_dve"), 1)
                dve.wait_ge(S("s_done"), b + 2)
                lk(TT(s_new, ps[:, 2, 0:TS], mask_new[:, bass.ds(b, 1), :].rearrange("p b k -> p (b k)"), ALU.add))
                dve.tensor_reduce(sst[:, 0:1], ps[:, 0:2, :].rearrange("p g c -> p (g c)"), AX.X, ALU.max)
                lk(dve.tensor_reduce(sst[:, 1:2], s_new, AX.X, ALU.max))
                lk(TT(sst[:, 2:3], sst[:, 0:1], sst[:, 1:2], ALU.max))
                lk(TT(sst[:, 3:4], sst[:, 2:3], fq_all[:, bass.ds(b, 1)], ALU.add))
                TT(sst[:, 4:5], fq_all[:, bass.ds(b, 1)], sst[:, 3:4], ALU.subtract).then_inc(S("less_max"), 1)
                dve.wait_ge(S("p_turned"), b + 1)
                CP(p_T[:, 4:8, :], ps[:, 1, :].rearrange("p (g c) -> p g c", g=4)).then_inc(S("pT_dve"), 1)
                CP(p_T[0:TS, 8, :], ps[0:TS, 2, P:2 * P]).then_inc(S("pT_dve"), 1)
                lk(TT(sst[:, 8:9], sst[:, 6:7], sst[:, 7:8], ALU.add))
                lk(dve.reciprocal(sst[:, 9:10], sst[:, 8:9]))
                dve.wait_ge(S("v_pages_free"), b + 2)
                lk(STT(o_own, ps[:, 7, 0:256].rearrange("p (g d) -> p g d", g=4), sst[:, 9:10],
                       K("quarter").unsqueeze(2).to_broadcast([P, 4, HD]), ALU.mult, ALU.mult))
                for e_ in range(2):
                    dve.tensor_reduce(o_two[:, e_ * HD:(e_ + 1) * HD], o_own.rearrange("p g d -> p d g"), AX.X,
                                      ALU.add).then_inc(S("o_own"), 1)
                dve.wait_ge(S("o_turned"), b + 1)
                for e_ in range(2):
                    pr = slice(e_ * HD, (e_ + 1) * HD)
                    CP(oT[pr, :, bass.ds(b * QS + TP, QS)],
                       ps[pr, 7, 256:384].rearrange("p (m e q) -> p m e q", m=HP, e=2)[:, :, e_, :]
                       ).then_inc(S("fox_out"), 1)
                for _ in range(PER - n_link[0]):
                    dve.sem_inc(S("dve_step"), 1)
                assert n_link[0] <= PER
            steps[0] = base + PER * BS
            dve.wait_ge(S("o_hi"), 2)
            low(oT_lo[:, :, TP:T], oT[:, :, TP:T], oT_hi[:, :, TP:T]).then_inc(S("o_split"), 1)
            residual("fo")
            ffn(3)
            dve.wait_ge(dve_freed, freed["d"][first["down3"] + DT])
            y_tok = [arena[:, 3 * TW + j * D:3 * TW + (j + 1) * D] for j in range(3)]
            for g, n in ((0, P), (1, P), (2, TS)):
                for j in range(2):
                    t = first["y"] + 2 * g + j
                    filled(t)
                    free(CP(y_tok[g][0:n, j * 512:(j + 1) * 512], bank(t, 512, n)))

        @block.gpsimd
        def _(pool):
            pool.wait_ge(dve_freed, freed["d"][first["shift_out"] + 2])
            rows_sh = arena[0:BS + 1, 8 * TW:8 * TW + D]
            pool.dma_start(O["shift_prompt"].rearrange("n b d -> (n b) d"), rows_sh[0:1, :]).then_inc(S("shift_stored"), 16)
            pool.dma_start(O["shift_sample"].rearrange("n b d -> (n b) d"), rows_sh[1:BS + 1, :]).then_inc(S("shift_stored"), 16)
            pool.wait_ge(S("scan_in"), 1)
            for b in range(BS):
                if b >= 2:
                    pool.wait_ge(tile_done, first["state_in"] + b - 1)
                pool.dma_start(state_in[b % 2][0:HD, :].rearrange("p (g j) -> p g j", g=H),
                               A["state_wkv"][0, b].rearrange("g i j -> i g j")).then_inc(S(f"state_in{b % 2}"), 16)

            def pairs(dst, src, hf, c):
                hs = slice(4 * hf, 4 * hf + 4)
                pool.tensor_tensor(dst[:, hs, :].rearrange("p m (e c) -> p m e c", e=2),
                                   src[:, hs, c * C:(c + 1) * C].unsqueeze(2).to_broadcast([P, 4, 2, C]),
                                   pair.rearrange("p (e c) -> p e c", e=2).unsqueeze(1).to_broadcast([P, 4, 2, C]),
                                   ALU.mult).then_inc(S("bd_ready"), 1)

            for c in range(CHUNKS):
                if c:
                    pool.wait_ge(tile_done, first[f"X{c - 1}"] + 2)
                for hf in range(2):
                    for dst, src in ((A_bd, Af), (B_bd, Bf), (K_bd, Kf), (V_bd, Vf)):
                        pairs(dst, src, hf, c)
                lvs = levels(c)
                for n_lv, lv in enumerate(lvs):
                    for hf in range(2):
                        hs = slice(4 * hf, 4 * hf + 4)
                        if lv == lvs[0]:
                            pool.wait_ge(tile_done, first[f"tok{c}"] + 4)
                            pool.wait_ge(dve_freed, freed["d"][first[f"LT{c}"] + 2])
                        else:
                            pool.wait_ge(tile_done, first[f"Z{c}_{lvs[n_lv - 1]}"] + hf + 1)
                        pool.tensor_tensor(join_bd[:, hs, :], LT_bd[:, hs, :],
                                           K(f"join{lv}").unsqueeze(1).to_broadcast([P, 4, P]), ALU.mult
                                           ).then_inc(S("join_ready"), 1)
                if c == CHUNKS - 2:
                    pool.wait_ge(dve_freed, freed["d"][first["wkv_prompt"] + 2])
                    for e in range(2):
                        pool.dma_start(
                            O["wkv_prompt"][0, 0].rearrange("(m e) i j -> e i m j", e=2)[e],
                            S_bd[e * HD:(e + 1) * HD, :, e * HD:(e + 1) * HD]).then_inc(S("wkv_prompt_out"), 16)
            pool.wait_ge(tile_done, first[f"DDT{CHUNKS - 1}_2"] + 2)
            for p in range(HP):
                if p >= 2:
                    n = p - 2
                    if n % 4 == 3:
                        pool.wait_ge(tile_done, first["own_state"] + n // 4 + 1)
                    else:
                        pool.wait_ge(S("S0_used"), n - n // 4 + 1)
                pool.tensor_tensor(
                    S0_bd[p % 2].rearrange("p m c -> p (m c)").rearrange("p (b e i) -> p b e i", b=BS, e=2),
                    S0[:, :, p, :].unsqueeze(2).to_broadcast([P, BS, 2, C]),
                    pair.rearrange("p (e c) -> p e c", e=2).unsqueeze(1).to_broadcast([P, BS, 2, C]),
                    ALU.mult).then_inc(S("S0_ready"), 1)
            c = CHUNKS - 1
            pool.wait_ge(act_freed, freed["a"][first[f"U{c}"] + 2])
            pool.wait_ge(tile_done, first[f"Y{c}"] + 2)
            pool.tensor_tensor(U_st, X_bd[:, :, 0:C], X_bd[:, :, C:2 * C], ALU.add).then_inc(S("st_ready"), 1)
            pool.tensor_tensor(V_st, V_tok[:, :, 0:C], V_tok[:, :, C:2 * C], ALU.add).then_inc(S("st_ready"), 1)
            pool.wait_ge(S("st_ready"), 2)

            def store_states(p):
                pool.wait_ge(act_freed, freed["a"][first[f"ST{p}"] + 2])
                for e in range(2):
                    pool.dma_start(O["wkv_sample"][0, :, 2 * p + e, :, :].rearrange("b i j -> i b j"),
                                   state_out[p % 2][0:HD, :].rearrange("p (b e j) -> p b e j", b=BS, e=2)[:, :, e, :]
                                   ).then_inc(S(f"state_out{p % 2}"), 16)

            for p in range(HP):
                if p >= 2:
                    pool.wait_ge(tile_done, first[f"SS{p - 2}"] + 1)
                for e, src in enumerate((U_st, V_st)):
                    pool.tensor_tensor(UV[p % 2][:, e, :, :], src[:, p, :].unsqueeze(1).to_broadcast([P, BS, C]),
                                       K("seq").unsqueeze(2).to_broadcast([P, BS, C]), ALU.mult
                                       ).then_inc(S("uv_ready"), 1)
                if p >= 1:
                    store_states(p - 1)
            store_states(HP - 1)
            pool.wait_ge(S("logf_tok_ready"), 1)
            pool.dma_start(O["logf_prompt"][0].rearrange("(g p) h -> p g h", p=P), lf_tok[:, 0:2, :]).then_inc(S("logf_stored"), 16)
            pool.dma_start(O["logf_sample"].rearrange("b t h -> (b t) h"), lf_tok[0:TS, 2, :]).then_inc(S("logf_stored"), 16)
            for name, src in (("k", k_tok), ("v", v_tok)):
                for g in range(3):
                    pool.wait_ge(dve_freed, freed["d"][first[name + "_tok"] + 2 * g + 2])
                    if g < 2:
                        dst = O[name + "_prompt"][0, g * P:(g + 1) * P].rearrange("t h d -> t (h d)")
                    else:
                        dst = O[name + "_sample"].rearrange("b t h d -> (b t) (h d)")
                    pool.dma_start(dst, src[0:P if g < 2 else TS, g, :]).then_inc(S(name + "_stored"), 16)
            pool.wait_ge(tile_done, first["down2"] + DT)
            pool.wait_ge(S("pt_in"), 16)
            with pool.Fori(0, BS) as b:
                for j in range(PAGES):
                    page = pool.value_load(pt_sb[0:1, bass.ds(b * PAGES + j, 1)], min_val=0,
                                           max_val=A["cache_k"].shape[0] - 1)
                    pool.dma_start(lfp[:, bass.ds(b, 1), j, :].rearrange("p b h -> p (b h)"),
                                   A["cache_logf"][bass.ds(page, 1)].rearrange("a t h -> (a t) h")
                                   ).then_inc(S("lfp_in"), 16)
            for g in range(3):
                pool.wait_ge(dve_freed, freed["d"][first["y"] + 2 * g + 2])
                dst = (O["y_prompt"][0, g * P:(g + 1) * P] if g < 2 else O["y_sample"].rearrange("b t d -> (b t) d"))
                pool.dma_start(dst, arena[0:P if g < 2 else TS, 3 * TW + g * D:3 * TW + (g + 1) * D]
                               ).then_inc(S("y_stored"), 16)
            pool.wait_ge(S("shift_stored"), 32)
            pool.wait_ge(S("wkv_prompt_out"), 32)
            pool.wait_ge(S("state_out0"), 16 * HP)
            pool.wait_ge(S("state_out1"), 16 * HP)
            pool.wait_ge(S("logf_stored"), 32)
            pool.wait_ge(S("k_stored"), 48)
            pool.wait_ge(S("v_stored"), 48)
            pool.wait_ge(S("y_stored"), 48)


_INS = ["x_prompt", "x_sample", "cache_k", "cache_v", "cache_logf", "state_wkv", "state_shift", "page_table",
        "ffn_norm", "ffn_w_in", "ffn_w_out", "mix_norm", "rw_mu", "rw_w_rkv", "rw_w0", "rw_w1", "rw_w2",
        "rw_a0", "rw_a1", "rw_a2", "rw_g1", "rw_g2", "rw_k_k", "rw_k_a", "rw_r_k", "rw_lnx_w", "rw_lnx_b",
        "rw_w_o", "kv_norm", "w_kv", "k_norm", "w_f", "b_f", "fox_w_q", "fox_q_norm", "fox_w_o"]
_OUTS = [("y_prompt", (1, TP, D)), ("y_sample", (BS, QS, D)), ("k_prompt", (1, TP, H, HD)),
         ("v_prompt", (1, TP, H, HD)), ("logf_prompt", (1, TP, H)), ("wkv_prompt", (1, 1, H, HD, HD)),
         ("shift_prompt", (1, 1, D)), ("k_sample", (BS, QS, H, HD)), ("v_sample", (BS, QS, H, HD)),
         ("logf_sample", (BS, QS, H)), ("wkv_sample", (1, BS, H, HD, HD)), ("shift_sample", (1, BS, D))]


def kernel(**inputs):
    import concourse.bacc as bacc
    from concourse.bass_utils import run_bass_kernel_spmd

    nc = bacc.Bacc("TRN2", target_bir_lowering=False, num_devices=1)
    arrays, A, O = {}, {}, {}
    given = {name: np.ascontiguousarray(inputs[name]) for name in _INS}
    given["const"] = const_arrays()[1]
    given["head_sel"] = head_selectors()
    for name, a in given.items():
        arrays["in_" + name] = a
        A[name] = nc.dram_tensor("in_" + name, a.shape, mybir.dt.from_np(a.dtype), kind="ExternalInput").ap()
    for name, shape in _OUTS:
        O[name] = nc.dram_tensor("out_" + name, shape, F32, kind="ExternalOutput").ap()
    build(nc, A, O)
    r = run_bass_kernel_spmd(nc, [arrays], core_ids=[0])
    return tuple(r.results[0]["out_" + name] for name, _ in _OUTS)
```

```python
from contextlib import ExitStack

import numpy as np

import concourse.bass as bass
from concourse import mybir

P = 128
D = 1024
DT = D // P
TP, BS, TS = 256, 8, 64
T = TP + TS
QS = TS // BS
H, HD = 16, 64
HP = H // 2
FF = 2816
FT = FF // P
PAST, PAGE = 1024, 128
PAGES = PAST // PAGE
C = 64
CHUNKS = T // C
RMS_EPS, LNX_EPS = 1e-6, 64e-5
SLAB = 2048
SLOTS = 4
NEG = -1e30
DECAY = float(np.exp(-0.5))

F32 = mybir.dt.float32
F32R = mybir.dt.float32r
I32 = mybir.dt.int32
ALU = mybir.AluOpType
ACT = mybir.ActivationFunctionType
AX = mybir.AxisListType

PARAMS = ["ffn_norm", "mix_norm", "rw_mu", "rw_w0", "rw_a0", "rw_k_k", "rw_k_a", "rw_r_k",
          "rw_lnx_w", "rw_lnx_b", "kv_norm"]
PARAM_ROWS = {"ffn_norm": 4, "mix_norm": 2, "rw_mu": 6}


def plan_tiles():
    first, owner = {}, []

    def add(name, n, who="d"):
        first[name] = len(owner)
        owner.extend(who * n if len(who) == 1 else who)

    def ffn(n):
        if n != 2:
            add(f"norm_ffn{n}", 1, "a")
        add(f"up{n}", 2 * FT)
        add(f"down{n}", DT)

    add("x", DT)
    add("params", 2)
    add("shift_in", 1)
    ffn(0)
    add("norm_mix0", 1, "a")
    add("w1", 1, "a")
    add("w2", DT, "a")
    add("a1", 1, "a")
    add("a2", DT, "a")
    add("k", DT)
    add("shift_out", 2)
    add("r", DT)
    add("kk_norm", 1)
    add("v", DT)
    add("kk_rep", DT)
    add("g1", 1, "a")
    add("g2", DT)
    for c in range(CHUNKS):
        last = c == CHUNKS - 1
        add(f"LT{c}", 2)
        add(f"KA{c}", 2)
        add(f"RG{c}", 2)
        add(f"tok{c}", 6, "a")
        add(f"D{c}", 2)
        for lv in levels(c):
            add(f"Z{c}_{lv}", 2, "a")
            if lv != levels(c)[-1]:
                add(f"DD{c}_{lv}", 2)
            add(f"DDT{c}_{lv}", 2)
        if last:
            add("own_state", 2)
        add(f"X{c}", 2, "a")
        add(f"U{c}", 2, "a")
        add(f"Y{c}", 2)
        if not last:
            add(f"S{c}", 2)
            if c == CHUNKS - 2:
                add("wkv_prompt", 2)
            add(f"state_in{c}", 2)
            if c == 1:
                add("bonus", DT)
    for p in range(HP + 1):
        if p < HP:
            add(f"SS{p}", 1)
        if p:
            add(f"ST{p - 1}", 2, "a")
    add("mean", DT)
    add("var", 1, "a")
    add("var_rep", DT)
    add("wo", DT)
    ffn(1)
    add("norm_kv", 1, "a")
    add("kk", DT)
    add("logf", 1)
    add("k_norm", 1, "a")
    add("vv", DT)
    add("k_rep", DT)
    add("logf_tok", 1)
    add("k_tok", 6)
    add("v_tok", 6)
    ffn(2)
    add("norm_mix1", 1, "a")
    add("fk_past", 4)
    add("fq_col", 1)
    add("q", DT)
    add("q_norm", 1, "a")
    add("q_rep", DT)
    add("fox", 3 * H)
    add("fo", DT)
    ffn(3)
    add("y", 6)
    return first, owner


def plan_slabs():
    slabs, first_slab, low_rank, count = [], {}, {}, [0] * SLOTS

    def take(slot, pieces=1):
        count[slot] += 16 * pieces
        return count[slot]

    def dense(name, slots):
        first_slab[name] = len(slabs)
        for slot in slots:
            slabs.append((slot, DT, take(slot)))

    def ffn(n, slot):
        first_slab[f"up{n}"] = len(slabs)
        for j in range(FT + 12):
            slabs.append(((slot + j) % SLOTS, DT if j < FT or (j - FT) % 3 < 2 else FT - 2 * DT,
                          take((slot + j) % SLOTS)))
            if j == FT - 1:
                first_slab[f"down{n}"] = len(slabs)

    ffn(0, 0)
    low_rank[1] = take(2, 4)
    dense("k", [3, 0, 1, 2])
    dense("r", [0, 1, 2, 0])
    dense("v", [1, 2, 0, 1])
    dense("wo", [2, 0, 1, 2])
    ffn(1, 0)
    for name in ("kk", "vv"):
        dense(name, [2, 3, 0, 1])
    ffn(2, 2)
    dense("q", [0, 1, 2, 3])
    dense("fo", [1, 2, 3, 0])
    ffn(3, 1)
    return slabs, first_slab, low_rank


def levels(c):
    return [1, 2, 3, 4, 5] if c < CHUNKS - 1 else [1, 2]


def const_arrays():
    i = np.arange(P)
    head, tok = i // C, i % C
    same = (head[:, None] == head[None, :])
    s, t = tok[:, None], tok[None, :]
    m = {}
    m["ident"] = np.eye(P)
    m["ones"] = np.ones((P, P))
    m["pair"] = same
    for kind, seq in (("p", True), ("s", s // QS == t // QS)):
        m["strict_" + kind] = same & (s < t) & seq
        incl = ((s <= t) & seq)[:, :C]
        m["upto_" + kind] = np.concatenate([incl, incl], 1)
        m["first_" + kind] = same & (s + 1 == t) & (t % 2 == 1) & seq
    for lv in range(1, 6):
        b = 2 ** lv
        m[f"join{lv}"] = same & (s // (2 * b) == t // (2 * b)) & (s // b % 2 == 0) & (t // b % 2 == 1)
    m["later"] = i[:, None] > i[None, :]
    m["seq"] = tok[:, None] // QS == np.arange(BS)[None, :]
    chunk_mask = np.ones((P, T))
    chunk_mask[:, 0:TP:C] = 0
    chunk_mask[:, TP::QS] = 0
    m["chunk"] = chunk_mask
    seq_mask = np.ones((P, T))
    seq_mask[:, 0] = 0
    seq_mask[:, TP::QS] = 0
    m["seqscan"] = seq_mask
    causal = np.where(i[:, None] >= i[None, :], 0, NEG)
    m["causal"] = np.concatenate([causal, np.zeros((P, P)), causal], 1)
    m["new"] = np.where(np.arange(QS)[None, :] <= i[:, None] % QS, 0, NEG)
    m["quarter"] = i[:, None] // QS % 4 == np.arange(4)[None, :]
    m["selcol"] = (i[:, None] == i[None, :] // QS)
    m["qpick"] = (i[:, None] % QS == np.arange(QS)[None, :])
    sums = np.zeros((P, 34))
    sums[:, 2], sums[:, 3] = head == 0, head == 1
    m["sums"] = sums
    for j in range(2):
        m[f"rep{j}"] = i[:, None] % 32 == 2 * j + head[None, :]
    at, out = {}, []
    n = 0
    for name, a in m.items():
        at[name] = (n, n + a.shape[1])
        n += a.shape[1]
        out.append(np.asarray(a, np.float32))
    return at, np.concatenate(out, 1)


def head_selectors():
    return np.repeat(np.eye(H, dtype=np.float32), P, 1)


def build(nc, A, O):
    first, owner = plan_tiles()
    at, const_np = const_arrays()
    N_CONST = const_np.shape[1]
    freed = {"d": [0], "a": [0]}
    for w in owner:
        for e in "da":
            freed[e].append(freed[e][-1] + (w == e))
    row_of, rows = {}, 0
    for name in PARAMS:
        row_of[name] = rows
        rows += PARAM_ROWS.get(name, 1) * DT
    row_of["head_norms"] = rows
    rows += 2
    slabs, first_slab, low_rank = plan_slabs()
    norms = ["ffn0", "mix0", "ffn1", "kv", "mix1", "ffn3"]
    normed = ["ffn0", "mix0", "ffn1", "kv", "ffn2", "mix1", "ffn3"]
    split_norms = ["ffn0", "ffn1", "kv", "ffn2", "mix1", "ffn3"]

    with ExitStack() as ctx:
        def sb(name, shape, dt=F32):
            return ctx.enter_context(nc.sbuf_tensor(name, shape, dt))

        sems = {}

        def S(name):
            if name not in sems:
                sems[name] = ctx.enter_context(nc.semaphore(name))
            return sems[name]

        TW = DT * T
        h_f = sb("h", [P, TW])
        with nc.sbuf_tensor("xn", [P, TW], F32) as xn_f, nc.sbuf_tensor("ring", [P, 3, 2 * SLAB], F32) as ring, \
                nc.sbuf_tensor("arena", [P, 11 * TW], F32) as arena:
            pass
        xn_r, ring_r, arena_r = sb("xn_r", [P, TW], F32R), sb("ring_r", [P, 3, 2 * SLAB], F32R), \
            sb("arena_r", [P, 11 * TW], F32R)
        extra = sb("extra", [P, 2048])
        const = sb("const", [P, N_CONST])
        par = sb("par", [P, 2, P])
        small = sb("small", [P, 800])
        root = sb("root", [P, T])
        rs = sb("rs", [P, T])
        pt_sb = sb("pt_sb", [1, BS * PAGES], I32)
        ps = ctx.enter_context(nc.psum_tensor("ps", [P, 8, 512], F32))

        def feat(x):
            return x.rearrange("p (m t) -> p m t", m=DT)

        h, xn = feat(h_f[:, :]), feat(xn_f[:, :])

        def A_(n):
            return feat(arena[:, n * TW:(n + 1) * TW])

        def AR_(n):
            return feat(arena_r[:, n * TW:(n + 1) * TW])

        def K(name):
            return const[:, at[name][0]:at[name][1]]

        def prm(name, m, row=0):
            r = row_of[name] + row * DT + m
            return par[:, r // P, r % P:r % P + 1]

        ident, ones, pair = K("ident"), K("ones"), K("pair")
        used = [0]

        def sm(n):
            used[0] += n
            assert used[0] <= 800, used
            return small[:, used[0] - n:used[0]]

        eps, eps_ln, b_f = sm(1), sm(1), sm(1)
        omka = sm(DT)
        w_f = sm(DT * H).rearrange("p (k n) -> p k n", k=DT)
        shT = sm(DT * BS).rearrange("p (m b) -> p m b", m=DT)
        shc = sm(DT * (BS + 1)).rearrange("p (m b) -> p m b", m=DT)
        lf_tok = sm(3 * H).rearrange("p (g h) -> p g h", g=3)
        F_tok = sm(3 * H).rearrange("p (g h) -> p g h", g=3)
        F_row = sm(TS)
        fq_all, tmp_fq = sm(BS), sm(TS)
        hn_scale = sm(2)

        o_kT = 2 * FT * T
        o_v, o_xh = o_kT + TW, o_kT + TW + 3 * D
        o_sg, o_slot = o_xh + TW, o_xh + TW + 4 * T
        assert o_slot + 2 * SLAB <= 11 * TW
        hid = arena[:, 0:FT * T].rearrange("p (f t) -> p f t", f=FT)
        hid_lo = arena_r[:, 0:FT * T].rearrange("p (f t) -> p f t", f=FT)
        hid_hi = arena_r[:, FT * T:2 * FT * T].rearrange("p (f t) -> p f t", f=FT)
        sg = arena[:, o_sg:o_sg + 4 * T].rearrange("p (g t) -> p g t", g=4)
        sq = feat(arena[:, o_xh:o_xh + TW])
        xn_hi, xn_lo = feat(arena_r[:, o_xh:o_xh + TW]), feat(xn_r[:, :])

        tile_done = S("tile_done")
        dve_freed = S("dve_freed_bank")
        act_freed = S("act_freed_bank")

        def bank(t, n=512, rows_=P):
            return ps[0:rows_, t % 8, 0:n]

        w_in = A["ffn_w_in"].rearrange("l s k m -> (l s) k m")
        w_out = A["ffn_w_out"].rearrange("l s k m -> (l s) k m")

        def cols(w, k0, k1, c0, n):
            return w[k0 * P:k1 * P, c0:c0 + n].rearrange("(k p) m -> p k m", p=P)

        def slot_(slot, r=False):
            if slot < 3:
                return (ring_r if r else ring)[:, slot, :]
            return (arena_r if r else arena)[:, o_slot:o_slot + 2 * SLAB]

        def slab(slot, k, n=256):
            return slot_(slot)[:, 0:k * n].rearrange("p (k m) -> p k m", k=k)

        def part(s, hi):
            slot, k, _ = slabs[s]
            return slot_(slot, True)[:, hi * SLAB:hi * SLAB + k * 256].rearrange("p (k m) -> p k m", k=k)

        def raw(s):
            return slab(slabs[s][0], slabs[s][1])

        dense = {
            "r": A["rw_w_rkv"][0, 0], "k": A["rw_w_rkv"][0, 1], "v": A["rw_w_rkv"][0, 2],
            "wo": A["rw_w_o"][0], "kk": A["w_kv"][:, 0:D], "vv": A["w_kv"][:, D:2 * D],
            "q": A["fox_w_q"][0], "fo": A["fox_w_o"][0],
        }
        LORA = 2
        wa1 = slot_(LORA)[:, 0:8 * P].rearrange("p (k m) -> p k m", k=DT)
        wa2 = slot_(LORA)[0:HD, SLAB:2 * SLAB]
        g1 = extra[:, 0:8 * P].rearrange("p (k m) -> p k m", k=DT)
        g2 = extra[:, 8 * P:16 * P]

        def buf(j):
            if j < 2:
                x = xn_f[:, j * D:(j + 1) * D]
            elif j < 10:
                x = ring[:, (j - 2) // 4, (j - 2) % 4 * D:(j - 2) % 4 * D + D]
            elif j < 12:
                x = extra[:, (j - 10) * D:(j - 9) * D]
            else:
                x = arena[:, 6 * TW + 4096:6 * TW + 4096 + D]
            return x.rearrange("p (m c) -> p m c", m=HP)

        (A_bd, B_bd, K_bd, V_bd, LT_bd, KA_bd, RG_bd, V_tok, B_tok, K_tok, DT_bd, X_bd, S_bd) = (
            buf(j) for j in range(13))
        join_bd, Z_bd, D_bd = B_bd, K_bd, V_bd
        S0 = arena[:, 6 * TW:6 * TW + 4096].rearrange("p (b m i) -> p b m i", b=BS, m=HP)
        state_in = [slot_(2)[:, SLAB + j * D:SLAB + (j + 1) * D] for j in range(2)]
        XT_bd, Y0 = V_bd, LT_bd.rearrange("p m c -> p (m c)")[:, 0:512].rearrange("p (m c) -> p m c", m=HP)
        U_st = A_bd.rearrange("p m c -> p (m c)")[:, 0:512].rearrange("p (m c) -> p m c", m=HP)
        V_st = A_bd.rearrange("p m c -> p (m c)")[:, 512:1024].rearrange("p (m c) -> p m c", m=HP)
        UV = [x.rearrange("p m c -> p (m c)").rearrange("p (e b i) -> p e b i", e=2, b=BS) for x in (B_bd, K_bd)]
        SF = V_bd.rearrange("p m c -> p (m c)").rearrange("p (e b i) -> p e b i", e=2, b=BS)
        state_out = [x.rearrange("p m c -> p (m c)") for x in (LT_bd, KA_bd)]
        Yf = A_(9)
        own = arena[:, 0:6 * TW].rearrange("p (s r) -> p s r", s=2)
        mix_row = {"r": 0, "k": 1, "v": 2, "w": 3, "a": 4, "g": 5}
        mixes = "wakrvg"
        mix_last = {"w": "w1", "a": "a1", "k": "k", "r": "r", "v": "v", "g": "g1"}
        xs_hi = {"k": AR_(8), "r": AR_(5), "v": AR_(8)}
        Af, Bf, bonus, Rf, Kf, Vf, gf, Ef = A_(0), A_(1), A_(2), A_(3), A_(4), A_(5), A_(8), A_(10)

        kT = feat(arena[:, o_kT:o_kT + TW])
        v_tok = arena[:, o_v:o_v + 3 * D].rearrange("p (g d) -> p g d", g=3)
        k_tok = arena[:, o_kT - 3 * D:o_kT].rearrange("p (g d) -> p g d", g=3)
        o_q = PAGES * D
        q_f = feat(arena[:, o_q:o_q + TW])
        q_sq = feat(arena[:, o_q + TW:o_q + 2 * TW])
        oT, oT_lo, oT_hi = xn, xn_lo, feat(arena_r[:, o_q + TW:o_q + 2 * TW])
        head_sel = arena[0:H, o_xh:o_xh + H * P].rearrange("p (h c) -> p h c", h=H)
        o10 = o_xh + H * 384
        assert o_q + 2 * TW + 3 * 256 <= o_kT and o10 + 1792 <= 11 * TW
        qp_bd = arena[:, o10:o10 + 1024].rearrange("p (j e t) -> p j e t", j=2, e=2)
        s_pr = arena[:, o10 + 1024:o10 + 1792].rearrange("p (j c) -> p j c", j=2)
        o_pT = o_q + 2 * TW
        pT = arena[:, o_pT:o_pT + 768].rearrange("p (j c) -> p j c", j=2)
        fstat = sb("fstat", [P, 2, 10])

        def v_page(j):
            return arena[:, j * D:(j + 1) * D]

        def k_page(j):
            return ring[:, 0, j * D:j * D + D]

        o7 = o_xh
        k_feat = [arena[:, o7 + j * 2048:o7 + (j + 1) * 2048].rearrange("p (m t) -> p m t", m=HP) for j in range(2)]
        p_row = arena[:, o7 + 4096:o7 + 5184]
        p_T = arena[:, o7 + 5184:o7 + 6336].rearrange("p (g c) -> p g c", g=9)
        nfk_rep = arena[:, o7 + 6336:o7 + 7360]
        mask_new = arena[:, o7 + 7360:o7 + 7872].rearrange("p (b k) -> p b k", b=BS)
        o_two = arena[:, o7 + 7872:o7 + 8000]
        o_own = arena[:, o7 + 8000:o7 + 8256].rearrange("p (g d) -> p g d", g=4)
        s_new = arena[:, o_pT:o_pT + 64]
        q_cur = arena[:, o_pT + 64:o_pT + 320]
        sst = arena[:, o_pT + 320:o_pT + 336]
        nfk = extra[:, 640:1664].rearrange("p (b j h) -> p b j h", b=BS, j=PAGES)
        lfp = nfk
        FT_, LF = extra[0:H, 0:T], extra[0:H, T:2 * T]
        lw = [extra[0:H, (2 + j) * T:(3 + j) * T] for j in range(4)]
        nF_dup = extra[0:H, 1664:2048]
        N_PARAM_DMAS = sum(2 if row_of[n] < P < row_of[n] + PARAM_ROWS.get(n, 1) * DT else 1 for n in PARAMS) + 4
        join_count, n_join = {}, 0
        for c in range(CHUNKS):
            for lv in levels(c):
                join_count[c, lv] = n_join
                n_join += 2
        fox_order = [(0, 0)]
        for hd in range(H):
            fox_order += ([(0, hd + 1)] if hd + 1 < H else []) + ([(2, hd - 1)] if hd else []) + [(1, hd)]
        fox_order.append((2, H - 1))

        def fox_tile(hd, kind):
            return fox_order.index((kind, hd))

        block = ctx.enter_context(nc.Block())

        @block.sync
        def _(sp):
            free_at = [None] * SLOTS

            def load(slot, pieces, frees):
                if free_at[slot]:
                    sp.wait_ge(*free_at[slot])
                for dst, src in pieces:
                    sp.dma_start(dst, src).then_inc(S(f"slab{slot}"), 16)
                free_at[slot] = frees

            def free_after(s, sem, value):
                free_at[slabs[s][0]] = (sem, value)

            def load_slab(s, src):
                load(slabs[s][0], [(raw(s), src)], None)

            def load_dense(name):
                for q in range(4):
                    s = first_slab[name] + q
                    load_slab(s, cols(dense[name], 0, DT, 256 * q, 256))
                    free_after(s, tile_done, first[name] + 2 * q + 2)

            def load_ffn(n):
                base, s0 = first[f"up{n}"], first_slab[f"up{n}"]
                w = w_in[n]
                for j in range(4):
                    load_slab(s0 + j, cols(w, 0, DT, j // 2 * 256 + j % 2 * FF, 256))
                with sp.Fori(1, 5) as i:
                    for j in range(4):
                        sp.wait_ge(tile_done, i * 8 + (base - 8 + 2 * j + 2))
                        src = w[:, bass.ds(i * 512 + (j // 2 * 256 + j % 2 * FF), 256)]
                        slot = slabs[s0 + j][0]
                        sp.dma_start(slab(slot, DT), src.rearrange("(k p) m -> p k m", p=P)
                                     ).then_inc(S(f"slab{slot}"), 16)
                for j in range(4):
                    free_after(s0 + j, tile_done, base + 32 + 2 * j + 2)
                for j in range(2):
                    load_slab(s0 + 20 + j, cols(w, 0, DT, 2560 + j * FF, 256))
                    free_after(s0 + 20 + j, tile_done, base + 40 + 2 * j + 2)
                for mp in range(4):
                    for s3 in range(3):
                        s = first_slab[f"down{n}"] + 3 * mp + s3
                        k0, k1 = 8 * s3, min(8 * s3 + 8, FT)
                        load_slab(s, cols(w_out[n], k0, k1, 256 * mp, 256))
                        if s3 < 2:
                            free_after(s, S("down_slab_used"), 8 * n + 2 * mp + s3 + 1)
                        else:
                            free_after(s, tile_done, first[f"down{n}"] + 2 * mp + 2)

            xt = arena[:, 3 * TW:3 * TW + 3 * D].rearrange("p (g d) -> p g d", g=3)
            sp.dma_start(const[:, :], A["const"]).then_inc(S("const_in"), 16)
            for g in range(2):
                sp.dma_start(xt[:, g, :], A["x_prompt"][0, g * P:(g + 1) * P, :]).then_inc(S("x_in"), 16)
            sp.dma_start(xt[0:TS, 2, :], A["x_sample"].rearrange("b t d -> (b t) d")).then_inc(S("x_in"), 16)
            prow = arena[:, 5 * TW:5 * TW + 2 * P].rearrange("p (g d) -> p g d", g=2)
            for name in PARAMS:
                n = PARAM_ROWS.get(name, 1) * DT
                flat = A[name]
                dims = "abc"[:len(flat.shape)]
                if len(dims) > 1:
                    flat = flat.rearrange(" ".join(dims) + " -> (" + " ".join(dims) + ")")
                flat = flat.rearrange("(r c) -> r c", c=P)
                r0 = row_of[name]
                for a, b in ((r0, min(r0 + n, P)), (max(r0, P), r0 + n)):
                    if a < b:
                        sp.dma_start(prow[a % P:a % P + b - a, a // P, :], flat[a - r0:b - r0, :]
                                     ).then_inc(S("param_in"), 16)
            for j, src in enumerate((A["k_norm"], A["fox_q_norm"][0])):
                for e in range(2):
                    r = row_of["head_norms"] + j
                    sp.dma_start(prow[r % P:r % P + 1, 1, e * HD:(e + 1) * HD],
                                 src.rearrange("(a d) -> a d", a=1)).then_inc(S("param_in"), 16)
            sp.dma_start(arena[0:BS, 6 * TW:6 * TW + D], A["state_shift"][0]).then_inc(S("shift_in"), 16)
            sp.dma_start(w_f, A["w_f"].rearrange("(k p) n -> p k n", p=P)).then_inc(S("wf_in"), 16)
            sp.dma_start(b_f[0:H, :], A["b_f"].rearrange("(h a) -> h a", a=1)).then_inc(S("wf_in"), 16)
            sp.dma_start(pt_sb[:, :], A["page_table"].rearrange("(a b) n -> a (b n)", a=1)).then_inc(S("pt_in"), 16)

            load_ffn(0)
            load(LORA, [(wa1[:, :, 0:64], A["rw_w1"][0].rearrange("(k p) m -> p k m", p=P)),
                        (wa1[:, :, 64:128], A["rw_a1"][0].rearrange("(k p) m -> p k m", p=P)),
                        (wa2[:, 0:D], A["rw_w2"][0]), (wa2[:, D:2 * D], A["rw_a2"][0])],
                 (tile_done, first["a2"] + DT))
            sp.dma_start(g1, A["rw_g1"][0].rearrange("(k p) m -> p k m", p=P)).then_inc(S("gate_in"), 16)
            sp.dma_start(g2, A["rw_g2"][0]).then_inc(S("gate_in"), 16)
            for name in "krv":
                load_dense(name)
            load_slab(first_slab["wo"], cols(dense["wo"], 0, DT, 0, 256))
            free_at[0] = free_at[1] = (tile_done, first[f"ST{HP - 1}"] + 2)
            free_at[2] = (tile_done, first["wo"] + 2)
            free_at[3] = (tile_done, first["wo"] + DT)
            for j in range(2):
                sp.wait_ge(S(f"state_out{j}"), 16 * HP)
            for q in range(1, 4):
                s = first_slab["wo"] + q
                load_slab(s, cols(dense["wo"], 0, DT, 256 * q, 256))
                free_after(s, tile_done, first["wo"] + 2 * q + 2)
            load_ffn(1)
            load_dense("kk")
            load_dense("vv")
            load_ffn(2)
            load_dense("q")
            for q in range(2):
                s = first_slab["fo"] + q
                load_slab(s, cols(dense["fo"], 0, DT, 256 * q, 256))
                free_after(s, tile_done, first["fo"] + 2 * q + 2)
            sp.wait_ge(tile_done, first["q"] + DT)
            sp.dma_start(arena[0:H, o_xh:o_xh + H * P], A["head_sel"]).then_inc(S("head_sel_in"), 16)
            sp.wait_ge(S("pt_in"), 16)
            sp.wait_ge(S("page_space"), 1)

            def page_of(b, j):
                return sp.value_load(pt_sb[0:1, bass.ds(b * PAGES + j, 1)], min_val=0,
                                     max_val=A["cache_k"].shape[0] - 1)

            def load_k(b, j, page):
                sp.wait_ge(S("k_page_free"), b * PAGES + (j + 1))
                sp.dma_start(k_page(j % 4), A["cache_k"][bass.ds(page, 1)].rearrange("a t h d -> (a t) (h d)")
                             ).then_inc(S(f"k_page{j % 4}"), 16)

            def load_v(b, j, page):
                sp.wait_ge(S("v_page_free"), b * PAGES + (j + 1))
                sp.dma_start(v_page(j), A["cache_v"][bass.ds(page, 1)].rearrange("a t h d -> (a t) (h d)")
                             ).then_inc(S(f"v_page{j}"), 16)

            def load_sequence(b, last):
                pages = [page_of(b, j) for j in range(PAGES)]
                following = [] if last else [page_of(b + 1, j) for j in range(4)]
                for j in range(4, PAGES):
                    load_k(b, j, pages[j])
                for j in range(PAGES):
                    load_v(b, j, pages[j])
                    if not last and j in (3, 5, 6, 7):
                        k = (3, 5, 6, 7).index(j)
                        load_k(b + 1, k, following[k])

            for j, page in enumerate([page_of(0, j) for j in range(4)]):
                load_k(0, j, page)
            with sp.Fori(0, BS - 1) as b:
                load_sequence(b, False)
            load_sequence(BS - 1, True)
            free_at[0] = free_at[3] = (S("fox_out"), 2 * BS)
            for q in range(2, 4):
                s = first_slab["fo"] + q
                load_slab(s, cols(dense["fo"], 0, DT, 256 * q, 256))
                free_after(s, tile_done, first["fo"] + 2 * q + 2)
            load_ffn(3)
        @block.tensor
        def _(pe):
            def begin(t):
                if t >= 8:
                    who = owner[t - 8]
                    pe.wait_ge({"d": dve_freed, "a": act_freed}[who], freed[who][t - 7])

            def end(mm):
                mm.then_inc(tile_done, 1)

            def split(s):
                pe.wait_ge(S("w_lo"), s + 1)

            def mm3(out, s, k, mt, x_hi, x_lo, first_, last):
                cs = slice(mt * P, (mt + 1) * P)
                pe.matmul(out, part(s, 1)[:, k, cs], x_hi, start=first_, stop=False)
                pe.matmul(out, part(s, 1)[:, k, cs], x_lo, start=False, stop=False)
                return pe.matmul(out, part(s, 0)[:, k, cs], x_hi, start=False, stop=last)

            def dve_done(t):
                pe.wait_ge(dve_freed, freed["d"][t + 1])

            def act_done(t):
                pe.wait_ge(act_freed, freed["a"][t + 1])

            def norm(name):
                i, t = norms.index(name), first["norm_" + name]
                begin(t)
                for k in range(DT):
                    pe.wait_ge(S("sq_ready"), i * DT + k + 1)
                    mm = pe.matmul(bank(t, T), ones, sq[:, k, :], start=(k == 0), stop=(k == DT - 1))
                end(mm)

            def gemm(name, x_hi, x_lo, ready=None):
                for q in range(4):
                    s = first_slab[name] + q
                    split(s)
                    t = first[name] + 2 * q
                    order = [(k, mt) for k in range(DT) for mt in range(2)] if q == 0 else [
                        (k, mt) for mt in range(2) for k in range(DT)]
                    for k, mt in order:
                        if k == 0:
                            begin(t + mt)
                        if ready and q == mt == 0:
                            pe.wait_ge(ready[0], ready[1] + k + 1)
                        mm = mm3(bank(t + mt, T), s, k, mt, x_hi[:, k, :], x_lo[:, k, :], k == 0, k == DT - 1)
                        if k == DT - 1:
                            end(mm)

            def xn_ready(name):
                return S("xn_split"), split_norms.index(name) * DT

            def ffn(n):
                if n != 2:
                    norm(f"ffn{n}")
                base, s0 = first[f"up{n}"], first_slab[f"up{n}"]
                d0 = freed["d"][base]
                pe.wait_ge(act_freed, freed["a"][base])
                pe.wait_ge(dve_freed, d0)
                xr = xn_ready(f"ffn{n}")

                def up(j, k, mt):
                    mm = mm3(ps[:, (base + 2 * j + mt) % 8, 0:T], s0 + j % 4, k, mt, xn_hi[:, k, :], xn_lo[:, k, :],
                             k == 0, k == DT - 1)
                    if k == DT - 1:
                        end(mm)

                with pe.Fori(0, 5) as i:
                    for j in range(4):
                        pe.wait_ge(S("w_lo"), i * 4 + (s0 + j + 1))
                        order = [(k, mt) for k in range(DT) for mt in range(2)] if j == 0 else [
                            (k, mt) for mt in range(2) for k in range(DT)]
                        for k, mt in order:
                            if k == 0:
                                pe.wait_ge(dve_freed, i * 8 + (d0 + 2 * j + mt - 7))
                            if j == mt == 0:
                                pe.wait_ge(xr[0], xr[1] + k + 1)
                            up(j, k, mt)
                for j in (20, 21):
                    split(s0 + j)
                    for mt in range(2):
                        begin(base + 2 * j + mt)
                        for k in range(DT):
                            up(j, k, mt)
                down = first[f"down{n}"]
                for mp in range(4):
                    for s3 in range(3):
                        s = first_slab[f"down{n}"] + 3 * mp + s3
                        k0, k1 = 8 * s3, min(8 * s3 + 8, FT)
                        split(s)
                        for mt in range(2):
                            t = down + 2 * mp + mt
                            if s3 == 0:
                                begin(t)
                            for k in range(k0, k1):
                                if mp == mt == 0:
                                    pe.wait_ge(S("hid_split"), FT * n + k + 1)
                                mm = mm3(bank(t, T), s, k - k0, mt, hid_hi[:, k, :], hid_lo[:, k, :],
                                         k == 0, k == FT - 1)
                            if s3 == 2:
                                end(mm)
                        if s3 < 2:
                            mm.then_inc(S("down_slab_used"), 1)

            prow = arena[:, 5 * TW:5 * TW + 2 * P].rearrange("p (g d) -> p g d", g=2)
            xt = arena[:, 3 * TW:3 * TW + 3 * D].rearrange("p (g d) -> p g d", g=3)
            pe.sem_inc(S("k_page_free"), 4)
            pe.sem_inc(S("v_page_free"), PAGES)
            pe.sem_inc(S("kT_act"), 2)
            pe.sem_inc(S("kT_dve"), 2)
            pe.sem_inc(S("s_done"), 1)
            pe.wait_ge(S("const_in"), 16)
            pe.wait_ge(S("x_in"), 48)
            for m in range(DT):
                t = first["x"] + m
                begin(t)
                for g, n in ((0, P), (1, P), (2, TS)):
                    mm = pe.transpose(ps[:, t % 8, g * P:g * P + n], xt[0:n, g, m * P:(m + 1) * P],
                                      ident[0:n, 0:n])
                end(mm)
            pe.wait_ge(S("param_in"), 16 * N_PARAM_DMAS)
            t = first["params"]
            begin(t)
            end(pe.transpose(bank(t, P), prow[:, 0, :], ident))
            begin(t + 1)
            end(pe.transpose(bank(t + 1, rows - P), prow[0:rows - P, 1, :], ident[0:rows - P, 0:rows - P]))
            pe.wait_ge(S("shift_in"), 16)
            t = first["shift_in"]
            begin(t)
            for m in range(DT):
                mm = pe.transpose(ps[:, t % 8, m * BS:(m + 1) * BS],
                                  arena[0:BS, 6 * TW + m * P:6 * TW + (m + 1) * P], ident[0:BS, 0:BS])
            end(mm)

            ffn(0)
            norm("mix0")

            def low_rank_vector(name, w1, n):
                t = first[name + "1"]
                begin(t)
                j = mixes.index(name)
                for k in range(DT):
                    pe.wait_ge(S("xs_raw"), j * DT + k + 1)
                    mm = pe.matmul(ps[0:n, t % 8, 0:T], w1[:, k, :], A_(1 + j % 2)[:, k, :],
                                   start=(k == 0), stop=(k == DT - 1))
                end(mm)

            def low_rank_out(name, w2, vec):
                act_done(first[name + "1"])
                for m in range(DT):
                    t = first[name + "2"] + m
                    begin(t)
                    end(pe.matmul(bank(t, T), w2[:, m * P:(m + 1) * P], vec, start=True, stop=True))

            def mixed_gemm(name):
                gemm(name, xs_hi[name], AR_(1 + mixes.index(name) % 2), (S("xs_split"), "krv".index(name) * DT))

            pe.wait_ge(S(f"slab{LORA}"), low_rank[1])
            low_rank_vector("w", wa1[:, :, 0:64], 64)
            low_rank_out("w", wa2[:, 0:D], root[0:64, :])
            low_rank_vector("a", wa1[:, :, 64:128], 64)
            low_rank_out("a", wa2[:, D:2 * D], rs[0:64, :])
            mixed_gemm("k")
            pe.wait_ge(S("shift_cols"), 1)
            for j in range(2):
                t = first["shift_out"] + j
                begin(t)
                for m in range(4):
                    mm = pe.transpose(ps[0:BS + 1, t % 8, m * P:(m + 1) * P], shc[:, 4 * j + m, :], ident)
                end(mm)
            mixed_gemm("r")

            def head_sums(name, src, ready):
                for m in range(DT):
                    t = first[name] + m
                    begin(t)
                    pe.wait_ge(ready, m + 1)
                    end(pe.matmul(bank(t, T), pair, src[:, m, :], start=True, stop=True))

            def head_totals(name, src, ready):
                t = first[name]
                begin(t)
                for m in range(DT):
                    pe.wait_ge(ready, m + 1)
                    g, c0 = m % 4 * 32, 2 - m // 4 * 2
                    mm = pe.matmul(ps[g:g + 32, t % 8, 0:T], K("sums")[:, c0:c0 + 32], src[:, m, :],
                                   start=(m < 4), stop=(m >= 4))
                end(mm)

            rep_count = [0]

            def head_rep(name, rn):
                rep_count[0] += 1
                pe.wait_ge(S("rn_ready"), rep_count[0])
                for m in range(DT):
                    t = first[name] + m
                    begin(t)
                    g = m % 4 * 32
                    end(pe.matmul(bank(t, T), K(f"rep{m // 4}")[g:g + 32, :], rn[g:g + 32, :], start=True, stop=True))

            head_totals("kk_norm", A_(10), S("kk_sq"))
            mixed_gemm("v")
            head_rep("kk_rep", rs[:, :])
            pe.wait_ge(S("gate_in"), 32)
            low_rank_vector("g", g1, P)
            low_rank_out("g", g2, root[:, :])

            def states_in(c):
                for b in (2 * c, 2 * c + 1):
                    t = first[f"state_in{c}"] + b % 2
                    begin(t)
                    pe.wait_ge(S(f"state_in{b % 2}"), 16 * (b // 2 + 1))
                    for p in range(HP):
                        mm = pe.transpose(ps[:, t % 8, p * HD:(p + 1) * HD],
                                          state_in[b % 2][0:HD, p * P:(p + 1) * P], ident[0:HD, 0:HD])
                    end(mm)

            def halves(name, body, *waits):
                for hf in range(2):
                    t = first[name] + hf
                    begin(t)
                    for w in waits:
                        w(hf)
                    for q in range(4):
                        mm = body(4 * hf + q, t % 8, q)
                    end(mm)

            def mmul(out, lhsT, rhs, start=True, stop=True):
                return pe.matmul(out, lhsT, rhs, start=start, stop=stop)

            for c in range(CHUNKS):
                sample = c == CHUNKS - 1

                def R_c(p):
                    return Rf[:, p, c * C:(c + 1) * C]

                def o(b_, q, n=P, off=0):
                    return ps[:, b_, q * P + off:q * P + off + n]

                halves(f"LT{c}", lambda p, b_, q: mmul(o(b_, q), B_bd[:, p, :], A_bd[:, p, :]),
                       lambda hf: pe.wait_ge(S("A_ready"), 2 * c + hf + 1),
                       lambda hf: pe.wait_ge(S("bd_ready"), 6 * c + hf + 1))
                halves(f"KA{c}", lambda p, b_, q: mmul(o(b_, q), K_bd[:, p, :], A_bd[:, p, :]),
                       lambda hf: pe.wait_ge(S("bd_ready"), 6 * c + 2 + hf + 1))

                def grams(p, b_, q):
                    mmul(o(b_, q, C), B_bd[:, p, :], R_c(p))
                    return mmul(o(b_, q, C, C), K_bd[:, p, :], R_c(p))
                halves(f"RG{c}", grams)
                for j, src in enumerate((V_bd, B_bd, K_bd)):
                    for hf in range(2):
                        t = first[f"tok{c}"] + 2 * j + hf
                        begin(t)
                        if j == 0:
                            pe.wait_ge(S("bd_ready"), 6 * c + 4 + hf + 1)
                        for q in range(4):
                            mm = pe.transpose(o(t % 8, q), src[:, 4 * hf + q, :], ident)
                        end(mm)
                halves(f"D{c}", lambda p, b_, q: pe.transpose(o(b_, q), DT_bd[:, p, :], ident),
                       lambda hf: pe.wait_ge(S("DT_ready"), 2 * c + hf + 1))
                lvs = levels(c)
                for n_lv, lv in enumerate(lvs):
                    prev = f"D{c}" if lv == lvs[0] else f"DD{c}_{lvs[n_lv - 1]}"
                    halves(f"Z{c}_{lv}", lambda p, b_, q: mmul(o(b_, q), join_bd[:, p, :], D_bd[:, p, :]),
                           lambda hf: pe.wait_ge(S("join_ready"), join_count[c, lv] + hf + 1),
                           lambda hf: dve_done(first[prev] + hf))
                    if lv != lvs[0]:
                        dve_done(first[f"DDT{c}_{lvs[n_lv - 1]}"] + 1)
                    if lv != lvs[-1]:
                        halves(f"DD{c}_{lv}", lambda p, b_, q: mmul(o(b_, q), DT_bd[:, p, :], Z_bd[:, p, :]),
                               lambda hf: act_done(first[f"Z{c}_{lv}"] + hf))
                    halves(f"DDT{c}_{lv}", lambda p, b_, q: mmul(o(b_, q), Z_bd[:, p, :], DT_bd[:, p, :]),
                           lambda hf: act_done(first[f"Z{c}_{lv}"] + hf))
                if sample:
                    for hf in range(2):
                        t = first["own_state"] + hf
                        begin(t)
                        for q in range(4):
                            p = 4 * hf + q
                            for b in range(BS):
                                cc = p * T + TP + b * QS
                                for e in range(2):
                                    pr = slice(e * HD, (e + 1) * HD)
                                    out = ps[pr, t % 8, q * P:(q + 1) * P].rearrange("p (s c) -> p s c", s=2)
                                    mm = mmul(out[:, :, b * QS:(b + 1) * QS], S0[pr, b, p, :],
                                              own[pr, :, cc:cc + QS])
                        end(mm)

                def solve_rhs(p, b_, q):
                    if c > 0:
                        mmul(o(b_, q), XT_bd[:, p, :] if sample else A_bd[:, p, :],
                             ident if sample else S_bd[:, p, :], True, False)
                    return mmul(o(b_, q), KA_bd[:, p, :], V_tok[:, p, :], c == 0, True)
                halves(f"X{c}", solve_rhs,
                       lambda hf: act_done(first[f"tok{c}"] + 1),
                       lambda hf: dve_done(first["own_state"] + hf if sample else
                                           first[f"S{c - 1}"] + hf if c else first[f"KA{c}"] + hf))
                halves(f"U{c}", lambda p, b_, q: mmul(o(b_, q), DT_bd[:, p, :], X_bd[:, p, :]),
                       lambda hf: act_done(first[f"X{c}"] + hf),
                       lambda hf: dve_done(first[f"DDT{c}_{lvs[-1]}"] + hf))

                def outputs(p, b_, q):
                    if c > 0 and not sample:
                        mmul(o(b_, q, C), S_bd[:, p, :], R_c(p), True, False)
                    mmul(o(b_, q, C), X_bd[:, p, :], RG_bd[:, p, 0:C], c == 0 or sample, False)
                    return mmul(o(b_, q, C), V_tok[:, p, :], RG_bd[:, p, C:2 * C], False, True)
                halves(f"Y{c}", outputs, lambda hf: act_done(first[f"U{c}"] + hf))
                if not sample:
                    def states(p, b_, q):
                        mmul(o(b_, q), B_tok[:, p, :], X_bd[:, p, :], True, False)
                        return mmul(o(b_, q), K_tok[:, p, :], V_tok[:, p, :], False, True)
                    halves(f"S{c}", states)
                    if c == CHUNKS - 2:
                        halves("wkv_prompt", lambda p, b_, q: pe.transpose(o(b_, q), S_bd[:, p, :], ident),
                               lambda hf: dve_done(first[f"S{c}"] + hf))
                    states_in(c)
                    if c == 1:
                        head_sums("bonus", bonus, S("rk_ready"))
            for p in range(HP + 1):
                if p < HP:
                    t = first[f"SS{p}"]
                    begin(t)
                    pe.wait_ge(S("U_masked"), p + 1)
                    pe.wait_ge(S("V_masked"), p + 1)
                    mmul(bank(t), B_tok[:, p, :], UV[p % 2][:, 0, :, :], True, False)
                    end(mmul(bank(t), K_tok[:, p, :], UV[p % 2][:, 1, :, :], False, True))
                if p:
                    dve_done(first[f"SS{p - 1}"])
                    for j in range(2):
                        t = first[f"ST{p - 1}"] + j
                        begin(t)
                        for q in range(4):
                            mm = pe.transpose(ps[0:HD, t % 8, q * P:(q + 1) * P], SF[:, (p - 1) % 2, 4 * j + q, :],
                                              ident)
                        end(mm)

            head_sums("mean", Yf, S("y_ready"))
            head_totals("var", A_(0), S("y_sq"))
            head_rep("var_rep", rs[:, :])
            gemm("wo", AR_(3), AR_(9), (S("wo_split"), 0))
            ffn(1)

            norm("kv")
            gemm("kk", xn_hi, xn_lo, xn_ready("kv"))
            t = first["logf"]
            begin(t)
            pe.wait_ge(S("wf_in"), 32)
            for k in range(DT):
                mmul(ps[0:H, t % 8, 0:T], w_f[:, k, :], xn_hi[:, k, :].bitcast(F32), k == 0, False)
                mm = mmul(ps[0:H, t % 8, 0:T], w_f[:, k, :], xn_lo[:, k, :].bitcast(F32), False, k == DT - 1)
            end(mm)
            head_totals("k_norm", A_(1), S("k_sq"))
            gemm("vv", xn_hi, xn_lo, xn_ready("kv"))
            head_rep("k_rep", sg[:, 1, :])
            t = first["logf_tok"]
            begin(t)
            pe.wait_ge(S("logf_ready"), 2)
            for e, src in enumerate((LF, FT_)):
                for g, n in ((0, P), (1, P), (2, TS)):
                    mm = pe.transpose(ps[0:n, t % 8, (3 * e + g) * H:(3 * e + g + 1) * H],
                                      src[:, g * P:g * P + n], ident[0:H, 0:H])
            end(mm)

            def to_tokens(name, src, ready):
                for g, n in ((0, P), (1, P), (2, TS)):
                    for j in range(2):
                        t = first[name] + 2 * g + j
                        begin(t)
                        for m in range(4):
                            if g == 0:
                                ready(4 * j + m)
                            mm = pe.transpose(ps[0:n, t % 8, m * P:(m + 1) * P],
                                              src[:, 4 * j + m, g * P:g * P + n], ident)
                        end(mm)

            to_tokens("k_tok", kT, lambda m: pe.wait_ge(S("k_ready"), m + 1))
            to_tokens("v_tok", A_(0), lambda m: dve_done(first["vv"] + 7))
            ffn(2)

            norm("mix1")
            pe.wait_ge(S("lfp_in"), 16 * BS * PAGES)
            for j in range(4):
                t = first["fk_past"] + j
                begin(t)
                end(mmul(bank(t), K("later") if j < 2 else ones,
                         lfp.rearrange("p b j h -> p (b j h)")[:, j % 2 * 512:j % 2 * 512 + 512]))
            t = first["fq_col"]
            begin(t)
            end(mmul(bank(t, TS), K("selcol")[0:H, :], FT_[:, TP:T]))
            gemm("q", xn_hi, xn_lo, xn_ready("mix1"))
            head_totals("q_norm", q_sq, S("q_sq"))
            head_rep("q_rep", sg[:, 1, :])
            pe.wait_ge(S("head_sel_in"), 16)
            pe.wait_ge(S("nF_ready"), 1)

            def scores(hd):
                t = first["fox"] + fox_tile(hd, 0)
                begin(t)
                pe.wait_ge(S("qp_ready"), hd // 2 + 1)
                qp = qp_bd[:, hd // 2 % 2, hd % 2, :]
                pe.matmul(bank(t, 384), head_sel[:, hd, :], nF_dup, start=True, stop=False, skip_group_check=True)
                pe.matmul(ps[:, t % 8, 0:P], qp[:, 0:P], kT[:, hd // 2, 0:P], start=False, stop=False,
                          skip_group_check=True)
                end(pe.matmul(ps[:, t % 8, P:3 * P], qp[:, P:2 * P], kT[:, hd // 2, 0:2 * P], start=False, stop=True,
                              skip_group_check=True))

            def turn(hd):
                t = first["fox"] + fox_tile(hd, 1)
                begin(t)
                pe.wait_ge(S("p_ready"), 2 * hd + 2)
                for j in range(3):
                    mm = pe.transpose(ps[:, t % 8, j * P:(j + 1) * P], s_pr[:, hd % 2, j * P:(j + 1) * P], ident)
                end(mm)

            def values(hd):
                t = first["fox"] + fox_tile(hd, 2)
                begin(t)
                dve_done(first["fox"] + fox_tile(hd, 1))
                vc = slice(hd // 2 * P, (hd // 2 + 1) * P)
                mmul(ps[:, t % 8, 0:P], v_tok[:, 0, vc], pT[:, hd % 2, 0:P])
                mmul(ps[:, t % 8, P:2 * P], v_tok[:, 0, vc], pT[:, hd % 2, P:2 * P], True, False)
                end(mmul(ps[:, t % 8, P:2 * P], v_tok[:, 1, vc], pT[:, hd % 2, 2 * P:3 * P], False, True))

            for kind, hd in fox_order:
                (scores, turn, values)[kind](hd)

            def unit_scores(b, u):
                pe.wait_ge(S("kT_act"), b * PAGES + (2 * u + 4))
                pe.wait_ge(S("kT_dve"), b * PAGES + (2 * u + 4))
                bk, c0 = u // 2, u % 2 * 256
                for j in range(2):
                    pe.matmul(ps[:, bk, c0 + j * P:c0 + (j + 1) * P],
                              nfk_rep[:, (2 * u + j) * P:(2 * u + j + 1) * P], ident,
                              start=(j == 0), stop=False, skip_group_check=True)
                for r in range(2):
                    for g in range(4):
                        mm = pe.matmul(ps[32 * g:32 * g + 32, bk, c0:c0 + 256],
                                       q_cur[:, (2 * g + r) * 32:(2 * g + r + 1) * 32],
                                       k_feat[u % 2][:, 2 * g + r, :],
                                       start=False, stop=(r == 1), skip_group_check=True)
                return mm

            def turn_page(b, j):
                kb = 3 + j % 2 * 2
                pe.wait_ge(S(f"k_page{j % 4}"), b * 32 + (16 * (j // 4 + 1)))
                pe.wait_ge(S("kT_act"), b * PAGES + (j + 1))
                pe.wait_ge(S("kT_dve"), b * PAGES + (j + 1))
                for m in range(DT):
                    mm = pe.transpose(ps[:, kb + m // 4, m % 4 * P:(m % 4 + 1) * P],
                                      k_page(j % 4)[:, m * P:(m + 1) * P], ident)
                mm.then_inc(S("k_page_free"), 1)

            def sequence(b, last):
                pe.wait_ge(S("q_cur"), b * 4 + 4)
                pe.wait_ge(S("nfk_rep"), b + 1)
                unit_scores(b, 0)
                turn_page(b, 4)
                turn_page(b, 5)
                unit_scores(b, 1).then_inc(S("half_scored"), 1)
                turn_page(b, 6)
                turn_page(b, 7)
                unit_scores(b, 2)
                unit_scores(b, 3)
                for r in range(2):
                    for g in range(4):
                        mm = mmul(ps[32 * g:32 * g + 32, 2, 0:TS], q_cur[:, (2 * g + r) * 32:(2 * g + r + 1) * 32],
                                  kT[:, 2 * g + r, TP:T], r == 0, r == 1)
                mm.then_inc(S("s_done"), 1)
                if not last:
                    turn_page(b + 1, 0)
                    turn_page(b + 1, 1)
                for j in range(PAGES):
                    if j % 4 == 0:
                        pe.wait_ge(S("p_row"), b * 3 + (2 * (j // 4) + 1))
                    pe.transpose(ps[:, j // 4, j % 4 * P:(j % 4 + 1) * P], p_row[:, j * P:(j + 1) * P], ident)
                pe.transpose(ps[0:TS, 2, P:2 * P], p_row[:, PAST:PAST + TS], ident).then_inc(S("p_turned"), 1)
                if not last:
                    turn_page(b + 1, 2)
                pe.wait_ge(S("pT_act"), b + 1)
                pe.wait_ge(S("pT_dve"), b * 2 + 2)
                for j in range(PAGES + 1):
                    if j < PAGES:
                        pe.wait_ge(S(f"v_page{j}"), b * 16 + 16)
                    for g in range(4):
                        v = v_page(j) if j < PAGES else v_tok[0:TS, 2, :]
                        mm = mmul(ps[32 * g:32 * g + 32, 7, 0:256], p_T[0:v.shape[0], j, 32 * g:32 * g + 32],
                                  v[:, 256 * g:256 * g + 256], j == 0, j == PAGES)
                    mm.then_inc(S("v_page_free") if j < PAGES else S("outputs_done"), 1)
                if not last:
                    turn_page(b + 1, 3)
                pe.wait_ge(S("o_own"), b * 2 + 2)
                pe.transpose(ps[:, 7, 256:384], o_two, ident).then_inc(S("o_turned"), 1)

            dve_done(first["fox"] + 3 * H - 1)
            for j in range(4):
                turn_page(0, j)
            with pe.Fori(0, BS - 1) as b:
                sequence(b, False)
            sequence(BS - 1, True)
            pe.wait_ge(S("o_split"), 2)
            gemm("fo", oT_hi, oT_lo)
            ffn(3)
            to_tokens("y", h, lambda m: dve_done(first["down3"] + m))
        @block.scalar
        def _(act):
            def filled(t):
                act.wait_ge(tile_done, t + 1)

            def hi(s):
                slot, k, value = slabs[s]
                act.wait_ge(S(f"slab{slot}"), value)
                act.activation(part(s, 1), raw(s), ACT.Copy).then_inc(S("w_hi"), 1)

            def square(src, m):
                act.wait_ge(dve_freed, freed["d"][first[src] + m + 1])
                act.activation(sq[:, m, :], h[:, m, :], ACT.Square).then_inc(S("sq_ready"), 1)

            def root_mean(name):
                i, t = norms.index(name), first["norm_" + name]
                filled(t)
                if i:
                    act.wait_ge(S("rs_ready"), i)
                act.activation(root[:, :], bank(t, T), ACT.Sqrt, bias=eps, scale=1.0 / D).then_inc(act_freed, 1)

            def xn_high(name):
                for m in range(DT):
                    act.wait_ge(S("xn_raw"), normed.index(name) * DT + m + 1)
                    act.activation(xn_hi[:, m, :], xn[:, m, :], ACT.Copy).then_inc(S("xn_hi"), 1)

            def gemm(name, ahead=True, norm_next=False):
                for q in range(4):
                    if ahead:
                        hi(first_slab[name] + q + 2)
                    if norm_next:
                        square(name, 2 * q)
                        square(name, 2 * q + 1)

            def ffn(n):
                if n != 2:
                    root_mean(f"ffn{n}")
                xn_high(f"ffn{n}")
                base, s0 = first[f"up{n}"], first_slab[f"up{n}"]
                d0 = freed["d"][base]
                if n == 2:
                    act.wait_ge(S("k_stored"), 48)
                with act.Fori(0, 5) as i:
                    for j in range(4):
                        slot, _, value = slabs[s0 + j + 2]
                        act.wait_ge(S(f"slab{slot}"), i * 16 + value)
                        act.activation(part(s0 + j + 2, 1), raw(s0 + j + 2), ACT.Copy).then_inc(S("w_hi"), 1)
                        for mt in range(2):
                            if j % 2 == 0:
                                act.wait_ge(tile_done, i * 8 + (base + 2 * j + mt + 1))
                                act.activation(sg[:, j + mt, :], ps[:, (base + 2 * j + mt) % 8, 0:T], ACT.Silu
                                               ).then_inc(S("silu_ready"), 1)
                            else:
                                act.wait_ge(dve_freed, i * 8 + (d0 + 2 * j - 2 + (4 if mt else 1)))
                                f = 2 * (j // 2) + mt
                                act.activation(hid_hi[:, bass.ds(i * 4 + f, 1), :], hid[:, bass.ds(i * 4 + f, 1), :],
                                               ACT.Copy).then_inc(S("hid_hi"), 1)
                for j in range(2):
                    hi(s0 + 22 + j)
                    for mt in range(2):
                        if j == 0:
                            filled(base + 40 + mt)
                            act.activation(sg[:, mt, :], bank(base + 40 + mt, T), ACT.Silu).then_inc(S("silu_ready"), 1)
                        else:
                            act.wait_ge(dve_freed, d0 + 40 + (4 if mt else 1))
                            act.activation(hid_hi[:, 20 + mt, :], hid[:, 20 + mt, :], ACT.Copy
                                           ).then_inc(S("hid_hi"), 1)
                for mp in range(4):
                    for s3 in range(3):
                        s = first_slab[f"down{n}"] + 3 * mp + s3 + 2
                        if s < len(slabs):
                            hi(s)
                    if n < 3:
                        square(f"down{n}", 2 * mp)
                        square(f"down{n}", 2 * mp + 1)

            act.wait_ge(S("eps_ready"), 2)
            for m in range(DT):
                square("x", m)
            hi(0)
            hi(1)
            ffn(0)
            root_mean("mix0")
            def sigmoids(name, out, bias):
                for m in range(DT):
                    filled(first[name + "2"] + m)
                    act.activation(out[:, m, :], bank(first[name + "2"] + m, T), ACT.Sigmoid,
                                   bias=prm(bias, m)).then_inc(act_freed, 1)

            def high_inputs(name):
                j = mixes.index(name)
                for m in range(DT):
                    act.wait_ge(S("xs_raw"), j * DT + m + 1)
                    act.activation(xs_hi[name][:, m, :], A_(1 + j % 2)[:, m, :], ACT.Copy).then_inc(S("xs_hi"), 1)

            filled(first["w1"])
            act.wait_ge(S("rs_ready"), 2)
            act.activation(root[0:HD, :], bank(first["w1"], T, HD), ACT.Tanh).then_inc(act_freed, 1)
            sigmoids("w", A_(6), "rw_w0")
            act.wait_ge(S("xn_raw"), 2 * DT)
            filled(first["a1"])
            act.activation(rs[0:HD, :], bank(first["a1"], T, HD), ACT.Copy).then_inc(act_freed, 1)
            sigmoids("a", A_(7), "rw_a0")
            high_inputs("k")
            high_inputs("r")
            hi(first_slab["k"] + 2)
            hi(first_slab["k"] + 3)
            hi(first_slab["k"] + 4)
            hi(first_slab["k"] + 5)
            high_inputs("v")
            for m in range(DT):
                act.wait_ge(dve_freed, freed["d"][first["k"] + m + 1])
                act.wait_ge(S("k_scaled"), m + 1)
                act.activation(A_(10)[:, m, :], A_(10)[:, m, :], ACT.Square).then_inc(S("kk_sq"), 1)
            gemm("r")
            filled(first["kk_norm"])
            act.wait_ge(dve_freed, freed["d"][first["kk_norm"] + 1])
            act.activation(root[:, :], rs[:, :], ACT.Sqrt).then_inc(S("kk_root"), 1)
            act.wait_ge(S("decay_sums"), 1)
            act.activation(A_(10), A_(9), ACT.Exp, scale=-DECAY).then_inc(S("decays"), 1)
            hi(first_slab["v"] + 2)
            act.activation(A_(6), A_(6), ACT.Exp, scale=-DECAY).then_inc(S("decays"), 1)
            hi(first_slab["v"] + 3)
            act.wait_ge(S("decays"), 2)
            act.activation(A_(9), A_(9), ACT.Exp, scale=DECAY).then_inc(S("decays"), 1)
            filled(first["g1"])
            act.activation(root[:, :], bank(first["g1"], T), ACT.Sigmoid).then_inc(act_freed, 1)

            def copy_halves(name, dst):
                for hf in range(2):
                    filled(first[name] + hf)
                    act.activation(dst[:, 4 * hf:4 * hf + 4, :], bank(first[name] + hf), ACT.Copy
                                   ).then_inc(act_freed, 1)

            for c in range(CHUNKS):
                for j, dst in enumerate((V_tok, B_tok, K_tok)):
                    for hf in range(2):
                        t = first[f"tok{c}"] + 2 * j + hf
                        filled(t)
                        act.activation(dst[:, 4 * hf:4 * hf + 4, :], bank(t), ACT.Copy).then_inc(act_freed, 1)
                for lv in levels(c):
                    copy_halves(f"Z{c}_{lv}", Z_bd)
                copy_halves(f"X{c}", X_bd)
                copy_halves(f"U{c}", X_bd)
            for p in range(HP):
                if p >= 2:
                    act.wait_ge(S(f"state_out{p % 2}"), 32 * (p // 2))
                for j in range(2):
                    filled(first[f"ST{p}"] + j)
                    act.activation(state_out[p % 2][0:HD, j * 512:(j + 1) * 512], bank(first[f"ST{p}"] + j, 512, HD),
                                   ACT.Copy).then_inc(act_freed, 1)
            act.wait_ge(S("wkv_prompt_out"), 32)
            hi(first_slab["wo"])
            for m in range(DT):
                act.wait_ge(dve_freed, freed["d"][first["mean"] + m + 1])
                act.activation(A_(0)[:, m, :], Yf[:, m, :], ACT.Square).then_inc(S("y_sq"), 1)
            filled(first["var"])
            act.activation(root[:, :], bank(first["var"], T), ACT.Sqrt, bias=eps_ln, scale=1.0 / HD
                           ).then_inc(act_freed, 1)
            hi(first_slab["wo"] + 1)
            for m in range(DT):
                act.wait_ge(S("wo_raw"), m + 1)
                act.activation(AR_(3)[:, m, :], Yf[:, m, :], ACT.Copy).then_inc(S("wo_hi"), 1)
            act.wait_ge(S("wkv_prompt_out"), 32)
            gemm("wo", norm_next=True)
            ffn(1)
            root_mean("kv")
            xn_high("kv")

            def head_roots(name, src_name, src, dst, sq_sem):
                for q in range(4):
                    hi(first_slab[src_name] + q + 2)
                    for m in (2 * q, 2 * q + 1):
                        act.wait_ge(dve_freed, freed["d"][first[src_name] + m + 1])
                        act.activation(dst[:, m, :], src[:, m, :], ACT.Square).then_inc(S(sq_sem), 1)
                filled(first[name])
                act.activation(sg[:, 0, :], bank(first[name], T), ACT.Sqrt, bias=eps, scale=1.0 / HD
                               ).then_inc(act_freed, 1)

            head_roots("k_norm", "kk", kT, A_(1), "k_sq")
            act.wait_ge(S("logf_arg"), 1)
            act.activation(lw[1], lw[1], ACT.Exp).then_inc(S("logf_exp"), 1)
            gemm("vv")
            ffn(2)
            root_mean("mix1")
            xn_high("mix1")
            head_roots("q_norm", "q", q_f, q_sq, "q_sq")
            for hd in range(H):
                act.wait_ge(S("s_ready"), 2 * hd + 2)
                s = s_pr[:, hd % 2, :]
                st = fstat[:, hd % 2, :]
                act.activation(s[:, 0:P], s[:, 0:P], ACT.Exp, bias=st[:, 4:5], accum_out=st[:, 6:7]
                               ).then_inc(S("e_ready"), 1)
                act.activation(s[:, P:3 * P], s[:, P:3 * P], ACT.Exp, bias=st[:, 5:6], accum_out=st[:, 7:8]
                               ).then_inc(S("e_ready"), 1)
            act.wait_ge(dve_freed, freed["d"][first["fox"] + 3 * H])
            act.activation(oT_hi[:, :, 0:TP], oT[:, :, 0:TP], ACT.Copy).then_inc(S("o_hi"), 1)
            def page_copy(b, j):
                act.wait_ge(S("k_page_free"), b * PAGES + (j + 5))
                act.activation(k_feat[j // 2 % 2][:, 0:4, j % 2 * P:(j % 2 + 1) * P],
                               ps[:, 3 + j % 2 * 2, :].rearrange("p (m t) -> p m t", m=4), ACT.Copy
                               ).then_inc(S("kT_act"), 1)

            def past_forget(b):
                act.wait_ge(S("s_done"), b + 1)
                nf = nfk[:, bass.ds(b, 1), :, :].rearrange("p b j h -> p (b j h)")
                act.activation(nfk_rep.rearrange("p (n q) -> p n q", q=QS),
                               nf.unsqueeze(2).to_broadcast([P, PAGES * H, QS]), ACT.Copy
                               ).then_inc(S("nfk_rep"), 1)

            def sequence(b, last):
                for j in range(4, PAGES):
                    page_copy(b, j)
                act.wait_ge(S("less_max"), b + 1)
                for g in range(2):
                    act.activation(p_row[:, g * 512:(g + 1) * 512], ps[:, g, :], ACT.Exp,
                                   bias=sst[:, 4:5], accum_out=sst[:, 11 + g:12 + g]).then_inc(S("p_row"), 1)
                act.activation(p_row[:, PAST:PAST + TS], s_new, ACT.Exp,
                               bias=sst[:, 4:5], accum_out=sst[:, 13:14]).then_inc(S("p_row"), 1)
                if not last:
                    page_copy(b + 1, 0)
                    page_copy(b + 1, 1)
                act.wait_ge(S("p_turned"), b + 1)
                act.activation(p_T[:, 0:4, :], ps[:, 0, :].rearrange("p (g c) -> p g c", g=4), ACT.Copy
                               ).then_inc(S("pT_act"), 1)
                if not last:
                    page_copy(b + 1, 2)
                    past_forget(b + 1)
                    page_copy(b + 1, 3)

            past_forget(0)
            for j in range(4):
                page_copy(0, j)
            with act.Fori(0, BS - 1) as b:
                sequence(b, False)
            sequence(BS - 1, True)
            act.wait_ge(S("fox_out"), 2 * BS)
            act.activation(oT_hi[:, :, TP:T], oT[:, :, TP:T], ACT.Copy).then_inc(S("o_hi"), 1)
            gemm("fo", norm_next=True)
            ffn(3)

        @block.vector
        def _(dve):
            steps = [0]

            def link(ins):
                steps[0] += 1
                ins.then_inc(S("dve_step"), 1)
                dve.wait_ge(S("dve_step"), steps[0])

            def filled(t):
                dve.wait_ge(tile_done, t + 1)

            def free(ins, n=1):
                ins.then_inc(dve_freed, n)

            TT, TS_, STT, CP = dve.tensor_tensor, dve.tensor_scalar, dve.scalar_tensor_tensor, dve.tensor_copy

            def low(out, x, high):
                return TT(out, x, high.bitcast(F32), ALU.subtract)

            def lo(s):
                dve.wait_ge(S("w_hi"), s + 1)
                low(part(s, 0), raw(s), part(s, 1)).then_inc(S("w_lo"), 1)

            def norm(name, param, row):
                if name != "ffn2":
                    i, t = norms.index(name), first["norm_" + name]
                    dve.wait_ge(act_freed, freed["a"][t + 1])
                    dve.reciprocal(rs[:, :], root[:, :]).then_inc(S("rs_ready"), 1)
                    dve.wait_ge(S("rs_ready"), i + 1)

                def xn_low(m):
                    dve.wait_ge(S("xn_hi"), split_norms.index(name) * DT + m + 1)
                    low(xn_lo[:, m, :], xn[:, m, :], xn_hi[:, m, :]).then_inc(S("xn_split"), 1)

                for m in range(DT):
                    STT(xn[:, m, :], h[:, m, :], prm(param, m, row), rs[:, :], ALU.mult, ALU.mult
                        ).then_inc(S("xn_raw"), 1)
                    if m >= 2 and name != "mix0":
                        xn_low(m - 2)
                if name != "mix0":
                    xn_low(DT - 2)
                    xn_low(DT - 1)

            def ffn(n):
                norm(f"ffn{n}", "ffn_norm", n)
                base, s0 = first[f"up{n}"], first_slab[f"up{n}"]
                with dve.Fori(0, 5) as i:
                    for j in range(4):
                        dve.wait_ge(S("w_hi"), i * 4 + (s0 + j + 3))
                        low(part(s0 + j + 2, 0), raw(s0 + j + 2), part(s0 + j + 2, 1)).then_inc(S("w_lo"), 1)
                        if j % 2 == 0:
                            continue
                        dve.wait_ge(S("silu_ready"), i * 4 + (n * FT + j + 1))
                        for mt in range(2):
                            f = 2 * (j // 2) + mt
                            dve.wait_ge(tile_done, i * 8 + (base + 2 * j + mt + 1))
                            b_ = (base + 2 * j + mt) % 8
                            free(TT(hid[:, bass.ds(i * 4 + f, 1), :], sg[:, f:f + 1, :],
                                    ps[:, b_:b_ + 1, 0:T], ALU.mult), 3 if mt else 1)
                        for mt in range(2):
                            f = 2 * (j // 2) + mt
                            dve.wait_ge(S("hid_hi"), i * 4 + (n * FT + f + 1))
                            low(hid_lo[:, bass.ds(i * 4 + f, 1), :], hid[:, bass.ds(i * 4 + f, 1), :],
                                hid_hi[:, bass.ds(i * 4 + f, 1), :]).then_inc(S("hid_split"), 1)
                lo(s0 + 22)
                lo(s0 + 23)
                dve.wait_ge(S("silu_ready"), n * FT + FT)
                for mt in range(2):
                    filled(base + 42 + mt)
                    free(TT(hid[:, 20 + mt, :], sg[:, mt, :], bank(base + 42 + mt, T), ALU.mult), 3 if mt else 1)
                for mt in range(2):
                    dve.wait_ge(S("hid_hi"), n * FT + 20 + mt + 1)
                    low(hid_lo[:, 20 + mt, :], hid[:, 20 + mt, :], hid_hi[:, 20 + mt, :]).then_inc(S("hid_split"), 1)
                for mp in range(4):
                    for s3 in range(3):
                        s = first_slab[f"down{n}"] + 3 * mp + s3 + 2
                        if s < len(slabs):
                            lo(s)
                    for m in (2 * mp, 2 * mp + 1):
                        filled(first[f"down{n}"] + m)
                        free(STT(h[:, m, :], bank(first[f"down{n}"] + m, T), 0.5, h[:, m, :], ALU.mult, ALU.add))

            dve.memset(eps, RMS_EPS).then_inc(S("eps_ready"), 1)
            dve.memset(eps_ln, LNX_EPS).then_inc(S("eps_ready"), 1)
            for m in range(DT):
                filled(first["x"] + m)
                free(CP(h[:, m, :], bank(first["x"] + m, T)))
            dve.wait_ge(dve_freed, freed["d"][first["x"] + DT])
            t = first["params"]
            filled(t)
            free(CP(par[:, 0, :], bank(t, P)))
            filled(t + 1)
            free(CP(par[:, 1, 0:rows - P], bank(t + 1, rows - P)))
            dve.wait_ge(dve_freed, freed["d"][t + 2])
            link(TS_(omka, par[:, row_of["rw_k_a"] // P, row_of["rw_k_a"] % P:row_of["rw_k_a"] % P + DT],
                     -1.0, 1.0, ALU.mult, ALU.add))
            filled(first["shift_in"])
            free(CP(shT.rearrange("p m b -> p (m b)"), bank(first["shift_in"], DT * BS)))
            lo(0)
            lo(1)
            ffn(0)
            dve.wait_ge(dve_freed, freed["d"][first["down0"] + DT])
            norm("mix0", "mix_norm", 0)
            dve.wait_ge(S("xn_raw"), 2 * DT)
            CP(shc[:, :, 0:1], xn[:, :, TP - 1:TP])
            xs_sample = xn[:, :, TP:T].rearrange("p m (b t) -> p m b t", b=BS)
            link(CP(shc[:, :, 1:BS + 1], xs_sample[:, :, :, QS - 1]))
            dve.sem_inc(S("shift_cols"), 1)
            df = A_(0)
            df_s = df[:, :, TP:T].rearrange("p m (b t) -> p m b t", b=BS)
            TT(df[:, :, 1:TP], xn[:, :, 0:TP - 1], xn[:, :, 1:TP], ALU.subtract)
            TS_(df[:, :, 0:1], xn[:, :, 0:1], -1.0, None, ALU.mult)
            TT(df_s[:, :, :, 1:QS], xs_sample[:, :, :, 0:QS - 1], xs_sample[:, :, :, 1:QS], ALU.subtract)
            link(TT(df_s[:, :, :, 0], shT, xs_sample[:, :, :, 0], ALU.subtract))

            def mixed(j):
                name = mixes[j]
                if j >= 2:
                    last = mix_last[mixes[j - 2]]
                    filled(first[last] + (DT - 1 if len(last) == 1 else 0))
                for m in range(DT):
                    STT(A_(1 + j % 2)[:, m, :], df[:, m, :], prm("rw_mu", m, mix_row[name]), xn[:, m, :],
                        ALU.mult, ALU.add).then_inc(S("xs_raw"), 1)

            def mixed_low(j):
                name = mixes[j]
                for m in range(DT):
                    dve.wait_ge(S("xs_hi"), "krv".index(name) * DT + m + 1)
                    low(AR_(1 + j % 2)[:, m, :], A_(1 + j % 2)[:, m, :], xs_hi[name][:, m, :]
                        ).then_inc(S("xs_split"), 1)

            def head_rn(name, root_, rn):
                dve.wait_ge(act_freed, freed["a"][first[name] + 1])
                dve.reciprocal(rn, root_).then_inc(S("rn_ready"), 1)

            def copy_out(name, dst, ahead=4, between=()):
                for q in range(4):
                    if name in first_slab and q < ahead:
                        lo(first_slab[name] + q + 2)
                    if q < len(between):
                        between[q]()
                    for m in (2 * q, 2 * q + 1):
                        filled(first[name] + m)
                        free(CP(dst[:, m, :], bank(first[name] + m, T)))

            sig, cum = A_(6), A_(9)

            def sums_to(m0, m1):
                for m in range(m0, m1):
                    ins = dve.tensor_tensor_scan(cum[:, m, :], K("chunk"), sig[:, m, :], 0.0, ALU.mult, ALU.add)
                if m1 == DT:
                    link(ins)

            def sums_before():
                link(TT(sig, cum, sig, ALU.subtract))
                dve.sem_inc(S("decay_sums"), 1)

            def key_sums():
                filled(first["kk_norm"])
                free(TS_(rs[:, :], bank(first["kk_norm"], T), 1e-24, None, ALU.max))

            mixed(0)
            mixed(1)
            mixed(2)
            mixed(3)
            mixed_low(2)
            mixed_low(3)
            copy_out("k", Kf)
            dve.wait_ge(dve_freed, freed["d"][first["k"] + DT])
            for m in range(DT):
                TS_(A_(10)[:, m, :], Kf[:, m, :], prm("rw_k_k", m), None, ALU.mult).then_inc(S("k_scaled"), 1)
            for j in range(2):
                t = first["shift_out"] + j
                filled(t)
                free(CP(Rf[0:BS + 1, :, :].rearrange("p m t -> p (m t)")[:, j * 512:(j + 1) * 512],
                        bank(t, 512, BS + 1)))

            def mixed_v():
                mixed(4)
                mixed_low(4)

            mixed_v()
            dve.wait_ge(S("shift_stored"), 32)
            copy_out("r", Rf, between=(lambda: sums_to(0, 4), lambda: sums_to(4, DT), sums_before))
            mixed(5)
            key_sums()
            dve.wait_ge(S("kk_root"), 1)
            dve.reciprocal(rs[:, :], root[:, :]).then_inc(S("rn_ready"), 1)
            copy_out("v", Vf, 2)

            aa, tmp = A_(7), A_(1)
            for m in range(DT):
                TS_(tmp[:, m, :], aa[:, m, :], prm("rw_k_a", m), omka[:, m:m + 1], ALU.mult, ALU.add)
            for m in range(DT):
                filled(first["kk_rep"] + m)
                free(TS_(Af[:, m, :], bank(first["kk_rep"] + m, T), prm("rw_k_k", m), None, ALU.mult))
            dve.wait_ge(dve_freed, freed["d"][first["kk_rep"] + DT])
            filled(first["g1"])
            dve.wait_ge(S("decays"), 3)
            Ep, Em = A_(6), A_(9)
            r_k = par[:, row_of["rw_r_k"] // P, row_of["rw_r_k"] % P:row_of["rw_r_k"] % P + DT]

            def scan_inputs(cs):
                n = cs.stop - cs.start
                v = {nm: x[:, :, cs] for nm, x in dict(A=Af, B=Bf, K=Kf, R=Rf, a=aa, E=Ef, Em=Em, Ep=Ep, bo=bonus).items()}
                rk = r_k.unsqueeze(2).to_broadcast([P, DT, n])
                return [
                    lambda: (link(TT(v["A"], v["A"], v["K"], ALU.mult)),
                             link(TT(v["K"], v["K"], v["B"], ALU.mult))),
                    lambda: (TT(v["bo"], v["R"], v["K"], ALU.mult),
                             link(TT(v["B"], v["A"], v["a"], ALU.mult))),
                    lambda: (TT(v["bo"], v["bo"], rk, ALU.mult),
                             TT(v["B"], v["B"], v["Em"], ALU.mult)),
                    lambda: (link(STT(v["A"], v["A"], -1.0, v["Ep"], ALU.mult, ALU.mult)),
                             TT(v["K"], v["K"], v["Em"], ALU.mult)),
                    lambda: (link(TT(v["R"], v["R"], v["E"], ALU.mult)),
                             dve.sem_inc(S("scan_in"), 1)),
                ]

            def pairs(dst, src, hf, c):
                hs = slice(4 * hf, 4 * hf + 4)
                TT(dst[:, hs, :].rearrange("p m (e c) -> p m e c", e=2),
                   src[:, hs, c * C:(c + 1) * C].unsqueeze(2).to_broadcast([P, 4, 2, C]),
                   pair.rearrange("p (e c) -> p e c", e=2).unsqueeze(1).to_broadcast([P, 4, 2, C]),
                   ALU.mult).then_inc(S("A_ready"), 1)

            for step in scan_inputs(slice(0, C)):
                step()
            for hf in range(2):
                pairs(A_bd, Af, hf, 0)
            dve.wait_ge(S("A_ready"), 2)
            copy_out("g2", gf)
            rest = scan_inputs(slice(C, T))
            def quad(t):
                return bank(t).rearrange("p (q c) -> p q c", q=4)

            def over(x, n=4):
                return x.unsqueeze(1).to_broadcast([P, n, x.shape[1]])

            def masked(name, dst, mask, hf):
                t = first[name] + hf
                filled(t)
                free(TT(dst[:, 4 * hf:4 * hf + 4, :], quad(t), over(K(mask)), ALU.mult))

            for c in range(CHUNKS):
                sample = c == CHUNKS - 1
                kind = "s" if sample else "p"
                for hf in range(2):
                    masked(f"LT{c}", LT_bd, "strict_" + kind, hf)
                dve.wait_ge(dve_freed, freed["d"][first[f"LT{c}"] + 2])
                for hf in range(2):
                    hs = slice(4 * hf, 4 * hf + 4)
                    link(TT(DT_bd[:, hs, :], LT_bd[:, hs, :], over(K("first_" + kind)), ALU.mult))
                    TT(DT_bd[:, hs, :], DT_bd[:, hs, :], over(ident), ALU.add).then_inc(S("DT_ready"), 1)
                for hf in range(2):
                    masked(f"KA{c}", KA_bd, "strict_" + kind, hf)
                for hf in range(2):
                    masked(f"RG{c}", RG_bd, "upto_" + kind, hf)
                for hf in range(2):
                    filled(first[f"D{c}"] + hf)
                    free(CP(D_bd[:, 4 * hf:4 * hf + 4, :], quad(first[f"D{c}"] + hf)))
                if c == 0:
                    rest[0]()
                dve.wait_ge(dve_freed, freed["d"][first[f"D{c}"] + 2])
                dve.wait_ge(S("DT_ready"), 2 * c + 2)
                lvs = levels(c)
                for lv in lvs:
                    for nm, dst in (("DD", D_bd), ("DDT", DT_bd)):
                        if nm == "DD" and lv == lvs[-1]:
                            continue
                        for hf in range(2):
                            t = first[f"{nm}{c}_{lv}"] + hf
                            filled(t)
                            hs = slice(4 * hf, 4 * hf + 4)
                            free(TT(dst[:, hs, :], quad(t), dst[:, hs, :], ALU.add))
                    dve.wait_ge(dve_freed, freed["d"][first[f"DDT{c}_{lv}"] + 2])
                    if c == 0 and lv < 5:
                        rest[lv]()
                        if lv == 4:
                            for m in range(DT):
                                dve.sem_inc(S("rk_ready"), 1)
                if not sample:
                    filled(first[f"X{c}"] + 1)
                    for hf in range(2):
                        pairs(A_bd, Af, hf, c + 1)
                if sample:
                    for hf in range(2):
                        t = first["own_state"] + hf
                        filled(t)
                        hs = slice(4 * hf, 4 * hf + 4)
                        xt0 = quad(t)[:, :, 0:C].unsqueeze(2).to_broadcast([P, 4, 2, C])
                        out = XT_bd[:, hs, :].rearrange("p m (e c) -> p m e c", e=2)
                        mk = pair.rearrange("p (e c) -> p e c", e=2).unsqueeze(1).to_broadcast([P, 4, 2, C])
                        link(TT(out, xt0, mk, ALU.mult))
                        free(CP(Y0[:, hs, :], quad(t)[:, :, C:2 * C]))
                for hf in range(2):
                    t = first[f"Y{c}"] + hf
                    filled(t)
                    hs = slice(4 * hf, 4 * hf + 4)
                    dst = Yf[:, hs, c * C:(c + 1) * C]
                    if sample:
                        dve.wait_ge(dve_freed, freed["d"][first["own_state"] + 2])
                        free(TT(dst, quad(t)[:, :, 0:C], Y0[:, hs, :], ALU.add))
                    else:
                        free(CP(dst, quad(t)[:, :, 0:C]))
                if not sample:
                    for hf in range(2):
                        t = first[f"S{c}"] + hf
                        filled(t)
                        hs = slice(4 * hf, 4 * hf + 4)
                        wc = Ef[:, hs, (c + 1) * C - 1:(c + 1) * C].to_broadcast([P, 4, P])
                        if c == 0:
                            free(TT(S_bd[:, hs, :], quad(t), wc, ALU.mult))
                        else:
                            link(TT(S_bd[:, hs, :], quad(t), S_bd[:, hs, :], ALU.add))
                            free(TT(S_bd[:, hs, :], S_bd[:, hs, :], wc, ALU.mult))
                    dve.wait_ge(dve_freed, freed["d"][first[f"S{c}"] + 2])
                    if c == CHUNKS - 2:
                        for hf in range(2):
                            t = first["wkv_prompt"] + hf
                            filled(t)
                            free(CP(S_bd[:, 4 * hf:4 * hf + 4, :], quad(t)))
                    for b in (2 * c, 2 * c + 1):
                        t = first[f"state_in{c}"] + b % 2
                        filled(t)
                        free(CP(S0[:, b, :, :], bank(t).rearrange("p (m i) -> p m i", m=HP)))
                    if c == 1:
                        for m in range(DT):
                            t = first["bonus"] + m
                            filled(t)
                            free(TT(bonus[:, m, :], bank(t, T), Vf[:, m, :], ALU.mult))
            dve.wait_ge(act_freed, freed["a"][first[f"U{CHUNKS - 1}"] + 2])
            filled(first[f"Y{CHUNKS - 1}"] + 1)
            link(TT(U_st, X_bd[:, :, 0:C], X_bd[:, :, C:2 * C], ALU.add))

            def U_masked(p):
                if p >= 2:
                    filled(first[f"SS{p - 2}"])
                TT(UV[p % 2][:, 0, :, :], U_st[:, p, :].unsqueeze(1).to_broadcast([P, BS, C]),
                   K("seq").unsqueeze(2).to_broadcast([P, BS, C]), ALU.mult).then_inc(S("U_masked"), 1)

            U_masked(0)
            U_masked(1)
            for p in range(HP):
                t = first[f"SS{p}"]
                filled(t)
                sf = SF[:, p % 2, :, :]
                if p >= 2:
                    filled(first[f"ST{p - 2}"] + 1)
                wc = Ef[:, p, TP + QS - 1:T:QS].unsqueeze(2).to_broadcast([P, BS, C])
                link(TT(sf, bank(t).rearrange("p (b i) -> p b i", b=BS), S0[:, :, p, :], ALU.add))
                free(TT(sf, sf, wc, ALU.mult))
                if p + 2 < HP:
                    U_masked(p + 2)
            dve.sem_inc(S("y_ready"), DT)
            lo(first_slab["wo"])
            for m in range(DT):
                t = first["mean"] + m
                filled(t)
                free(STT(Yf[:, m, :], bank(t, T), -1.0 / HD, Yf[:, m, :], ALU.mult, ALU.add))

            def wo_low(m):
                dve.wait_ge(S("wo_hi"), m + 1)
                low(AR_(9)[:, m, :], Yf[:, m, :], AR_(3)[:, m, :]).then_inc(S("wo_split"), 1)

            head_rn("var", root[:, :], rs[:, :])
            for m in range(DT):
                t = first["var_rep"] + m
                filled(t)
                link(STT(Yf[:, m, :], Yf[:, m, :], prm("rw_lnx_w", m), bank(t, T), ALU.mult, ALU.mult))
                dve.sem_inc(dve_freed, 1)
                link(STT(Yf[:, m, :], Yf[:, m, :], prm("rw_lnx_b", m), bonus[:, m, :], ALU.add, ALU.add))
                TT(Yf[:, m, :], Yf[:, m, :], gf[:, m, :], ALU.mult).then_inc(S("wo_raw"), 1)
                if m:
                    wo_low(m - 1)
            wo_low(DT - 1)
            lo(first_slab["wo"] + 1)

            def residual(name):
                for q in range(4):
                    lo(first_slab[name] + q + 2)
                    for m in (2 * q, 2 * q + 1):
                        filled(first[name] + m)
                        free(TT(h[:, m, :], bank(first[name] + m, T), h[:, m, :], ALU.add))
                dve.wait_ge(dve_freed, freed["d"][first[name] + DT])

            residual("wo")
            ffn(1)
            dve.wait_ge(dve_freed, freed["d"][first["down1"] + DT])

            norm("kv", "kv_norm", 0)
            copy_out("kk", kT)
            for j in range(2):
                r = row_of["head_norms"] + j - P
                TS_(hn_scale[:, j:j + 1], par[:, 1, r:r + 1], HD ** -0.5 if j else 1.0, None, ALU.mult)
            x, e, z, z2 = lw

            def logf_start():
                t = first["logf"]
                filled(t)
                free(TS_(x, bank(t, T, H), b_f[0:H, :], None, ALU.add))
                dve.wait_ge(dve_freed, freed["d"][t + 1])
                link(TS_(e, x, -1.0, None, ALU.mult))
                link(TT(e, e, x, ALU.min))
                dve.sem_inc(S("logf_arg"), 1)

            def logf_ratio():
                dve.wait_ge(S("logf_exp"), 1)
                link(TS_(z, e, 2.0, None, ALU.add))
                link(dve.reciprocal(z, z))
                link(TT(z, z, e, ALU.mult))
                link(TT(z2, z, z, ALU.mult))
                link(TS_(e, z2, 1.0 / 19, None, ALU.mult))

            def logf_series():
                for n in range(8, 0, -1):
                    link(STT(e, e, 1.0 / (2 * n + 1), z2, ALU.add, ALU.mult))
                link(STT(z, e, 1.0, z, ALU.add, ALU.mult))

            def logf_end():
                link(TS_(x, x, 0.0, None, ALU.min))
                link(STT(LF, z, -2.0, x, ALU.mult, ALU.add))
                link(dve.tensor_tensor_scan(FT_, K("seqscan")[0:H, :], LF, 0.0, ALU.mult, ALU.add))
                dve.sem_inc(S("logf_ready"), 2)

            logf_start()
            head_rn("k_norm", sg[:, 0, :], sg[:, 1, :])
            copy_out("vv", A_(0), between=(logf_ratio, logf_series, logf_end))
            for m in range(DT):
                filled(first["k_rep"] + m)
                STT(kT[:, m, :], kT[:, m, :], hn_scale[:, 0:1], bank(first["k_rep"] + m, T), ALU.mult, ALU.mult
                    ).then_inc(S("k_ready"), 1)
            dve.wait_ge(S("k_ready"), DT)
            dve.sem_inc(dve_freed, DT)
            t = first["logf_tok"]
            filled(t)
            both = bank(t, 6 * H).rearrange("p (e g h) -> p e g h", e=2, g=3)
            CP(lf_tok[:, 0:2, :], both[:, 0, 0:2, :])
            CP(F_tok[:, 0:2, :], both[:, 1, 0:2, :])
            CP(lf_tok[0:TS, 2, :], both[0:TS, 0, 2, :])
            free(CP(F_tok[0:TS, 2, :], both[0:TS, 1, 2, :]))
            dve.wait_ge(dve_freed, freed["d"][t + 1])
            dve.sem_inc(S("logf_tok_ready"), 1)
            dve.wait_ge(S("wkv_prompt_out"), 32)
            for name, dst in (("k_tok", k_tok), ("v_tok", v_tok)):
                for g, n in ((0, P), (1, P), (2, TS)):
                    for j in range(2):
                        t = first[name] + 2 * g + j
                        filled(t)
                        free(CP(dst[0:n, g, j * 512:(j + 1) * 512], bank(t, 512, n)))
            dve.wait_ge(dve_freed, freed["d"][first["v_tok"] + 6])
            ffn(2)
            dve.wait_ge(dve_freed, freed["d"][first["down2"] + DT])

            norm("mix1", "mix_norm", 1)
            def past_copies():
                for j in range(4):
                    filled(first["fk_past"] + j)
                for j in range(2):
                    free(CP(nfk.rearrange("p b j h -> p (b j h)")[:, j * 512:(j + 1) * 512],
                            bank(first["fk_past"] + j)))
                for hb in range(2):
                    t = first["fk_past"] + 2 + hb
                    free(CP(tot[hb], bank(t).rearrange("p (b j h) -> p b j h", b=4, j=PAGES)))
                t = first["fq_col"]
                filled(t)
                free(CP(F_row, bank(t, TS)))
                dve.wait_ge(dve_freed, freed["d"][t + 1])

            tot = [arena[:, hb * 512:(hb + 1) * 512].rearrange("p (b j h) -> p b j h", b=4, j=PAGES)
                   for hb in range(2)]

            def later_pages(hb):
                bs = slice(4 * hb, 4 * hb + 4)
                for j in range(PAGES - 2, -1, -1):
                    if j < PAGES - 2:
                        link(TT(tot[hb][:, :, j + 1, :], tot[hb][:, :, j + 1, :], tot[hb][:, :, j + 2, :], ALU.add))
                    link(TT(nfk[:, bs, j, :], nfk[:, bs, j, :], tot[hb][:, :, j + 1, :], ALU.add))

            def query_forgets():
                fq = tmp_fq.rearrange("p (b q) -> p b q", b=BS)
                link(TT(fq, F_row.rearrange("p (b q) -> p b q", b=BS),
                        K("qpick").unsqueeze(1).to_broadcast([P, BS, QS]), ALU.mult))
                link(dve.tensor_reduce(fq_all, fq, AX.X, ALU.add))
                for dst, src in ((slice(0, P), slice(0, P)), (slice(P, 3 * P), slice(0, 2 * P))):
                    ins = TS_(nF_dup[:, dst], FT_[:, src], -1.0, None, ALU.mult)
                link(ins)
                dve.sem_inc(S("nF_ready"), 1)

            past_copies()
            copy_out("q", q_f, between=(lambda: later_pages(0), lambda: later_pages(1), query_forgets))
            dve.sem_inc(S("page_space"), 1)
            head_rn("q_norm", sg[:, 0, :], sg[:, 1, :])
            for m in range(DT):
                t = first["q_rep"] + m
                filled(t)
                free(STT(q_f[:, m, :], q_f[:, m, :], hn_scale[:, 1:2], bank(t, T), ALU.mult, ALU.mult))
            dve.wait_ge(dve_freed, freed["d"][first["q_rep"] + DT])

            def queries_of(p):
                if p >= 2:
                    filled(first["fox"] + fox_tile(2 * p - 3, 0))
                for e_ in range(2):
                    ins = TS_(qp_bd[:, p % 2, e_, :], q_f[:, p, 0:TP], pair[:, e_ * C:e_ * C + 1], None, ALU.mult)
                link(ins)
                dve.sem_inc(S("qp_ready"), 1)

            queries_of(0)
            def probabilities(hd):
                s, st = s_pr[:, hd % 2, :], fstat[:, hd % 2, :]
                dve.wait_ge(S("e_ready"), 2 * hd + 2)
                link(dve.reciprocal(st[:, 8:10], st[:, 6:8]))
                TS_(s[:, 0:P], s[:, 0:P], st[:, 8:9], None, ALU.mult).then_inc(S("p_ready"), 1)
                TS_(s[:, P:3 * P], s[:, P:3 * P], st[:, 9:10], None, ALU.mult).then_inc(S("p_ready"), 1)

            for kind, hd in fox_order:
                t = first["fox"] + fox_tile(hd, kind)
                s, st = s_pr[:, hd % 2, :], fstat[:, hd % 2, :]
                if kind == 0:
                    if hd % 2 == 0 and hd // 2 + 1 < HP:
                        queries_of(hd // 2 + 1)
                    if hd >= 1:
                        probabilities(hd - 1)
                    if hd >= 2:
                        filled(first["fox"] + fox_tile(hd - 2, 1))
                    filled(t)
                    TT(s, bank(t, 384), K("causal"), ALU.add).then_inc(dve_freed, 1)
                    dve.wait_ge(dve_freed, freed["d"][t + 1])
                    dve.tensor_reduce(st[:, 0:1], s[:, 0:P], AX.X, ALU.max)
                    link(dve.tensor_reduce(st[:, 1:2], s[:, P:3 * P], AX.X, ALU.max))
                    link(TT(st[:, 2:4], st[:, 0:2], F_tok[:, 0:2, hd], ALU.add))
                    link(TT(st[:, 4:6], F_tok[:, 0:2, hd], st[:, 2:4], ALU.subtract))
                    dve.sem_inc(S("s_ready"), 2)
                elif kind == 1:
                    filled(t)
                    free(CP(pT[:, hd % 2, :], bank(t, 384)))
                else:
                    filled(t)
                    e_ = hd % 2
                    free(CP(oT[e_ * HD:(e_ + 1) * HD, hd // 2, 0:TP], ps[e_ * HD:(e_ + 1) * HD, t % 8, 0:TP]))
                if (kind, hd) == (1, H - 2):
                    probabilities(H - 1)
            dve.wait_ge(dve_freed, freed["d"][first["fox"] + 3 * H])

            dve.wait_ge(S("o_hi"), 1)
            low(oT_lo[:, :, 0:TP], oT[:, :, 0:TP], oT_hi[:, :, 0:TP]).then_inc(S("o_split"), 1)
            link(dve.memset(mask_new.rearrange("p b k -> p (b k)"), NEG))
            for b in range(BS):
                ins = CP(mask_new[:, b, b * QS:(b + 1) * QS], K("new"))
            link(ins)
            link(TT(mask_new, mask_new, F_row.unsqueeze(1).to_broadcast([P, BS, TS]), ALU.subtract))
            link(dve.memset(q_cur, 0.0))
            base, PER = steps[0], 7
            def page_copy(b, j):
                dve.wait_ge(S("k_page_free"), b * PAGES + (j + 5))
                CP(k_feat[j // 2 % 2][:, 4:8, j % 2 * P:(j % 2 + 1) * P],
                   ps[:, 4 + j % 2 * 2, :].rearrange("p (m t) -> p m t", m=4)).then_inc(S("kT_dve"), 1)

            def queries(b):
                dve.wait_ge(S("s_done"), b + 1)
                for r in range(2):
                    for e_ in range(2):
                        off = 48 * r + QS * e_
                        TS_(q_cur.rearrange("p (g c) -> p g c", g=4)[:, :, off:off + QS],
                            q_f[:, r:HP:2, bass.ds(b * QS + TP, QS)], pair[:, e_ * C:e_ * C + 1], None, ALU.mult
                            ).then_inc(S("q_cur"), 1)

            def sequence(b, last):
                n_link = [0]

                def lk(ins):
                    n_link[0] += 1
                    ins.then_inc(S("dve_step"), 1)
                    dve.wait_ge(S("dve_step"), b * PER + (base + n_link[0]))

                for j in range(4, PAGES):
                    page_copy(b, j)
                dve.wait_ge(S("half_scored"), b + 1)
                dve.tensor_reduce(sst[:, 0:1], ps[:, 0, :], AX.X, ALU.max)
                dve.wait_ge(S("s_done"), b + 2)
                lk(TT(s_new, ps[:, 2, 0:TS], mask_new[:, bass.ds(b, 1), :].rearrange("p b k -> p (b k)"), ALU.add))
                dve.tensor_reduce(sst[:, 1:2], ps[:, 1, :], AX.X, ALU.max)
                lk(dve.tensor_reduce(sst[:, 2:3], s_new, AX.X, ALU.max))
                lk(dve.tensor_reduce(sst[:, 10:11], sst[:, 0:3], AX.X, ALU.max))
                lk(TT(sst[:, 3:4], sst[:, 10:11], fq_all[:, bass.ds(b, 1)], ALU.add))
                TT(sst[:, 4:5], fq_all[:, bass.ds(b, 1)], sst[:, 3:4], ALU.subtract).then_inc(S("less_max"), 1)
                if not last:
                    page_copy(b + 1, 0)
                    page_copy(b + 1, 1)
                dve.wait_ge(S("p_turned"), b + 1)
                CP(p_T[:, 4:8, :], ps[:, 1, :].rearrange("p (g c) -> p g c", g=4)).then_inc(S("pT_dve"), 1)
                CP(p_T[0:TS, 8, :], ps[0:TS, 2, P:2 * P]).then_inc(S("pT_dve"), 1)
                lk(dve.tensor_reduce(sst[:, 8:9], sst[:, 11:14], AX.X, ALU.add))
                lk(dve.reciprocal(sst[:, 9:10], sst[:, 8:9]))
                if not last:
                    page_copy(b + 1, 2)
                    queries(b + 1)
                dve.wait_ge(S("outputs_done"), b + 1)
                lk(STT(o_own, ps[:, 7, 0:256].rearrange("p (g d) -> p g d", g=4), sst[:, 9:10],
                       K("quarter").unsqueeze(2).to_broadcast([P, 4, HD]), ALU.mult, ALU.mult))
                for e_ in range(2):
                    dve.tensor_reduce(o_two[:, e_ * HD:(e_ + 1) * HD], o_own.rearrange("p g d -> p d g"), AX.X,
                                      ALU.add).then_inc(S("o_own"), 1)
                if not last:
                    page_copy(b + 1, 3)
                dve.wait_ge(S("o_turned"), b + 1)
                for e_ in range(2):
                    pr = slice(e_ * HD, (e_ + 1) * HD)
                    CP(oT[pr, :, bass.ds(b * QS + TP, QS)],
                       ps[pr, 7, 256:384].rearrange("p (m e q) -> p m e q", m=HP, e=2)[:, :, e_, :]
                       ).then_inc(S("fox_out"), 1)
                assert n_link[0] == PER, n_link

            queries(0)
            for j in range(4):
                page_copy(0, j)
            with dve.Fori(0, BS - 1) as b:
                sequence(b, False)
            sequence(BS - 1, True)
            steps[0] = base + PER * BS
            dve.wait_ge(S("o_hi"), 2)
            low(oT_lo[:, :, TP:T], oT[:, :, TP:T], oT_hi[:, :, TP:T]).then_inc(S("o_split"), 1)
            residual("fo")
            ffn(3)
            dve.wait_ge(dve_freed, freed["d"][first["down3"] + DT])
            y_tok = [arena[:, 3 * TW + j * D:3 * TW + (j + 1) * D] for j in range(3)]
            for g, n in ((0, P), (1, P), (2, TS)):
                for j in range(2):
                    t = first["y"] + 2 * g + j
                    filled(t)
                    free(CP(y_tok[g][0:n, j * 512:(j + 1) * 512], bank(t, 512, n)))

        @block.gpsimd
        def _(pool):
            pool.wait_ge(dve_freed, freed["d"][first["shift_out"] + 2])
            rows_sh = arena[0:BS + 1, 3 * TW:3 * TW + D]
            pool.dma_start(O["shift_prompt"].rearrange("n b d -> (n b) d"), rows_sh[0:1, :]).then_inc(S("shift_stored"), 16)
            pool.dma_start(O["shift_sample"].rearrange("n b d -> (n b) d"), rows_sh[1:BS + 1, :]).then_inc(S("shift_stored"), 16)
            def state_in_(b):
                if b >= 2:
                    pool.wait_ge(tile_done, first[f"state_in{b // 2 - 1}"] + b % 2 + 1)
                pool.dma_start(state_in[b % 2][0:HD, :].rearrange("p (g j) -> p g j", g=H),
                               A["state_wkv"][0, b].rearrange("g i j -> i g j")).then_inc(S(f"state_in{b % 2}"), 16)

            pool.wait_ge(tile_done, first["v"] + DT)
            state_in_(0)
            state_in_(1)

            def pairs(dst, src, hf, c):
                hs = slice(4 * hf, 4 * hf + 4)
                pool.tensor_tensor(dst[:, hs, :].rearrange("p m (e c) -> p m e c", e=2),
                                   src[:, hs, c * C:(c + 1) * C].unsqueeze(2).to_broadcast([P, 4, 2, C]),
                                   pair.rearrange("p (e c) -> p e c", e=2).unsqueeze(1).to_broadcast([P, 4, 2, C]),
                                   ALU.mult).then_inc(S("bd_ready"), 1)

            for c in range(CHUNKS):
                if c:
                    pool.wait_ge(tile_done, first[f"X{c - 1}"] + 2)
                if c < 2:
                    pool.wait_ge(S("scan_in"), c + 1)
                if c:
                    pool.wait_ge(act_freed, freed["a"][first[f"Z{c - 1}_{levels(c - 1)[-1]}"] + 2])
                for dst, src in ((B_bd, Bf), (K_bd, Kf), (V_bd, Vf)):
                    for hf in range(2):
                        pairs(dst, src, hf, c)
                lvs = levels(c)
                for n_lv, lv in enumerate(lvs):
                    for hf in range(2):
                        hs = slice(4 * hf, 4 * hf + 4)
                        if lv == lvs[0]:
                            pool.wait_ge(tile_done, first[f"tok{c}"] + 4)
                            pool.wait_ge(dve_freed, freed["d"][first[f"LT{c}"] + 2])
                        else:
                            pool.wait_ge(tile_done, first[f"Z{c}_{lvs[n_lv - 1]}"] + hf + 1)
                        pool.tensor_tensor(join_bd[:, hs, :], LT_bd[:, hs, :],
                                           K(f"join{lv}").unsqueeze(1).to_broadcast([P, 4, P]), ALU.mult
                                           ).then_inc(S("join_ready"), 1)
                if 0 < c < CHUNKS - 1:
                    state_in_(2 * c)
                    state_in_(2 * c + 1)
                if c == CHUNKS - 2:
                    pool.wait_ge(dve_freed, freed["d"][first["wkv_prompt"] + 2])
                    for e in range(2):
                        pool.dma_start(
                            O["wkv_prompt"][0, 0].rearrange("(m e) i j -> e i m j", e=2)[e],
                            S_bd[e * HD:(e + 1) * HD, :, e * HD:(e + 1) * HD]).then_inc(S("wkv_prompt_out"), 16)
            c = CHUNKS - 1
            pool.wait_ge(tile_done, first[f"Y{c}"] + 2)
            pool.tensor_tensor(V_st, V_tok[:, :, 0:C], V_tok[:, :, C:2 * C], ALU.add).then_inc(S("st_ready"), 1)
            pool.wait_ge(S("st_ready"), 1)

            def store_states(p):
                pool.wait_ge(act_freed, freed["a"][first[f"ST{p}"] + 2])
                for e in range(2):
                    pool.dma_start(O["wkv_sample"][0, :, 2 * p + e, :, :].rearrange("b i j -> i b j"),
                                   state_out[p % 2][0:HD, :].rearrange("p (b e j) -> p b e j", b=BS, e=2)[:, :, e, :]
                                   ).then_inc(S(f"state_out{p % 2}"), 16)

            for p in range(HP):
                if p >= 2:
                    pool.wait_ge(tile_done, first[f"SS{p - 2}"] + 1)
                pool.tensor_tensor(UV[p % 2][:, 1, :, :], V_st[:, p, :].unsqueeze(1).to_broadcast([P, BS, C]),
                                   K("seq").unsqueeze(2).to_broadcast([P, BS, C]), ALU.mult
                                   ).then_inc(S("V_masked"), 1)
                if p >= 2:
                    store_states(p - 2)
            store_states(HP - 2)
            store_states(HP - 1)
            pool.wait_ge(S("logf_tok_ready"), 1)
            pool.dma_start(O["logf_prompt"][0].rearrange("(g p) h -> p g h", p=P), lf_tok[:, 0:2, :]).then_inc(S("logf_stored"), 16)
            pool.dma_start(O["logf_sample"].rearrange("b t h -> (b t) h"), lf_tok[0:TS, 2, :]).then_inc(S("logf_stored"), 16)
            for name, src in (("k", k_tok), ("v", v_tok)):
                for g in range(3):
                    pool.wait_ge(dve_freed, freed["d"][first[name + "_tok"] + 2 * g + 2])
                    if g < 2:
                        dst = O[name + "_prompt"][0, g * P:(g + 1) * P].rearrange("t h d -> t (h d)")
                    else:
                        dst = O[name + "_sample"].rearrange("b t h d -> (b t) (h d)")
                    pool.dma_start(dst, src[0:P if g < 2 else TS, g, :]).then_inc(S(name + "_stored"), 16)
            pool.wait_ge(tile_done, first["logf_tok"] + 1)
            pool.wait_ge(S("pt_in"), 16)
            with pool.Fori(0, BS) as b:
                for j in range(PAGES):
                    page = pool.value_load(pt_sb[0:1, bass.ds(b * PAGES + j, 1)], min_val=0,
                                           max_val=A["cache_k"].shape[0] - 1)
                    pool.dma_start(lfp[:, bass.ds(b, 1), j, :].rearrange("p b h -> p (b h)"),
                                   A["cache_logf"][bass.ds(page, 1)].rearrange("a t h -> (a t) h")
                                   ).then_inc(S("lfp_in"), 16)
            for g in range(3):
                pool.wait_ge(dve_freed, freed["d"][first["y"] + 2 * g + 2])
                dst = (O["y_prompt"][0, g * P:(g + 1) * P] if g < 2 else O["y_sample"].rearrange("b t d -> (b t) d"))
                pool.dma_start(dst, arena[0:P if g < 2 else TS, 3 * TW + g * D:3 * TW + (g + 1) * D]
                               ).then_inc(S("y_stored"), 16)
            pool.wait_ge(S("shift_stored"), 32)
            pool.wait_ge(S("wkv_prompt_out"), 32)
            pool.wait_ge(S("state_out0"), 16 * HP)
            pool.wait_ge(S("state_out1"), 16 * HP)
            pool.wait_ge(S("logf_stored"), 32)
            pool.wait_ge(S("k_stored"), 48)
            pool.wait_ge(S("v_stored"), 48)
            pool.wait_ge(S("y_stored"), 48)


_INS = ["x_prompt", "x_sample", "cache_k", "cache_v", "cache_logf", "state_wkv", "state_shift", "page_table",
        "ffn_norm", "ffn_w_in", "ffn_w_out", "mix_norm", "rw_mu", "rw_w_rkv", "rw_w0", "rw_w1", "rw_w2",
        "rw_a0", "rw_a1", "rw_a2", "rw_g1", "rw_g2", "rw_k_k", "rw_k_a", "rw_r_k", "rw_lnx_w", "rw_lnx_b",
        "rw_w_o", "kv_norm", "w_kv", "k_norm", "w_f", "b_f", "fox_w_q", "fox_q_norm", "fox_w_o"]
_OUTS = [("y_prompt", (1, TP, D)), ("y_sample", (BS, QS, D)), ("k_prompt", (1, TP, H, HD)),
         ("v_prompt", (1, TP, H, HD)), ("logf_prompt", (1, TP, H)), ("wkv_prompt", (1, 1, H, HD, HD)),
         ("shift_prompt", (1, 1, D)), ("k_sample", (BS, QS, H, HD)), ("v_sample", (BS, QS, H, HD)),
         ("logf_sample", (BS, QS, H)), ("wkv_sample", (1, BS, H, HD, HD)), ("shift_sample", (1, BS, D))]


def kernel(**inputs):
    import concourse.bacc as bacc
    from concourse.bass_utils import run_bass_kernel_spmd

    nc = bacc.Bacc("TRN2", target_bir_lowering=False, num_devices=1)
    arrays, A, O = {}, {}, {}
    given = {name: np.ascontiguousarray(inputs[name]) for name in _INS}
    given["const"] = const_arrays()[1]
    given["head_sel"] = head_selectors()
    for name, a in given.items():
        arrays["in_" + name] = a
        A[name] = nc.dram_tensor("in_" + name, a.shape, mybir.dt.from_np(a.dtype), kind="ExternalInput").ap()
    for name, shape in _OUTS:
        O[name] = nc.dram_tensor("out_" + name, shape, F32, kind="ExternalOutput").ap()
    build(nc, A, O)
    r = run_bass_kernel_spmd(nc, [arrays], core_ids=[0])
    return tuple(r.results[0]["out_" + name] for name, _ in _OUTS)
```
